# Optimizing a Trainium2 kernel written in Bass

```python
import math
import jax, jax.numpy as jnp
from jax import lax
import numpy as np

D_MODEL = 1024
BATCH = 1
SEQ = 1024
DEPTH = 1
DEC_BATCH = 8
DEC_SEQ = 4
PAST_LEN = 4096
PAGE_SIZE = 128

N_META = 16
DIFF_HEADS = 4
DIFF_DK = 64
DIFF_DV = 128
DIFF_SCALE = DIFF_DK ** -0.5
GLA_HEADS = 4
GLA_DK = 64
GLA_DV = 128
GLA_GATE_RANK = 16
GLA_GATE_NORM = 16.0
GLA_CHUNK = 128
Q_BLOCK = 128
NUM_BUCKETS = 32
MAX_DISTANCE = 128
RMS_EPS = 1e-6
DIFF_WIDTH = DIFF_HEADS * DIFF_DV
GLA_WIDTH = GLA_HEADS * GLA_DV
D_MIX = DIFF_WIDTH + GLA_WIDTH
SPLITS = (DIFF_HEADS * 2 * DIFF_DK, DIFF_HEADS * 2 * DIFF_DK, DIFF_WIDTH, DIFF_WIDTH,
          GLA_HEADS * GLA_DK, GLA_HEADS * GLA_DK, GLA_WIDTH, GLA_WIDTH, GLA_GATE_RANK)
D_IN = sum(SPLITS)

kernel_name = "hymba_diffattn_gla_step"

def rms_norm(x, w):
    xf = x.astype(jnp.float32)
    y = xf * lax.rsqrt(jnp.mean(xf * xf, axis=-1, keepdims=True) + RMS_EPS)
    return y * w.astype(jnp.float32)

def rel_bucket(n):
    n = jnp.maximum(n, 0)
    max_exact = NUM_BUCKETS // 2
    nf = jnp.maximum(n, 1).astype(jnp.float32)
    large = max_exact + (jnp.log(nf / max_exact) / math.log(MAX_DISTANCE / max_exact)
                         * (NUM_BUCKETS - max_exact)).astype(jnp.int32)
    large = jnp.minimum(large, NUM_BUCKETS - 1)
    return jnp.where(n < max_exact, n, large)

def rel_bias_for(rel_bias, n):
    return jnp.transpose(rel_bias[rel_bucket(n)].astype(jnp.float32), (2, 0, 1))

def mixer_inputs(h, norm_w, w_in, q_norm_w, k_norm_w, gla_wa2, gla_ba):
    B, T, _ = h.shape
    hn = rms_norm(h, norm_w).astype(h.dtype)
    z = hn @ w_in
    idx = np.cumsum(SPLITS)[:-1].tolist()
    dq, dk, dv, dg, gq, gk, gv, gg, ga = jnp.split(z, idx, axis=-1)
    dq = rms_norm(dq.reshape(B, T, DIFF_HEADS, 2, DIFF_DK), q_norm_w)
    dk = rms_norm(dk.reshape(B, T, DIFF_HEADS, 2, DIFF_DK), k_norm_w).astype(h.dtype)
    dv = dv.reshape(B, T, DIFF_HEADS, DIFF_DV)
    gq = gq.reshape(B, T, GLA_HEADS, GLA_DK).astype(jnp.float32) * (GLA_DK ** -0.5)
    gk = gk.reshape(B, T, GLA_HEADS, GLA_DK).astype(jnp.float32)
    gv = gv.reshape(B, T, GLA_HEADS, GLA_DV).astype(jnp.float32)
    lg = jax.nn.log_sigmoid((ga @ gla_wa2 + gla_ba).astype(jnp.float32)) / GLA_GATE_NORM
    lg = lg.reshape(B, T, GLA_HEADS, GLA_DK)
    return dq, dk, dv, dg, gq, gk, gv, gg, lg

def diff_lambda(lam_q, lam_k, lam_init):
    lq = lam_q.astype(jnp.float32)
    lk = lam_k.astype(jnp.float32)
    return jnp.exp(jnp.sum(lq[0] * lk[0])) - jnp.exp(jnp.sum(lq[1] * lk[1])) + lam_init

def diff_attn_prompt(q, k, v, lam, rel_bias):
    B, L = q.shape[:2]
    nb = -(-L // Q_BLOCK)
    q_pad = jnp.pad(q, ((0, 0), (0, nb * Q_BLOCK - L), (0, 0), (0, 0), (0, 0)))
    kf = k.astype(jnp.float32)
    vf = v.astype(jnp.float32)
    kpos = jnp.arange(L)

    def block(j):
        q0 = j * Q_BLOCK
        qb = lax.dynamic_slice_in_dim(q_pad, q0, Q_BLOCK, axis=1)
        n = (q0 + jnp.arange(Q_BLOCK))[:, None] - kpos[None, :]
        s = jnp.einsum('bqhmd,bkhmd->bhmqk', qb, kf) * DIFF_SCALE + rel_bias_for(rel_bias, n)[None, :, None]
        s = jnp.where(n >= 0, s, -jnp.inf)
        a = jax.nn.softmax(s, axis=-1)
        p = a[:, :, 0] - lam * a[:, :, 1]
        return jnp.einsum('bhqk,bkhe->bqhe', p, vf)

    o = lax.map(block, jnp.arange(nb))
    o = jnp.transpose(o, (1, 0, 2, 3, 4)).reshape(B, nb * Q_BLOCK, DIFF_HEADS, DIFF_DV)
    return o[:, :L]

def diff_attn_sample(q, k, v, cache_k, cache_v, layer, page_table, lam, rel_bias):
    B, T = q.shape[:2]
    past = page_table.shape[1] * cache_k.shape[2]
    kp = cache_k[layer, page_table].reshape(B, past, DIFF_HEADS, 2, DIFF_DK).astype(jnp.float32)
    vp = cache_v[layer, page_table].reshape(B, past, DIFF_HEADS, DIFF_DV).astype(jnp.float32)
    qpos = past + jnp.arange(T)
    n_past = qpos[:, None] - jnp.arange(past)[None, :]
    n_new = qpos[:, None] - qpos[None, :]
    s_past = jnp.einsum('bqhmd,bkhmd->bhmqk', q, kp) * DIFF_SCALE + rel_bias_for(rel_bias, n_past)[None, :, None]
    s_new = jnp.einsum('bqhmd,bkhmd->bhmqk', q, k.astype(jnp.float32)) * DIFF_SCALE + rel_bias_for(rel_bias, n_new)[None, :, None]
    s_new = jnp.where(n_new >= 0, s_new, -jnp.inf)
    a = jax.nn.softmax(jnp.concatenate([s_past, s_new], axis=-1), axis=-1)
    p = a[:, :, 0] - lam * a[:, :, 1]
    return (jnp.einsum('bhqk,bkhe->bqhe', p[..., :past], vp)
            + jnp.einsum('bhqk,bkhe->bqhe', p[..., past:], v.astype(jnp.float32)))

def gla_chunk(S, q, k, v, lg):
    C = q.shape[1]
    b = jnp.cumsum(lg, axis=1)
    o_inter = jnp.einsum('bthd,bhde->bthe', q * jnp.exp(b), S)
    diff = b[:, :, None] - b[:, None, :]
    causal = (jnp.arange(C)[:, None] >= jnp.arange(C)[None, :])[None, :, :, None, None]
    decay = jnp.exp(jnp.where(causal, diff, -jnp.inf))
    A = jnp.einsum('bthd,btshd,bshd->bths', q, decay, k)
    o = o_inter + jnp.einsum('bths,bshe->bthe', A, v)
    b_last = b[:, -1]
    S_new = jnp.exp(b_last)[..., None] * S + jnp.einsum('bshd,bshe->bhde', k * jnp.exp(b_last[:, None] - b), v)
    return S_new, o

def gla_prompt(q, k, v, lg):
    B, L = q.shape[:2]
    S0 = jnp.zeros((B, GLA_HEADS, GLA_DK, GLA_DV), jnp.float32)
    S, o_meta = gla_chunk(S0, q[:, :N_META], k[:, :N_META], v[:, :N_META], lg[:, :N_META])
    nc = (L - N_META) // GLA_CHUNK

    def blocks(t):
        t = t[:, N_META:]
        return jnp.moveaxis(t.reshape((B, nc, GLA_CHUNK) + t.shape[2:]), 1, 0)

    def step(S, xs):
        return gla_chunk(S, *xs)

    S, o_rest = lax.scan(step, S, (blocks(q), blocks(k), blocks(v), blocks(lg)))
    o_rest = jnp.moveaxis(o_rest, 0, 1).reshape(B, nc * GLA_CHUNK, GLA_HEADS, GLA_DV)
    return jnp.concatenate([o_meta, o_rest], axis=1), S

def merge_out(h, o_d, dg, o_g, gg, diff_norm_w, gla_norm_w, lam_init, w_out):
    B, T = o_d.shape[:2]
    od = (rms_norm(o_d, diff_norm_w) * (1.0 - lam_init)).reshape(B, T, DIFF_WIDTH) * jax.nn.silu(dg.astype(jnp.float32))
    og = rms_norm(o_g, gla_norm_w).reshape(B, T, GLA_WIDTH) * jax.nn.silu(gg.astype(jnp.float32))
    mix = jnp.concatenate([od, og], axis=-1).astype(h.dtype)
    return h + mix @ w_out

def setup_inputs(seed: int = 0) -> dict:
    key = jax.random.key(seed)
    ks = jax.random.split(key, 20)
    n_pages = PAST_LEN // PAGE_SIZE
    n_used = DEC_BATCH * n_pages
    n_pool = n_used + max(1, n_used // 4)
    f32 = jnp.float32
    x_prompt = jax.random.normal(ks[0], (BATCH, SEQ, D_MODEL), f32)
    x_sample = jax.random.normal(ks[1], (DEC_BATCH, DEC_SEQ, D_MODEL), f32)
    cache_k = jax.random.normal(ks[2], (DEPTH, n_pool, PAGE_SIZE, DIFF_HEADS, 2 * DIFF_DK), f32)
    cache_v = jax.random.normal(ks[3], (DEPTH, n_pool, PAGE_SIZE, DIFF_HEADS, DIFF_DV), f32)
    state_gla = 0.5 * jax.random.normal(ks[4], (DEPTH, DEC_BATCH, GLA_HEADS, GLA_DK, GLA_DV), f32)
    page_table = jax.random.permutation(ks[5], n_pool)[:n_used].reshape(DEC_BATCH, n_pages).astype(jnp.int32)
    meta_tokens = jax.random.normal(ks[6], (N_META, D_MODEL), f32)
    rel_bias = 0.1 * jax.random.normal(ks[7], (NUM_BUCKETS, DIFF_HEADS), f32)
    norm_w = 1.0 + 0.02 * jax.random.normal(ks[8], (DEPTH, D_MODEL), f32)
    w_in = jax.random.normal(ks[9], (DEPTH, D_MODEL, D_IN), f32) * D_MODEL ** -0.5
    q_norm_w = 1.0 + 0.02 * jax.random.normal(ks[10], (DEPTH, 2, DIFF_DK), f32)
    k_norm_w = 1.0 + 0.02 * jax.random.normal(ks[11], (DEPTH, 2, DIFF_DK), f32)
    lam_q = 0.1 * jax.random.normal(ks[12], (DEPTH, 2, DIFF_DK), f32)
    lam_k = 0.1 * jax.random.normal(ks[13], (DEPTH, 2, DIFF_DK), f32)
    diff_norm_w = 1.0 + 0.02 * jax.random.normal(ks[14], (DEPTH, DIFF_DV), f32)
    gla_wa2 = jax.random.normal(ks[15], (DEPTH, GLA_GATE_RANK, GLA_HEADS * GLA_DK), f32) * GLA_GATE_RANK ** -0.5
    gla_ba = 0.1 * jax.random.normal(ks[16], (DEPTH, GLA_HEADS * GLA_DK), f32)
    gla_norm_w = 1.0 + 0.02 * jax.random.normal(ks[17], (DEPTH, GLA_DV), f32)
    w_out = jax.random.normal(ks[18], (DEPTH, D_MIX, D_MODEL), f32) * D_MIX ** -0.5
    return {"x_prompt": x_prompt, "x_sample": x_sample, "cache_k": cache_k, "cache_v": cache_v,
            "state_gla": state_gla, "page_table": page_table, "meta_tokens": meta_tokens,
            "rel_bias": rel_bias, "norm_w": norm_w, "w_in": w_in, "q_norm_w": q_norm_w,
            "k_norm_w": k_norm_w, "lam_q": lam_q, "lam_k": lam_k, "diff_norm_w": diff_norm_w,
            "gla_wa2": gla_wa2, "gla_ba": gla_ba, "gla_norm_w": gla_norm_w, "w_out": w_out}

def reference(x_prompt, x_sample, cache_k, cache_v, state_gla, page_table, meta_tokens, rel_bias,
              norm_w, w_in, q_norm_w, k_norm_w, lam_q, lam_k, diff_norm_w, gla_wa2, gla_ba,
              gla_norm_w, w_out):
    B = x_prompt.shape[0]
    L = x_prompt.shape[1] + N_META
    DB, T = x_sample.shape[:2]
    meta = jnp.broadcast_to(meta_tokens[None].astype(x_prompt.dtype), (B, N_META, D_MODEL))
    h_p = jnp.concatenate([meta, x_prompt], axis=1)
    h_s = x_sample
    kp_rows, vp_rows, sp_list, ks_rows, vs_rows, ss_list = [], [], [], [], [], []
    for l in range(DEPTH):
        lam_init = 0.8 - 0.6 * math.exp(-0.3 * l)
        lam = diff_lambda(lam_q[l], lam_k[l], lam_init)
        dq, dk, dv, dg, gq, gk, gv, gg, lg = mixer_inputs(h_p, norm_w[l], w_in[l], q_norm_w[l], k_norm_w[l], gla_wa2[l], gla_ba[l])
        o_d = diff_attn_prompt(dq, dk, dv, lam, rel_bias)
        o_g, s_fin = gla_prompt(gq, gk, gv, lg)
        h_p = merge_out(h_p, o_d, dg, o_g, gg, diff_norm_w[l], gla_norm_w[l], lam_init, w_out[l])
        kp_rows.append(dk.reshape(B, L, DIFF_HEADS, 2 * DIFF_DK))
        vp_rows.append(dv)
        sp_list.append(s_fin.astype(x_prompt.dtype))
        dq, dk, dv, dg, gq, gk, gv, gg, lg = mixer_inputs(h_s, norm_w[l], w_in[l], q_norm_w[l], k_norm_w[l], gla_wa2[l], gla_ba[l])
        o_d = diff_attn_sample(dq, dk, dv, cache_k, cache_v, l, page_table, lam, rel_bias)
        s_new, o_g = gla_chunk(state_gla[l].astype(jnp.float32), gq, gk, gv, lg)
        h_s = merge_out(h_s, o_d, dg, o_g, gg, diff_norm_w[l], gla_norm_w[l], lam_init, w_out[l])
        ks_rows.append(dk.reshape(DB, T, DIFF_HEADS, 2 * DIFF_DK).astype(cache_k.dtype))
        vs_rows.append(dv.astype(cache_v.dtype))
        ss_list.append(s_new.astype(state_gla.dtype))
    y_prompt = h_p[:, N_META:]
    y_sample = h_s
    k_prompt = jnp.stack(kp_rows)
    v_prompt = jnp.stack(vp_rows)
    s_prompt = jnp.stack(sp_list)
    k_sample = jnp.stack(ks_rows)
    v_sample = jnp.stack(vs_rows)
    s_sample = jnp.stack(ss_list)
    return (y_prompt, y_sample, k_prompt, v_prompt, s_prompt, k_sample, v_sample, s_sample)


_drawn_inputs = setup_inputs


def setup_inputs(seed=0):
    import zlib

    import numpy as np

    out = dict(_drawn_inputs(seed))
    spreads = {}
    factors = {'rel_bias': 3.026, 'q_norm_w': 7.893, 'diff_norm_w': 8.0, 'gla_norm_w': 7.713}
    for name, (base, spread) in spreads.items():
        noise = np.random.default_rng([zlib.crc32(name.encode()), seed]).standard_normal(out[name].shape)
        drawn = base * np.exp(spread * noise) if base else spread * noise
        out[name] = __import__('jax').numpy.asarray(drawn.astype(out[name].dtype))
    for name, factor in factors.items():
        out[name] = (out[name] * factor).astype(out[name].dtype)
    return out
```

```python
from contextlib import ExitStack
import math

import concourse.bass as bass
from concourse import mybir

F32 = mybir.dt.float32
F32R = mybir.dt.float32r
I32 = mybir.dt.int32
ALU = mybir.AluOpType
ACT = mybir.ActivationFunctionType
AX = mybir.AxisListType

P = 128
D = 1024
KT = D // P
NMETA, SEQ = 16, 1024
L = NMETA + SEQ
NB, TS = 8, 4
NS = NB * TS
TILES = L // P + 1
TAIL = L - P * (TILES - 1)
LASTW = 64
S0 = 32
NTOK = P * (TILES - 1) + LASTW
H, DK, DV = 4, 64, 128
W = H * DV
PAGE, NPAGES, POOL = 128, 32, 320
GRP = 4
G = NPAGES // GRP
PAST = PAGE * NPAGES
DIN = 3600
CB = 256
EPS = 1e-6
LAM_INIT = 0.8 - 0.6 * math.exp(0.0)
NEG = -1e30

HALVES = (64, 32, 16)
DIAG = 16
LV = len(HALVES) + 1

KINDS = ["q", "q", "k", "k", "v", "v", "dg", "dg", "gq", "gk", "gv", "gv", "gg", "gg"]

W_AT = [CB * c for c in range(len(KINDS) + 1)]


def rows_of(i):
    return P if i < TILES - 1 else LASTW


def hymba_kernel(nc, x_prompt, x_sample, cache_k, cache_v, state_gla, page_table, meta_tokens, rel_bias,
                 norm_w, w_in, q_norm_w, k_norm_w, lam_q, lam_k, diff_norm_w, gla_wa2, gla_ba, gla_norm_w,
                 w_out, c_ident, c_cum, c_cum8, c_mask, c_mask8, c_oh, c_hotp, c_hotn, c_negn, c_negp, c_rowq, c_selT,
                 c_colm, c_rowm, c_m01,
                 y_prompt, y_sample, k_prompt, v_prompt, s_prompt, k_sample, v_sample, s_sample):
    ctx = ExitStack()
    with ctx:
        def sem(name):
            return ctx.enter_context(nc.semaphore(name))

        def sb(stack, name, shape, dt=F32):
            return stack.enter_context(nc.sbuf_tensor(name, shape, dt))

        def ps(stack, name, shape):
            return stack.enter_context(nc.psum_tensor(name, shape, F32))

        def dram(name, shape):
            return nc.dram_tensor(name, shape, F32, kind="Internal").ap()

        gate_d = dram("gate_d", (TILES, P, W))
        gate_g = dram("gate_g", (TILES, P, W))
        val_g = dram("val_g", (TILES, P, W))
        val_d = dram("val_d", (TILES, P, W))
        skew = dram("skew", (H, P * 384))

        ident = sb(ctx, "ident", [P, P])
        qT = sb(ctx, "qT", [P, H, NTOK])
        kT = sb(ctx, "kT", [P, H, NTOK])
        gqT = sb(ctx, "gqT", [P, 2, NTOK])
        gkT = sb(ctx, "gkT", [P, 2, NTOK])
        bT = sb(ctx, "bT", [P, 2, NTOK])
        lam = sb(ctx, "lam", [P, 8])
        nlam = lam[:, 7:8]
        od_s = sb(ctx, "od_s", [NS, W])

        with ExitStack() as st:
            xTh = sb(st, "xTh", [P, KT, NTOK], F32R)
            xTl = sb(st, "xTl", [P, KT, NTOK], F32R)
            xb = sb(st, "xb", [P, 2, D])
            wraw = sb(st, "wraw", [P, 2, KT, CB])
            wh = sb(st, "wh", [P, 2, KT, CB], F32R)
            wl = sb(st, "wl", [P, 2, KT, CB], F32R)
            squares = sb(st, "squares", [P, D])
            nw = sb(st, "nw", [P, KT])
            qwr = sb(st, "qwr", [P, 2, CB])
            ss = sb(st, "ss", [P, 4, TILES])
            sq = sb(st, "sq", [P, 2, CB])
            rms = sb(st, "rms", [P, 2, 3, 4])
            nrm = sb(st, "nrm", [P, CB])
            nat = sb(st, "nat", [P, 3, CB])
            gaT = sb(st, "gaT", [17, NTOK])
            wa2 = sb(st, "wa2", [17, CB])
            cum = sb(st, "cum", [P, P])
            cum8 = sb(st, "cum8", [LASTW, LASTW])
            lg = squares[:, 0:2 * CB].rearrange("p (a c) -> p a c", a=2)
            lgm = squares[:, 2 * CB:4 * CB].rearrange("p (a c) -> p a c", a=2)
            lmv = sb(st, "lmv", [P, 4, P])
            pz = [ps(st, f"pz{n}", [P, 512]) for n in range(3)]
            pt = ps(st, "pt", [P, 2, 512])
            pn = ps(st, "pn", [P, 2, 512])

            x_loaded = [sem(f"x_loaded{n}") for n in range(2)]
            x_zero = sem("x_zero")
            consts_in = sem("consts_in")
            w_loaded = [sem(f"w_loaded{n}") for n in range(2)]
            sumsq_done = sem("sumsq_done")
            meansq_done = sem("meansq_done")
            ln_done = sem("ln_done")
            rstd_done = sem("rstd_done")
            hn_done = sem("hn_done")
            xt_done = sem("xt_done")
            xhi_done = sem("xhi_done")
            xlo_done = sem("xlo_done")
            whi_done = sem("whi_done")
            wlo_done = sem("wlo_done")
            z_done = sem("z_done")
            turned_out = sem("turned_out")
            sq_done = sem("sq_done")
            ms_done = sem("ms_done")
            r_done = sem("r_done")
            nat_done = sem("nat_done")
            nt_done = sem("nt_done")
            nt_out = sem("nt_out")
            nat_stored = [sem(f"nat_stored{n}") for n in range(3)]
            dchain = sem("dchain_a")
            achain = sem("achain_a")
            ga_done = sem("ga_done")
            log_in = sem("log_in")
            lnexp_done = sem("lnexp_done")
            lg_done = sem("lg_done")
            cum_done = sem("cum_done")
            cum_out = sem("cum_out")
            lam_exp = sem("lam_exp")
            lam_sum = sem("lam_sum")

            natural = [(c, i) for c, k in enumerate(KINDS) if k not in ("gq", "gk") for i in range(TILES)]
            turned = [c for c, k in enumerate(KINDS) if k in ("gq", "gk")]
            NN = len(natural)

            def kind(s):
                return KINDS[natural[s][0]]

            def count(kinds, s):
                return sum(1 for t in range(s + 1) if kind(t) in kinds)

            ACTIVE = ("q", "k", "dg", "gg")
            CH = [(0, 512), (512, 512), (1024, LASTW)]
            uses = []
            for c, k in enumerate(KINDS):
                if k in ("gq", "gk"):
                    uses += [("t", c, m, n) for m in range(2) for n in range(3)]
                else:
                    uses += [("n", c, i) for i in range(TILES)]
            uses += [("a", n) for n in range(3)]
            uses += [("l", i) for i in range(TILES)]
            use_of = {u: n for n, u in enumerate(uses)}
            step_of = {x: n for n, x in enumerate(natural)}
            turned_uses = [u for u in uses if u[0] in "ta"]
            BLOCK_END = [1 + max(n for n, u in enumerate(uses) if u[0] in "nt" and u[1] == c)
                         for c in range(len(KINDS))]
            X_IN = [32, 16, 48, 32, 64, 48, 80, 64, 112]

            def wait_z(eng, u):
                if u < 3:
                    return
                before = uses[u - 3]
                if before[0] == "n":
                    eng.wait_ge(nat_done, step_of[before[1:]] + 1)
                elif before[0] in "ta":
                    eng.wait_ge(turned_out, turned_uses.index(before) + 1)
                else:
                    eng.wait_ge(lg_done, before[1] + 1)

            def z_at(n):
                return pz[n % 3]

            def stored(s):
                c, i = natural[s]
                k = KINDS[c]
                last = i == TILES - 1
                return {"q": 0, "k": 1 + last, "v": 2 + last}.get(k, 1)

            def stored_upto(s, slot):
                return sum(stored(t) for t in range(s + 1) if t % 3 == slot)

            block = st.enter_context(nc.Block())

            @block.sync
            def _(sp):
                sp.dma_start(ident[:], c_ident).then_inc(consts_in, 16)
                sp.dma_start(nw[:], norm_w.rearrange("a (t p) -> p (a t)", p=P), allow_slow_non_contiguous=True).then_inc(consts_in, 16)
                for m in range(2):
                    sp.dma_start(lmv[:, m, :], lam_q.rearrange("a m d -> a (m d)").to_broadcast([P, P]) if m == 0
                                 else lam_k.rearrange("a m d -> a (m d)").to_broadcast([P, P])).then_inc(consts_in, 16)
                for n, wt in enumerate((q_norm_w, k_norm_w)):
                    for h in range(2):
                        sp.dma_start(qwr[:, n, h * P:(h + 1) * P],
                                     wt.rearrange("a m d -> a (m d)").to_broadcast([P, P])).then_inc(consts_in, 16)
                sp.dma_start(cum[:], c_cum).then_inc(consts_in, 16)
                sp.dma_start(cum8[:], c_cum8).then_inc(consts_in, 16)
                sp.dma_start(wa2[0:16, :], gla_wa2[0]).then_inc(consts_in, 16)
                sp.dma_start(wa2[16:17, :], gla_ba).then_inc(consts_in, 16)

                def load_x(i):
                    if i >= 2:
                        sp.wait_ge(xt_done, 2 * (i - 1))
                    if i == 0:
                        sp.dma_start(xb[0:NMETA, 0, :], meta_tokens).then_inc(x_loaded[0], 16)
                        sp.dma_start(xb[NMETA:P, 0, :], x_prompt[0, 0:P - NMETA, :]).then_inc(x_loaded[0], 16)
                    elif i < TILES - 1:
                        sp.dma_start(xb[:, i % 2, :], x_prompt[0, P * i - NMETA:P * (i + 1) - NMETA, :])\
                          .then_inc(x_loaded[i % 2], 16)
                    else:
                        sp.wait_ge(x_zero, 1)
                        sp.dma_start(xb[0:TAIL, i % 2, :], x_prompt[0, SEQ - TAIL:SEQ, :])\
                          .then_inc(x_loaded[i % 2], 16)
                        sp.dma_start(xb[S0:S0 + NS, i % 2, :], x_sample.rearrange("b t d -> (b t) d"))\
                          .then_inc(x_loaded[i % 2], 16)

                def load_w(c):
                    if c >= 2:
                        sp.wait_ge(whi_done, KT * (c - 1))
                        sp.wait_ge(wlo_done, KT * (c - 1))
                    n = min(CB, DIN - W_AT[c])
                    sp.dma_start(wraw[:, c % 2, :, 0:n],
                                 w_in[0, :, W_AT[c]:W_AT[c] + n].rearrange("(t p) n -> p t n", p=P))\
                      .then_inc(w_loaded[c % 2], 16)

                load_x(0)
                load_x(1)
                load_w(0)
                load_w(1)
                for i in range(2, TILES):
                    load_x(i)
                stores = {"v": (val_d, 4), "gv": (val_g, 10), "dg": (gate_d, 6), "gg": (gate_g, 12)}
                nextw = 2
                for s, (c, i) in enumerate(natural):
                    if i == 0:
                        while nextw <= min(c + 2, len(W_AT) - 1):
                            load_w(nextw)
                            nextw += 1
                    k = kind(s)
                    at = nat_stored[s % 3]
                    sp.wait_ge(nat_done, s + 1)
                    r = rows_of(i)
                    if k == "q":
                        continue
                    if k in stores:
                        to, first = stores[k]
                        cols = slice((c - first) * CB, (c - first + 1) * CB)
                        sp.dma_start(to[i, 0:r, cols], nat[0:r, s % 3, :]).then_inc(at, 16)
                    if k in ("k", "v"):
                        first = 2 if k == "k" else 4
                        op, os_ = (k_prompt, k_sample) if k == "k" else (v_prompt, v_sample)
                        cols = slice((c - first) * CB, (c - first + 1) * CB)
                        dst = op.rearrange("a b l h d -> (a b l) (h d)")
                        n = P if i < TILES - 1 else TAIL
                        sp.dma_start(dst[P * i:P * i + n, cols], nat[0:n, s % 3, :]).then_inc(at, 16)
                        if i == TILES - 1:
                            dst = os_.rearrange("a b t h d -> (a b t) (h d)")
                            sp.dma_start(dst[:, cols], nat[S0:S0 + NS, s % 3, :]).then_inc(at, 16)
                while nextw < len(W_AT):
                    load_w(nextw)
                    nextw += 1
                for n in range(3):
                    sp.wait_ge(nat_stored[n], 16 * stored_upto(NN - 1, n))

            @block.gpsimd
            def _(pool):
                pass

            @block.scalar
            def _(act):
                link = [0]

                def linked(ins):
                    link[0] += 1
                    ins.then_inc(achain, 1)
                    act.wait_ge(achain, link[0])

                def x_sumsq(i):
                    r = rows_of(i)
                    act.wait_ge(x_loaded[i % 2], X_IN[i])
                    act.activation(squares[0:r, :], xb[0:r, i % 2, :], ACT.Square,
                                   accum_out=ss[0:r, 0, i:i + 1]).then_inc(sumsq_done, 1)
                    act.wait_ge(meansq_done, i + 1)
                    linked(act.activation(ss[0:r, 2, i:i + 1], ss[0:r, 1, i:i + 1], ACT.Ln))
                    act.activation(ss[0:r, 3, i:i + 1], ss[0:r, 2, i:i + 1], ACT.Exp, scale=-0.5)\
                       .then_inc(rstd_done, 1)

                def x_hi(i):
                    r = rows_of(i)
                    for half in range(2):
                        act.wait_ge(xt_done, 2 * i + half + 1)
                        for k in range(4):
                            kk = 4 * half + k
                            ins = act.activation(xTh[:, kk, P * i:P * i + r], pt[:, half, k * P:k * P + r],
                                                 ACT.Copy, scale=nw[:, kk:kk + 1])
                        ins.then_inc(xhi_done, 1)

                def w_hi(c):
                    n = min(CB, DIN - W_AT[c])
                    act.wait_ge(w_loaded[c % 2], 16 * (c // 2 + 1))
                    if c >= 2:
                        act.wait_ge(z_done, BLOCK_END[c - 2])
                    for k in range(KT):
                        act.activation(wh[:, c % 2, k, 0:n], wraw[:, c % 2, k, 0:n], ACT.Copy).then_inc(whi_done, 1)

                act.wait_ge(consts_in, 16 * 12)
                x_sumsq(0)
                x_sumsq(1)
                x_hi(0)
                w_hi(0)
                act.wait_ge(lam_sum, 1)
                act.activation(lam[:, 2:4], lam[:, 0:2], ACT.Exp).then_inc(lam_exp, 1)

                def first(s):
                    k = kind(s)
                    if k not in ACTIVE:
                        return
                    r = rows_of(natural[s][1])
                    u = use_of[("n", *natural[s])]
                    act.wait_ge(z_done, u + 1)
                    n = count(ACTIVE, s)
                    if n > 2:
                        act.wait_ge(nat_done, last_active(s, 2) + 1)
                    if k in ("q", "k"):
                        act.activation(sq[0:r, n % 2, :], z_at(u)[0:r, 0:CB], ACT.Square).then_inc(sq_done, 1)
                    else:
                        act.activation(sq[0:r, n % 2, :], z_at(u)[0:r, 0:CB], ACT.Exp, scale=-1.0)\
                           .then_inc(sq_done, 1)

                def second(s):
                    if kind(s) not in ("q", "k"):
                        return
                    r = rows_of(natural[s][1])
                    act.wait_ge(ms_done, s + 1)
                    linked(act.activation(rms[0:r, s % 2, 1, :], rms[0:r, s % 2, 0, :], ACT.Ln))
                    act.activation(rms[0:r, s % 2, 2, :], rms[0:r, s % 2, 1, :], ACT.Exp, scale=-0.5)\
                       .then_inc(r_done, 1)

                def third(s):
                    if kind(s) not in ("q", "k"):
                        return
                    c, i = natural[s]
                    r = rows_of(i)
                    to = qT if kind(s) == "q" else kT
                    act.wait_ge(nt_done, s + 1)
                    act.activation(to[:, 2 * (c % 2):2 * (c % 2) + 2, P * i:P * i + r],
                                   pn[:, s % 2, 0:2 * P].rearrange("p (h t) -> p h t", h=2)[:, :, 0:r],
                                   ACT.Copy).then_inc(nt_out, 1)

                def last_active(s, back):
                    t = s
                    while back:
                        t -= 1
                        if kind(t) in ACTIVE:
                            back -= 1
                    return t

                def turn_out(c):
                    to, sc = (gqT, DK ** -0.5) if KINDS[c] == "gq" else (gkT, 1.0)
                    for m in range(2):
                        for n, (t0, tn) in enumerate(CH):
                            u = use_of[("t", c, m, n)]
                            act.wait_ge(z_done, u + 1)
                            act.activation(to[:, m, t0:t0 + tn], z_at(u)[:, 0:tn], ACT.Copy, scale=sc)\
                               .then_inc(turned_out, 1)

                for s in range(NN + 3):
                    if s < NN:
                        c, i = natural[s]
                        if i == 0 and c == 10:
                            w_hi(9)
                            turn_out(8)
                            w_hi(10)
                            turn_out(9)
                        if c == 0:
                            if i + 2 < TILES:
                                x_sumsq(i + 2)
                            if i + 1 < TILES:
                                x_hi(i + 1)
                        first(s)
                        if i == 3:
                            w_hi(c + 1)
                    if 1 <= s <= NN:
                        second(s - 1)
                    if s >= 3:
                        third(s - 3)
                for n, (t0, tn) in enumerate(CH):
                    u = use_of[("a", n)]
                    act.wait_ge(z_done, u + 1)
                    act.wait_ge(ga_done, 1)
                    act.activation(gaT[0:16, t0:t0 + tn], z_at(u)[0:16, 0:tn], ACT.Copy).then_inc(turned_out, 1)
                for i in range(TILES):
                    r = rows_of(i)
                    u = use_of[("l", i)]
                    act.wait_ge(z_done, u + 1)
                    linked(act.activation(lgm[0:r, i % 2, :], z_at(u)[0:r, 0:CB], ACT.Abs))
                    linked(act.activation(lg[0:r, i % 2, :], lgm[0:r, i % 2, :], ACT.Exp, scale=-1.0))
                    act.activation(lgm[0:r, i % 2, :], lg[0:r, i % 2, :], ACT.Ln, bias=1.0).then_inc(lnexp_done, 1)
                    act.wait_ge(cum_done, i + 1)
                    act.activation(bT[:, :, P * i:P * i + r],
                                   pt[:, i % 2, 0:2 * r].rearrange("p (m t) -> p m t", m=2), ACT.Copy)\
                       .then_inc(cum_out, 1)

            @block.tensor
            def _(pe):
                def x_turn(i):
                    r = rows_of(i)
                    pe.wait_ge(hn_done, i + 1)
                    for half in range(2):
                        if i >= 1:
                            pe.wait_ge(xhi_done, 2 * (i - 1) + half + 1)
                            pe.wait_ge(xlo_done, 2 * (i - 1) + half + 1)
                        for k in range(4):
                            kk = 4 * half + k
                            ins = pe.transpose(pt[:, half, k * P:k * P + r], xb[0:r, i % 2, kk * P:(kk + 1) * P],
                                               ident[0:r, 0:r])
                        ins.then_inc(xt_done, 1)

                def z_nat(c, i, lastcols=CB):
                    u = use_of[("n", c, i)]
                    r = rows_of(i)
                    wait_z(pe, u)
                    n = 0
                    for k in range(KT):
                        if i == 0:
                            pe.wait_ge(whi_done, KT * c + k + 1)
                            pe.wait_ge(wlo_done, KT * c + k + 1)
                        for a, b in ((xTh, wh), (xTl, wh), (xTh, wl)):
                            ins = pe.matmul(z_at(u)[0:r, 0:CB], a[:, k, P * i:P * i + r], b[:, c % 2, k, :],
                                            start=(n == 0), stop=(n == 3 * KT - 1))
                            n += 1
                    ins.then_inc(z_done, 1)

                def z_turned(u, c, m0, mn, t0, tn):
                    wait_z(pe, u)
                    n = 0
                    for k in range(KT):
                        pe.wait_ge(whi_done, KT * c + k + 1)
                        pe.wait_ge(wlo_done, KT * c + k + 1)
                        for a, b in ((xTh, wh), (xTl, wh), (xTh, wl)):
                            ins = pe.matmul(z_at(u)[0:mn, 0:tn], b[:, c % 2, k, m0:m0 + mn], a[:, k, t0:t0 + tn],
                                            start=(n == 0), stop=(n == 3 * KT - 1))
                            n += 1
                    ins.then_inc(z_done, 1)

                def nat_turn(s):
                    if kind(s) not in ("q", "k"):
                        return
                    r = rows_of(natural[s][1])
                    pe.wait_ge(nat_done, s + 1)
                    if s >= 2:
                        pe.wait_ge(nt_out, s - 1)
                    for h in range(2):
                        ins = pe.transpose(pn[:, s % 2, h * P:h * P + r], nat[0:r, s % 3, h * P:(h + 1) * P],
                                           ident[0:r, 0:r])
                    ins.then_inc(nt_done, 1)

                pe.wait_ge(consts_in, 16 * 12)
                x_turn(0)
                s = 0
                for c, k in enumerate(KINDS):
                    if k in ("gq", "gk"):
                        for m in range(2):
                            for n, (t0, tn) in enumerate(CH):
                                z_turned(use_of[("t", c, m, n)], c, m * P, P, t0, tn)
                        continue
                    for i in range(TILES):
                        if c == 0:
                            if i + 1 < TILES:
                                x_turn(i + 1)
                            pe.wait_ge(xhi_done, 2 * i + 2)
                            pe.wait_ge(xlo_done, 2 * i + 2)
                        z_nat(c, i)
                        if s >= 2:
                            nat_turn(s - 2)
                        s += 1
                for n, (t0, tn) in enumerate(CH):
                    z_turned(use_of[("a", n)], 14, 0, 16, t0, tn)
                for i in range(TILES + 1):
                    if i < TILES:
                        r = rows_of(i)
                        u = use_of[("l", i)]
                        wait_z(pe, u)
                        pe.wait_ge(turned_out, len(turned_uses))
                        pe.matmul(z_at(u)[0:r, 0:CB], gaT[:, P * i:P * i + r], wa2[:], start=True, stop=True)\
                          .then_inc(z_done, 1)
                    if i >= 1:
                        j = i - 1
                        r = rows_of(j)
                        pe.wait_ge(lg_done, j + 1)
                        if j >= 2:
                            pe.wait_ge(cum_out, j - 1)
                        for m in range(2):
                            ins = pe.matmul(pt[:, j % 2, m * r:(m + 1) * r], lg[0:r, j % 2, m * P:(m + 1) * P],
                                            cum[:, :] if r == P else cum8[:, :], start=True, stop=True)
                        ins.then_inc(cum_done, 1)

            @block.vector
            def _(dve):
                link = [0]

                def linked(ins):
                    link[0] += 1
                    ins.then_inc(dchain, 1)
                    dve.wait_ge(dchain, link[0])

                dve.memset(gaT[:], 1.0).then_inc(ga_done, 1)
                dve.wait_ge(consts_in, 16 * 12)
                linked(dve.tensor_tensor(lmv[:, 2, :], lmv[:, 0, :], lmv[:, 1, :], ALU.mult))
                dve.tensor_reduce(lam[:, 0:2], lmv[:, 2, :].rearrange("p (m d) -> p m d", m=2), AX.X, ALU.add)\
                   .then_inc(lam_sum, 1)
                linked(dve.tensor_scalar(qwr[:, 0, :], qwr[:, 0, :], DK ** -0.5, None, ALU.mult))

                def x_norm(i):
                    r = rows_of(i)
                    dve.wait_ge(sumsq_done, i + 1)
                    dve.tensor_scalar(ss[0:r, 1, i:i + 1], ss[0:r, 0, i:i + 1], 1.0 / D, EPS, ALU.mult, ALU.add)\
                       .then_inc(meansq_done, 1)
                    dve.wait_ge(rstd_done, i + 1)
                    dve.tensor_scalar(xb[0:r, i % 2, :], xb[0:r, i % 2, :], ss[0:r, 3, i:i + 1], None, ALU.mult)\
                       .then_inc(hn_done, 1)

                def x_lo(i):
                    r = rows_of(i)
                    for half in range(2):
                        dve.wait_ge(xhi_done, 2 * i + half + 1)
                        for k in range(4):
                            kk = 4 * half + k
                            ins = dve.scalar_tensor_tensor(
                                out=xTl[:, kk, P * i:P * i + r], in0=pt[:, half, k * P:k * P + r],
                                scalar=nw[:, kk:kk + 1], in1=xTh[:, kk, P * i:P * i + r].bitcast(F32),
                                op0=ALU.mult, op1=ALU.subtract)
                        ins.then_inc(xlo_done, 1)

                def w_lo(c):
                    n = min(CB, DIN - W_AT[c])
                    for k in range(KT):
                        dve.wait_ge(whi_done, KT * c + k + 1)
                        dve.tensor_tensor(wl[:, c % 2, k, 0:n], wraw[:, c % 2, k, 0:n],
                                          wh[:, c % 2, k, 0:n].bitcast(F32), ALU.subtract).then_inc(wlo_done, 1)

                x_norm(0)
                x_norm(1)
                x_lo(0)
                w_lo(0)
                dve.wait_ge(lam_exp, 1)
                linked(dve.tensor_tensor(lam[:, 4:5], lam[:, 3:4], lam[:, 2:3], ALU.subtract))
                dve.tensor_scalar(nlam, lam[:, 4:5], -LAM_INIT, None, ALU.add)

                def reduce_sq(s):
                    k = kind(s)
                    if k not in ACTIVE:
                        return
                    r = rows_of(natural[s][1])
                    n = count(ACTIVE, s)
                    dve.wait_ge(sq_done, n)
                    if k in ("q", "k"):
                        linked(dve.tensor_reduce(rms[0:r, s % 2, 0, :],
                                                 sq[0:r, n % 2, :].rearrange("p (g d) -> p g d", g=4),
                                                 AX.X, ALU.add))
                        dve.tensor_scalar(rms[0:r, s % 2, 0, :], rms[0:r, s % 2, 0, :], 1.0 / DK, EPS,
                                          ALU.mult, ALU.add).then_inc(ms_done, 1)
                    else:
                        linked(dve.tensor_scalar(sq[0:r, n % 2, :], sq[0:r, n % 2, :], 1.0, None, ALU.add))
                        linked(dve.reciprocal(sq[0:r, n % 2, :], sq[0:r, n % 2, :]))

                def finish(s):
                    c, i = natural[s]
                    r = rows_of(i)
                    k = kind(s)
                    n = count(ACTIVE, s)
                    u = use_of[("n", c, i)]
                    z = z_at(u)[0:r, 0:CB]
                    to = nat[0:r, s % 3, :]
                    if s >= 3:
                        if stored_upto(s - 3, s % 3):
                            dve.wait_ge(nat_stored[s % 3], 16 * stored_upto(s - 3, s % 3))
                        if kind(s - 3) in ("q", "k"):
                            dve.wait_ge(nt_done, s - 2)
                    if k in ("q", "k"):
                        dve.wait_ge(r_done, s + 1)
                        g4 = lambda a: a.rearrange("p (g d) -> p g d", g=4)
                        linked(dve.tensor_tensor(g4(nrm[0:r, :]), g4(z),
                                                 rms[0:r, s % 2, 2, :].unsqueeze(2).to_broadcast([r, 4, DK]),
                                                 ALU.mult))
                        dve.tensor_tensor(to, nrm[0:r, :], qwr[0:r, 0 if k == "q" else 1, :], ALU.mult)\
                           .then_inc(nat_done, 1)
                        dve.wait_ge(nat_done, s + 1)
                    elif k in ("dg", "gg"):
                        dve.tensor_tensor(to, z, sq[0:r, n % 2, :], ALU.mult).then_inc(nat_done, 1)
                        dve.wait_ge(nat_done, s + 1)
                    else:
                        dve.wait_ge(z_done, u + 1)
                        dve.tensor_copy(to, z).then_inc(nat_done, 1)
                        dve.wait_ge(nat_done, s + 1)

                for s in range(NN + 1):
                    if s < NN:
                        c, i = natural[s]
                        if i == 0 and c == 10:
                            finish(s - 1)
                            w_lo(9)
                            w_lo(10)
                            reduce_sq(s)
                            continue
                        if c == 0:
                            if i + 2 == TILES - 1:
                                dve.wait_ge(xt_done, 2 * i + 2)
                                dve.memset(xb[0:S0, i % 2, :], 0.0).then_inc(x_zero, 1)
                            if i + 2 < TILES:
                                x_norm(i + 2)
                            if i + 1 < TILES:
                                x_lo(i + 1)
                        reduce_sq(s)
                        if i == 3:
                            finish(s - 1)
                            w_lo(c + 1)
                            continue
                    if s >= 1:
                        finish(s - 1)
                for i in range(TILES):
                    r = rows_of(i)
                    u = use_of[("l", i)]
                    dve.wait_ge(lnexp_done, i + 1)
                    dve.scalar_tensor_tensor(out=lg[0:r, i % 2, :], in0=z_at(u)[0:r, 0:CB], scalar=0.0,
                                             in1=lgm[0:r, i % 2, :], op0=ALU.min, op1=ALU.subtract)\
                       .then_inc(lg_done, 1)
                    dve.wait_ge(lg_done, i + 1)

        with ExitStack() as st:
            KR, VR = 4, 2
            kraw = sb(st, "kraw", [P, KR, GRP, W])
            vraw = sb(st, "vraw", [P, VR, GRP, W])
            kth = sb(st, "kth", [P, H, GRP * PAGE], F32R)
            ktl = sb(st, "ktl", [P, H, GRP * PAGE], F32R)
            vh = sb(st, "vh", [P, 2, GRP, W], F32R)
            vl = sb(st, "vl", [P, 2, GRP, W], F32R)
            sc = sb(st, "sc", [32, PAST + NS])
            pr = sb(st, "pr", [32, 2, GRP * PAGE])
            pT = sb(st, "pT", [P, 2, GRP, 64], F32R)
            pages = sb(st, "pages", [1, NB * NPAGES], I32)
            qqh = sb(st, "qqh", [P, 160], F32R)
            qql = sb(st, "qql", [P, 160], F32R)
            knh = sb(st, "knh", [P, H, NS], F32R)
            knl = sb(st, "knl", [P, H, NS], F32R)
            vn = sb(st, "vn", [NS, W])
            vnh = sb(st, "vnh", [NS, W], F32R)
            vnl = sb(st, "vnl", [NS, W], F32R)
            relb = sb(st, "relb", [32, H])
            rowq = sb(st, "rowq", [32, TS, 32])
            relq = sb(st, "relq", [32, TS, 32])
            oh, negp = sc[:, 0:384], sc[0:H, 512:896]
            hotp = sc[:, 1024:1024 + TS * PAGE].rearrange("k (q j) -> k q j", q=TS)
            hotn = sc[:, 2048:2048 + TS * NB * NS].rearrange("k (q j) -> k q j", q=TS)
            dlast = sb(st, "dlast", [32, PAGE])
            dnew = sb(st, "dnew", [32, NB * NS])
            band = sb(st, "band", [H, 384])
            selT = sb(st, "selT", [64, NB, H, NS])
            selc = sb(st, "selc", [64, H, P])
            m01 = sb(st, "m01", [64, 2])
            mx = sb(st, "mx", [32, G + 1])
            stat = sb(st, "stat", [64, 8])
            lsum = sb(st, "lsum", [32, G + 1])
            osb = sb(st, "osb", [64, W])
            pk = [ps(st, f"pk{n}", [P, 512]) for n in range(3)]
            psc = [ps(st, f"psc{n}", [32, 512]) for n in range(2)]
            ppt = ps(st, "ppt", [P, 512])
            po = ps(st, "po", [64, 512])
            pod = ps(st, "pod", [P, 512])
            negmax, rec, coef = stat[0:32, 0:1], stat[0:32, 1:2], stat[:, 2:3]
            c_in = sem("c_in")
            pages_in = sem("pages_in")
            k_in = [sem(f"k_in{n}") for n in range(KR)]
            v_in = [sem(f"v_in{n}") for n in range(VR)]
            setup = sem("setup_c")
            rel_done = sem("rel_done")
            band_out = sem("band_out")
            kt_done = sem("kt_done")
            khi_done = sem("khi_done")
            klo_done = sem("klo_done")
            sc_unit = sem("sc_unit")
            sc_out = sem("sc_out")
            max_done = sem("max_done")
            negmax_done = sem("negmax_done")
            exp_done = sem("exp_done")
            pt_done = sem("pt_done")
            phi_done = sem("phi_done")
            plo_done = sem("plo_done")
            vhi_done = sem("vhi_done")
            vlo_done = sem("vlo_done")
            pv_done = sem("pv_done")
            o_out = sem("o_out")
            qq_done = sem("qq_done")
            sel_done = sem("sel_done")
            od_done = sem("od_done")
            od_added = sem("od_added")
            new_done = sem("new_done")
            bias_done = sem("bias_done")
            dch = sem("dchain_c")
            NCONST = 10

            block = st.enter_context(nc.Block())

            @block.sync
            def _(sp):
                sp.dma_start(pages[:], page_table.rearrange("(o b) n -> o (b n)", o=1)).then_inc(pages_in, 16)
                sp.dma_start(vn[:], v_sample.rearrange("a b t h d -> (a b t) (h d)")).then_inc(c_in, 16)
                for to, of in ((relb[:], rel_bias), (rowq[:], c_rowq), (hotp, c_hotp.rearrange("k (q j) -> k q j", q=TS)),
                               (hotn, c_hotn), (dnew[:], c_negn), (oh, c_oh), (negp, c_negp), (selT[:], c_selT),
                               (m01[:], c_m01)):
                    sp.dma_start(to, of).then_inc(c_in, 16)
                sp.wait_ge(pages_in, 16)

                def load_keys(kb, peeled):
                    for g in range(G):
                        if not (peeled and g < KR):
                            sp.wait_ge(kt_done, kb * (4 * G) + 4 * (g - KR + 1))
                        for n in range(GRP):
                            page = sp.value_load(pages[0:1, bass.ds(kb * NPAGES + GRP * g + n, 1)],
                                                 min_val=0, max_val=POOL - 1)
                            sp.dma_start(kraw[:, g % KR, n, :],
                                         cache_k.rearrange("a n p h d -> (a n) p (h d)")[bass.ds(page, 1)]
                                         .rearrange("o p c -> (o p) c")).then_inc(k_in[g % KR], 16)

                load_keys(0, True)
                with sp.Fori(1, NB) as kb:
                    load_keys(kb, False)
                sp.wait_ge(band_out, 1)
                for h in range(H):
                    sp.dma_start(skew[h:h + 1].rearrange("o (q x) -> o q x", q=P),
                                 band[h:h + 1, :].unsqueeze(1).to_broadcast([1, P, 384])).then_inc(c_in, 16)
                sp.wait_ge(c_in, 16 * (NCONST + H))

            @block.gpsimd
            def _(pool):
                pool.wait_ge(pages_in, 16)

                def load_values(b, peeled):
                    for g in range(G):
                        if not (peeled and g < VR):
                            pool.wait_ge(vhi_done, b * G + g - VR + 1)
                            pool.wait_ge(vlo_done, b * G + g - VR + 1)
                        for n in range(GRP):
                            page = pool.value_load(pages[0:1, bass.ds(b * NPAGES + GRP * g + n, 1)],
                                                   min_val=0, max_val=POOL - 1)
                            pool.dma_start(vraw[:, g % VR, n, :],
                                           cache_v.rearrange("a n p h d -> (a n) p (h d)")[bass.ds(page, 1)]
                                           .rearrange("o p c -> (o p) c")).then_inc(v_in[g % VR], 16)

                load_values(0, True)
                with pool.Fori(1, NB) as b:
                    load_values(b, False)

            @block.scalar
            def _(act):
                def key_hi(kb, g, h):
                    act.wait_ge(kt_done, kb * (4 * G) + 4 * g + h + 1)
                    if not (isinstance(kb, int) and kb == 0 and g == 0):
                        act.wait_ge(sc_unit, kb * (4 * G) + 4 * (g - 1) + h + 1)
                    act.activation(kth[:, h, :], pk[(4 * g + h) % 3][:], ACT.Copy).then_inc(khi_done, 1)

                def scores_out(kb, g):
                    n = NS if g == G else 512
                    if g < G:
                        act.wait_ge(sc_unit, kb * (4 * G) + 4 * g + 4)
                    else:
                        act.wait_ge(new_done, kb + 1)
                    act.activation(sc[:, 512 * g:512 * g + n], psc[g % 2][:, 0:n], ACT.Copy).then_inc(sc_out, 1)

                def expo(b, g):
                    n = NS if g == G else 512
                    if g == 0:
                        act.wait_ge(negmax_done, b + 1)
                    if not (isinstance(b, int) and b == 0 and g < 2):
                        act.wait_ge(pt_done, b * (G + 1) + max(g - 1, 0))
                    act.activation(pr[:, g % 2, 0:n], sc[:, 512 * g:512 * g + n], ACT.Exp, bias=negmax,
                                   accum_out=lsum[:, g:g + 1]).then_inc(exp_done, 1)

                def probs_hi(b, g):
                    act.wait_ge(pt_done, b * (G + 1) + g + 1)
                    if not (isinstance(b, int) and b == 0 and g < 2):
                        act.wait_ge(pv_done, b * (G + 1) + max(g - 1, 0))
                    if g < G:
                        act.activation(pT[:, g % 2, :, 0:32], ppt[:, 0:128].rearrange("p (n r) -> p n r", n=GRP),
                                       ACT.Copy).then_inc(phi_done, 1)
                    else:
                        act.activation(pT[0:32, g % 2, 0, 0:32], ppt[0:32, 0:32], ACT.Copy).then_inc(phi_done, 1)

                def values_hi(b, g):
                    act.wait_ge(v_in[g % VR], b * (4 * 64) + 64 * (g // 2 + 1))
                    if not (isinstance(b, int) and b == 0 and g < 2):
                        act.wait_ge(pv_done, b * (G + 1) + max(g - 1, 0))
                    act.activation(vh[:, g % 2, :, :], vraw[:, g % VR, :, :], ACT.Copy).then_inc(vhi_done, 1)

                def row(kb, b):
                    for g in range(G):
                        if b is not None:
                            expo(b, g)
                        if kb is not None:
                            for h in range(3):
                                key_hi(kb, g, h)
                            if g >= 1:
                                scores_out(kb, g - 1)
                        if b is not None:
                            probs_hi(b, g)
                        if kb is not None:
                            key_hi(kb, g, 3)
                        if b is not None:
                            values_hi(b, g)
                    if b is not None:
                        expo(b, G)
                    if kb is not None:
                        scores_out(kb, G - 1)
                    if b is not None:
                        probs_hi(b, G)
                    if kb is not None:
                        scores_out(kb, G)
                    if b is not None:
                        act.wait_ge(pv_done, b * (G + 1) + G + 1)
                        if not (isinstance(b, int) and b == 0):
                            act.wait_ge(od_done, b + 0)
                        act.activation(osb[:], po[:, :], ACT.Copy).then_inc(o_out, 1)

                row(0, None)
                row(1, 0)
                with act.Fori(1, NB - 1) as b:
                    row(b + 1, b)
                row(None, NB - 1)

            @block.tensor
            def _(pe):
                def turn_keys(kb, g, h):
                    if h == 0:
                        pe.wait_ge(k_in[g % KR], kb * 128 + 64 * (g // KR + 1))
                    u = 4 * g + h
                    if not (isinstance(kb, int) and kb == 0 and u < 3):
                        pe.wait_ge(khi_done, kb * (4 * G) + (u - 2 if u >= 3 else 0))
                        pe.wait_ge(klo_done, kb * (4 * G) + (u - 2 if u >= 3 else 0))
                    for n in range(GRP):
                        ins = pe.transpose(pk[u % 3][:, n * PAGE:(n + 1) * PAGE],
                                           kraw[:, g % KR, n, h * P:(h + 1) * P], ident[:])
                    ins.then_inc(kt_done, 1)

                def scores(kb, g, h):
                    u = 4 * g + h
                    pe.wait_ge(khi_done, kb * (4 * G) + u + 1)
                    pe.wait_ge(klo_done, kb * (4 * G) + u + 1)
                    if h == 0:
                        if g == 0:
                            pe.wait_ge(qq_done, 4 * (kb + 1))
                        if g >= 2:
                            pe.wait_ge(sc_out, kb * (G + 1) + g - 1)
                        elif not (isinstance(kb, int) and kb == 0):
                            pe.wait_ge(sc_out, kb * (G + 1))
                    for n, (q, k) in enumerate(((qqh, kth), (qql, kth), (qqh, ktl))):
                        ins = pe.matmul(psc[g % 2][:, :], q[:, 32 * h:32 * h + 32], k[:, h, :],
                                        start=(h == 0 and n == 0), stop=(h == 3 and n == 2))
                    ins.then_inc(sc_unit, 1)

                def new_scores(kb):
                    pe.wait_ge(sc_out, kb * (G + 1) + G - 1)
                    for h in range(H):
                        for n, (q, k) in enumerate(((qqh, knh), (qql, knh), (qqh, knl))):
                            ins = pe.matmul(psc[0][:, 0:NS], q[:, 32 * h:32 * h + 32], k[:, h, :],
                                            start=(h == 0 and n == 0), stop=(h == 3 and n == 2))
                    ins.then_inc(new_done, 1)

                def turn_probs(b, g):
                    if g < G:
                        for n in range(GRP):
                            ins = pe.transpose(ppt[:, 32 * n:32 * n + 32], pr[:, g % 2, n * PAGE:(n + 1) * PAGE],
                                               ident[0:32, 0:32])
                    else:
                        ins = pe.transpose(ppt[0:NS, 0:32], pr[:, g % 2, 0:NS], ident[0:32, 0:32])
                    ins.then_inc(pt_done, 1)

                def probs_ready(b, g):
                    pe.wait_ge(exp_done, b * (G + 1) + g + 1)

                def values(b, g):
                    pe.wait_ge(phi_done, b * (G + 1) + g + 1)
                    pe.wait_ge(plo_done, b * (G + 1) + g + 1)
                    if g == 0 and not (isinstance(b, int) and b == 0):
                        pe.wait_ge(o_out, b + 0)
                    if g < G:
                        pe.wait_ge(vhi_done, b * G + g + 1)
                        pe.wait_ge(vlo_done, b * G + g + 1)
                        for n in range(GRP):
                            for v in (vh, vl):
                                ins = pe.matmul(po[:, :], pT[:, g % 2, n, :], v[:, g % 2, n, :],
                                                start=(g == 0 and n == 0 and v is vh), stop=False)
                    else:
                        pe.matmul(po[:, :], pT[0:NS, g % 2, 0, :], vnh[:], start=False, stop=False)
                        ins = pe.matmul(po[:, :], pT[0:NS, g % 2, 0, :], vnl[:], start=False, stop=True)
                    ins.then_inc(pv_done, 1)

                def row(kb, b):
                    for g in range(G):
                        if kb is not None:
                            for h in range(3):
                                if h == 2 and g == 0 and b is not None:
                                    probs_ready(b, 0)
                                turn_keys(kb, g, h)
                        elif g == 0:
                            probs_ready(b, 0)
                        if b is not None:
                            if g >= 1:
                                probs_ready(b, g)
                                values(b, g - 1)
                            turn_probs(b, g)
                        if kb is not None:
                            scores(kb, g, 0)
                            turn_keys(kb, g, 3)
                            for h in range(1, 4):
                                scores(kb, g, h)
                    if b is not None:
                        probs_ready(b, G)
                        values(b, G - 1)
                        turn_probs(b, G)
                    if kb is not None:
                        new_scores(kb)
                    if b is not None:
                        values(b, G)
                        pe.wait_ge(o_out, b + 1)
                        pe.wait_ge(sel_done, b + 1)
                        if not (isinstance(b, int) and b == 0):
                            pe.wait_ge(od_added, b + 0)
                        for h in range(H):
                            ins = pe.matmul(pod[:, h * DV:(h + 1) * DV], selc[:, h, :], osb[:, h * DV:(h + 1) * DV],
                                            start=True, stop=True)
                        ins.then_inc(od_done, 1)

                pe.wait_ge(setup, 1)
                for q in range(TS):
                    pe.matmul(pk[0][0:32, 0:PAGE], relq[:, q, :], hotp[:, q, :], start=(q == 0), stop=(q == TS - 1))
                for q in range(TS):
                    pe.matmul(pk[1][0:32, 0:NB * NS], relq[:, q, :], hotn[:, q, :], start=(q == 0),
                              stop=(q == TS - 1))
                pe.matmul(pk[2][0:H, 0:384], relb[:], oh, start=True, stop=True).then_inc(rel_done, 1)
                pe.wait_ge(band_out, 1)
                row(0, None)
                row(1, 0)
                with pe.Fori(1, NB - 1) as b:
                    row(b + 1, b)
                row(None, NB - 1)

            @block.vector
            def _(dve):
                link = [0]

                def linked(ins):
                    link[0] += 1
                    ins.then_inc(dch, 1)
                    dve.wait_ge(dch, link[0])

                dve.wait_ge(c_in, 16 * NCONST)
                linked(dve.tensor_tensor(
                    relq[:].rearrange("k q (h x) -> k q h x", h=H),
                    rowq[:].rearrange("k q (h x) -> k q h x", h=H),
                    relb[:].unsqueeze(1).unsqueeze(3).to_broadcast([32, TS, H, 8]), ALU.mult))
                dve.memset(od_s[:], 0.0)
                dve.memset(selc[:], 0.0)
                dve.memset(qqh[:].bitcast(F32), 0.0)
                dve.memset(qql[:].bitcast(F32), 0.0).then_inc(setup, 1)
                dve.wait_ge(setup, 1)
                new = slice(P * (TILES - 1) + S0, P * (TILES - 1) + S0 + NS)
                linked(dve.tensor_copy(knh[:], kT[:, :, new]))
                linked(dve.tensor_tensor(knl[:], kT[:, :, new], knh[:].bitcast(F32), ALU.subtract))
                linked(dve.tensor_copy(vnh[:], vn[:]))
                linked(dve.tensor_tensor(vnl[:], vn[:], vnh[:].bitcast(F32), ALU.subtract))
                dve.wait_ge(rel_done, 1)
                linked(dve.tensor_copy(dlast[:], pk[0][0:32, 0:PAGE]))
                linked(dve.tensor_tensor(dnew[:], dnew[:], pk[1][0:32, 0:NB * NS], ALU.add))
                dve.tensor_tensor(band[:], negp, pk[2][0:H, 0:384], ALU.add).then_inc(band_out, 1)
                dve.wait_ge(band_out, 1)
                SETUP = link[0]
                LINKS = 5
                at = [None, 0]

                def rowlinked(ins, b):
                    at[1] += 1
                    ins.then_inc(dch, 1)
                    dve.wait_ge(dch, b * LINKS + SETUP + at[1])

                def queries(kb):
                    if not (isinstance(kb, int) and kb == 0):
                        dve.wait_ge(new_done, kb + 0)
                    for m in range(2):
                        half = slice(DK * m, DK * m + DK)
                        of = qT[half, :, bass.ds(kb * TS + P * (TILES - 1) + S0, TS)]
                        view = lambda a: a[half, :].rearrange("p (h x) -> p h x", h=H)[:, :, 4 * m:4 * m + 4]
                        dve.tensor_copy(view(qqh), of).then_inc(qq_done, 1)
                        dve.wait_ge(qq_done, 4 * kb + 2 * m + 1)
                        dve.tensor_tensor(view(qql), of, view(qqh).bitcast(F32), ALU.subtract).then_inc(qq_done, 1)

                def key_lo(kb, g, h):
                    u = 4 * g + h
                    dve.wait_ge(khi_done, kb * (4 * G) + u + 1)
                    dve.tensor_tensor(ktl[:, h, :], pk[u % 3][:], kth[:, h, :].bitcast(F32), ALU.subtract)\
                       .then_inc(klo_done, 1)

                def group_max(kb, g):
                    n = NS if g == G else 512
                    s = sc[:, 512 * g:512 * g + n]
                    dve.wait_ge(sc_out, kb * (G + 1) + g + 1)
                    if g == G - 1:
                        last = sc[:, PAST - PAGE:PAST]
                        dve.tensor_tensor(last, last, dlast[:], ALU.add).then_inc(bias_done, 1)
                        dve.wait_ge(bias_done, 2 * kb + 1)
                    if g == G:
                        dve.tensor_tensor(s, s, dnew[:, bass.ds(kb * NS, NS)], ALU.add).then_inc(bias_done, 1)
                        dve.wait_ge(bias_done, 2 * kb + 2)
                    dve.tensor_reduce(mx[:, g:g + 1], s, AX.X, ALU.max).then_inc(max_done, 1)

                def row_max(b):
                    dve.wait_ge(max_done, b * (G + 1) + G + 1)
                    dve.tensor_reduce(negmax, mx[:], AX.X, ALU.max, negate=True).then_inc(negmax_done, 1)
                    dve.wait_ge(negmax_done, b + 1)

                def probs_lo(b, g):
                    dve.wait_ge(phi_done, b * (G + 1) + g + 1)
                    if g < G:
                        dve.tensor_tensor(pT[:, g % 2, :, 32:64], ppt[:, 0:128].rearrange("p (n r) -> p n r", n=GRP),
                                          pT[:, g % 2, :, 0:32].bitcast(F32), ALU.subtract).then_inc(plo_done, 1)
                    else:
                        dve.tensor_tensor(pT[0:32, g % 2, 0, 32:64], ppt[0:32, 0:32],
                                          pT[0:32, g % 2, 0, 0:32].bitcast(F32), ALU.subtract).then_inc(plo_done, 1)

                def values_lo(b, g):
                    dve.wait_ge(vhi_done, b * G + g + 1)
                    dve.tensor_tensor(vl[:, g % 2, :, :], vraw[:, g % VR, :, :], vh[:, g % 2, :, :].bitcast(F32),
                                      ALU.subtract).then_inc(vlo_done, 1)

                def row(kb, b):
                    if b is not None:
                        row_max(b)
                    if kb is not None:
                        queries(kb)
                    for g in range(G):
                        if kb is not None:
                            for h in range(3):
                                key_lo(kb, g, h)
                        if b is not None:
                            probs_lo(b, g)
                        if kb is not None:
                            key_lo(kb, g, 3)
                        if b is not None:
                            values_lo(b, g)
                        if kb is not None and g >= 1:
                            group_max(kb, g - 1)
                    if kb is not None:
                        group_max(kb, G - 1)
                    if b is not None:
                        probs_lo(b, G)
                        at[1] = 0
                        dve.wait_ge(exp_done, b * (G + 1) + G + 1)
                        rowlinked(dve.tensor_reduce(stat[0:32, 3:4], lsum[:], AX.X, ALU.add), b)
                        rowlinked(dve.reciprocal(rec, stat[0:32, 3:4]), b)
                        rowlinked(dve.scalar_tensor_tensor(out=stat[0:32, 4:5], in0=m01[0:32, 1:2],
                                                           scalar=nlam[0:32], in1=m01[0:32, 0:1],
                                                           op0=ALU.mult, op1=ALU.add), b)
                        rowlinked(dve.tensor_tensor(coef[0:32], rec, stat[0:32, 4:5], ALU.mult), b)
                        rowlinked(dve.tensor_copy(coef[32:64], coef[0:32]), b)
                        if not (isinstance(b, int) and b == 0):
                            dve.wait_ge(od_done, b + 0)
                        dve.tensor_scalar(selc[:, :, 0:NS], selT[:, bass.ds(b, 1), :, :].rearrange("p o h t -> p (o h) t"),
                                          coef, None, ALU.mult).then_inc(sel_done, 1)
                    if kb is not None:
                        group_max(kb, G)
                    if b is not None:
                        dve.wait_ge(od_done, b + 1)
                        dve.tensor_tensor(od_s[:], od_s[:], pod[0:NS, :], ALU.add).then_inc(od_added, 1)
                        dve.wait_ge(od_added, b + 1)

                row(0, None)
                row(1, 0)
                with dve.Fori(1, NB - 1) as b:
                    row(b + 1, b)
                row(None, NB - 1)

        mixT = sb(ctx, "mixT", [P, 2 * H, NTOK])

        with ExitStack() as st:
            vd = sb(st, "vd", [P, TILES, W])
            gd = sb(st, "gd", [P, 2, W])
            dband = sb(st, "dband", [P, H, 2 * P])
            dw = sb(st, "dw", [P, DV])
            e = sb(st, "e", [P, 2, 2, L])
            pT = sb(st, "pT_b", [P, TILES, P])
            ob = sb(st, "ob", [P, W])
            sqb = sb(st, "sqb", [P, W])
            mix = sb(st, "mix_b", [P, W])
            r4 = sb(st, "r4", [P, 3, 4])
            sm = sb(st, "sm", [P, 2, 8])
            pS = [ps(st, f"pS{m}", [P, 3 * 512]) for m in range(2)]
            pPT = ps(st, "pPT", [P, 512])
            pO = ps(st, "pO", [P, 512])
            b_in = sem("b_in")
            gd_in = [sem(f"gd_in{n}") for n in range(2)]
            sdone = sem("sdone")
            smax = sem("smax")
            sexp = sem("sexp")
            pdone = sem("pdone")
            ptd = sem("ptd")
            pto = sem("pto")
            odone = sem("odone")
            ocopy = sem("ocopy")
            osq = sem("osq")
            oms = sem("oms")
            orr = sem("orr")
            mixd = sem("mixd")
            mtd = sem("mtd")
            mto = sem("mto")
            tail_ready = sem("tail_ready")
            dch2 = sem("dchain_b")
            ach2 = sem("achain_b")
            units = [(i, h) for i in range(TILES) for h in range(H)]
            NU = len(units)

            def rq(i):
                return P if i < TILES - 1 else TAIL

            def keys(i):
                return P * i + rq(i)

            batches = [[(u, j0, min(j0 + 4, units[u][0] + 1)) for j0 in range(0, units[u][0] + 1, 4)]
                       for u in range(NU)]
            batch_no = {b: n for n, b in enumerate(x for bs in batches for x in bs)}

            def last_batch(u):
                return batch_no[batches[u][-1]]

            block = st.enter_context(nc.Block())

            @block.sync
            def _(sp):
                sp.dma_start(dw[:], diff_norm_w.to_broadcast([P, DV])).then_inc(b_in, 16)
                for h in range(H):
                    sp.dma_start(dband[:, h, :], skew[h, P - 1:P - 1 + P * 383].rearrange("(q x) -> q x", x=383)
                                 [:, 0:2 * P]).then_inc(b_in, 16)
                for i in range(TILES):
                    sp.dma_start(vd[0:rows_of(i), i, :], val_d[i, 0:rows_of(i), :]).then_inc(b_in, 16)
                for i in range(TILES):
                    if i >= 2:
                        sp.wait_ge(mixd, i - 1)
                    sp.dma_start(gd[0:rows_of(i), i % 2, :], gate_d[i, 0:rows_of(i), :]).then_inc(gd_in[i % 2], 16)

            @block.tensor
            def _(pe):
                def scores(u):
                    i, h = units[u]
                    nq, nk = rq(i), keys(i)
                    for m in range(2):
                        if u >= 1:
                            pe.wait_ge(sexp, 2 * (u - 1) + m + 1)
                        half = slice(DK * m, DK * m + DK)
                        for k0 in range(0, nk, 512):
                            kn = min(512, nk - k0)
                            ins = pe.matmul(pS[m][0:nq, k0:k0 + kn], qT[half, h, P * i:P * i + nq],
                                            kT[half, h, k0:k0 + kn], start=True, stop=True)
                        ins.then_inc(sdone, 1)

                def weigh(u):
                    i, h = units[u]
                    nq = rq(i)
                    pe.wait_ge(pdone, u + 1)
                    for b in batches[u]:
                        n = batch_no[b]
                        if n >= 1:
                            pe.wait_ge(pto, n)
                        if b is batches[u][0] and h == 2 and i >= 1:
                            pe.wait_ge(mto, i)
                        for j in range(b[1], b[2]):
                            kn = P if j < i else nq
                            ins = pe.transpose(pPT[0:kn, (j - b[1]) * P:(j - b[1]) * P + nq],
                                               e[0:nq, u % 2, 0, P * j:P * j + kn], ident[0:nq, 0:nq])
                        ins.then_inc(ptd, 1)
                    if h == 0 and i >= 1:
                        pe.wait_ge(ocopy, i)
                    for b in batches[u]:
                        pe.wait_ge(pto, batch_no[b] + 1)
                        for j in range(b[1], b[2]):
                            kn = P if j < i else nq
                            ins = pe.matmul(pO[0:nq, h * DV:(h + 1) * DV], pT[0:kn, j, 0:nq],
                                            vd[0:kn, j, h * DV:(h + 1) * DV], start=(j == 0), stop=(j == i))
                    ins.then_inc(odone, 1)

                def turn_mix(i):
                    r = rows_of(i)
                    pe.wait_ge(mixd, i + 1)
                    pe.wait_ge(pto, last_batch(min(4 * i + 5, NU - 1)) + 1)
                    for k in range(H):
                        ins = pe.transpose(pPT[:, k * P:k * P + r], mix[0:r, k * P:(k + 1) * P], ident[0:r, 0:r])
                    ins.then_inc(mtd, 1)

                pe.wait_ge(b_in, 16 * (1 + H + TILES))
                for u in range(NU + 1):
                    if u < NU:
                        scores(u)
                    if u >= 1:
                        weigh(u - 1)
                        if units[u - 1][1] == 1 and units[u - 1][0] >= 1:
                            turn_mix(units[u - 1][0] - 1)
                turn_mix(TILES - 1)

            @block.scalar
            def _(act):
                link = [0]

                def linked(ins):
                    link[0] += 1
                    ins.then_inc(ach2, 1)
                    act.wait_ge(ach2, link[0])

                def expo(u):
                    i, h = units[u]
                    nq, nk = rq(i), keys(i)
                    for m in range(2):
                        act.wait_ge(smax, 2 * u + m + 1)
                        if u >= 2:
                            act.wait_ge(pdone, u - 1)
                            if m == 0:
                                act.wait_ge(ptd, last_batch(u - 2) + 1)
                        act.activation(e[0:nq, u % 2, m, 0:nk], pS[m][0:nq, 0:nk], ACT.Exp,
                                       bias=sm[0:nq, u % 2, m:m + 1], accum_out=sm[0:nq, u % 2, 2 + m:3 + m])\
                           .then_inc(sexp, 1)

                def turned(u):
                    i, h = units[u]
                    nq = rq(i)
                    for b in batches[u]:
                        act.wait_ge(ptd, batch_no[b] + 1)
                        if u >= 1:
                            act.wait_ge(odone, u)
                        nb = b[2] - b[1]
                        full = [j for j in range(b[1], b[2]) if j < i or nq == P]
                        ins = None
                        if full:
                            ins = act.activation(
                                pT[:, b[1]:b[1] + len(full), 0:nq],
                                pPT[:, 0:len(full) * P].rearrange("p (j q) -> p j q", q=P)[:, :, 0:nq], ACT.Copy)
                        if len(full) < nb:
                            ins = act.activation(pT[0:nq, i, 0:nq],
                                                 pPT[0:nq, (i - b[1]) * P:(i - b[1]) * P + nq], ACT.Copy)
                        ins.then_inc(pto, 1)

                def out(i):
                    nq, r = rq(i), rows_of(i)
                    act.wait_ge(odone, 4 * i + 4)
                    if i >= 1:
                        act.wait_ge(mixd, i)
                    if i == TILES - 1:
                        act.wait_ge(tail_ready, 1)
                    act.activation(ob[0:nq, :], pO[0:nq, :], ACT.Copy).then_inc(ocopy, 1)
                    act.wait_ge(ocopy, i + 1)
                    act.activation(sqb[0:r, :], ob[0:r, :], ACT.Square).then_inc(osq, 1)

                def root(i):
                    r = rows_of(i)
                    act.wait_ge(oms, i + 1)
                    linked(act.activation(r4[0:r, 1, :], r4[0:r, 0, :], ACT.Ln))
                    act.activation(r4[0:r, 2, :], r4[0:r, 1, :], ACT.Exp, scale=-0.5).then_inc(orr, 1)

                def mixed(i):
                    r = rows_of(i)
                    act.wait_ge(mtd, i + 1)
                    act.activation(mixT[:, 0:H, P * i:P * i + r],
                                   pPT[:, :].rearrange("p (k t) -> p k t", k=H)[:, :, 0:r], ACT.Copy)\
                       .then_inc(mto, 1)

                for u in range(NU + 1):
                    if u < NU:
                        expo(u)
                    if u >= 2 and units[u - 2][1] == 3:
                        root(units[u - 2][0])
                    if u >= 1:
                        i, h = units[u - 1]
                        turned(u - 1)
                        if h == 3:
                            out(i)
                        if h == 1 and i >= 1:
                            mixed(i - 1)
                root(TILES - 1)
                mixed(TILES - 1)

            @block.vector
            def _(dve):
                link = [0]

                def linked(ins):
                    link[0] += 1
                    ins.then_inc(dch2, 1)
                    dve.wait_ge(dch2, link[0])

                def maxima(u):
                    i, h = units[u]
                    nq, nk = rq(i), keys(i)
                    for m in range(2):
                        dve.wait_ge(sdone, 2 * u + m + 1)
                        if u >= 2 and m == 0:
                            dve.wait_ge(pdone, u - 1)
                        w = min(nk, P + nq)
                        near = pS[m][0:nq, nk - w:nk]
                        d0 = P - (w - nq)
                        linked(dve.tensor_tensor(near, near, dband[0:nq, h, d0:d0 + w], ALU.add))
                        dve.tensor_reduce(sm[0:nq, u % 2, m:m + 1], pS[m][0:nq, 0:nk], AX.X, ALU.max, negate=True)\
                           .then_inc(smax, 1)

                def combine(u):
                    i, h = units[u]
                    nq, nk = rq(i), keys(i)
                    s = sm[0:nq, u % 2, :]
                    dve.wait_ge(sexp, 2 * u + 2)
                    linked(dve.reciprocal(s[:, 4:6], s[:, 2:4]))
                    linked(dve.tensor_scalar(s[:, 5:6], s[:, 5:6], nlam[0:nq], None, ALU.mult))
                    e1 = e[0:nq, u % 2, 1, 0:nk]
                    linked(dve.tensor_scalar(e1, e1, s[:, 5:6], None, ALU.mult))
                    dve.scalar_tensor_tensor(out=e[0:nq, u % 2, 0, 0:nk], in0=e[0:nq, u % 2, 0, 0:nk],
                                             scalar=s[:, 4:5], in1=e1, op0=ALU.mult, op1=ALU.add)\
                       .then_inc(pdone, 1)

                def norm(i):
                    r = rows_of(i)
                    dve.wait_ge(osq, i + 1)
                    linked(dve.tensor_reduce(r4[0:r, 0, :], sqb[0:r, :].rearrange("p (h d) -> p h d", h=H),
                                             AX.X, ALU.add))
                    dve.tensor_scalar(r4[0:r, 0, :], r4[0:r, 0, :], 1.0 / DV, EPS, ALU.mult, ALU.add)\
                       .then_inc(oms, 1)
                    h4 = lambda a: a[0:r, :].rearrange("p (h d) -> p h d", h=H)
                    dve.wait_ge(gd_in[i % 2], 16 * (i // 2 + 1))
                    if i >= 1:
                        dve.wait_ge(mtd, i)
                    linked(dve.tensor_tensor(h4(sqb), dw[0:r, :].unsqueeze(1).to_broadcast([r, H, DV]),
                                             gd[0:r, i % 2, :].rearrange("p (h d) -> p h d", h=H), ALU.mult))
                    dve.wait_ge(orr, i + 1)
                    linked(dve.tensor_tensor(h4(ob), h4(ob), r4[0:r, 2, :].unsqueeze(2).to_broadcast([r, H, DV]),
                                             ALU.mult))
                    dve.tensor_tensor(mix[0:r, :], ob[0:r, :], sqb[0:r, :], ALU.mult).then_inc(mixd, 1)
                    dve.wait_ge(mixd, i + 1)

                dve.wait_ge(b_in, 16 * (1 + H + TILES))
                linked(dve.tensor_scalar(dw[:], dw[:], 1.0 - LAM_INIT, None, ALU.mult))
                for u in range(NU + 1):
                    if u < NU:
                        maxima(u)
                    if u >= 2 and units[u - 2][1] == 3:
                        norm(units[u - 2][0])
                        if units[u - 2][0] == TILES - 2:
                            linked(dve.memset(ob[0:S0, :], 0.0))
                            dve.tensor_copy(ob[S0:S0 + NS, :], od_s[:]).then_inc(tail_ready, 1)
                    if u >= 1:
                        combine(u - 1)
                norm(TILES - 1)

        with ExitStack() as st:
            NL = LV + 1
            vg = sb(st, "vg", [P, 2, W])
            gg = sb(st, "gg", [P, 2, W])
            gw = sb(st, "gw", [P, DV])
            mask = sb(st, "mask", [P, LV, P])
            mask8 = sb(st, "mask8", [LASTW, LASTW])
            colm = sb(st, "colm", [P, NB + 1, LASTW])
            rowm = sb(st, "rowm", [LASTW, NB + 1])
            dd = sb(st, "dd", [P, NL, 2, 2, P])
            ff = sb(st, "ff", [P, 2, NL, 2, 2, P])
            ebl = sb(st, "ebl", [P, 2, 2, NB + 1])
            am = sb(st, "am", [P, 2, 2, 2, P])
            at = sb(st, "at", [P, 2, 2, 2, P])
            kd = sb(st, "kd", [P, 2, P])
            kd8 = sb(st, "kd8", [LASTW, NB + 1, 2 * P])
            q8 = sb(st, "q8", [P, 2, 2, NB + 1, LASTW])
            sp_ = sb(st, "state_p", [P, 2, DV])
            ss_ = sb(st, "state_s", [P, NB, 2, DV])
            og = sb(st, "og", [P, W])
            sqg = sb(st, "sqg", [P, W])
            mixg = sb(st, "mix_g", [P, W])
            r4g = sb(st, "r4g", [P, 3, 4])
            pA = ps(st, "pA", [P, 4, 512])
            qz = sb(st, "qz", [P, 2, 2, 2, P])
            pOg = ps(st, "pOg", [P, 512])
            pK = ps(st, "pK", [P, 512])
            pdS = ps(st, "pdS", [P, 512])
            pM = ps(st, "pM", [P, 512])
            g_in = sem("g_in")
            vg_in = [sem(f"vg_in{n}") for n in range(2)]
            dzero = sem("dzero")
            dexp_in = sem("dexp_in")
            dexp = sem("dexp")
            fdone = sem("fdone")
            adone = sem("adone")
            amask = sem("amask")
            atd = sem("atd")
            ogd = sem("ogd")
            ogc = sem("ogc")
            kdt = sem("kdt")
            kdo = sem("kdo")
            kd8d = sem("kd8d")
            q8d = sem("q8d")
            dsd = sem("dsd")
            sdn = sem("state_done")
            gsq = sem("gsq")
            gms = sem("gms")
            grr = sem("grr")
            mgd = sem("mgd")
            mgt = sem("mgt")
            mgo = sem("mgo")
            g_out = sem("g_out")
            dch3 = sem("dchain_g")
            ach3 = sem("achain_g")
            LVS = list(range(LV))

            def levels(i):
                return LVS if i < TILES - 1 else [LV - 1]

            A0 = lambda i, n: LV * i + n if i < TILES - 1 else LV * i

            block = st.enter_context(nc.Block())

            @block.sync
            def _(sp):
                sp.dma_start(gw[:], gla_norm_w.to_broadcast([P, DV])).then_inc(g_in, 16)
                sp.dma_start(mask[:], c_mask).then_inc(g_in, 16)
                sp.dma_start(mask8[:], c_mask8).then_inc(g_in, 16)
                sp.dma_start(colm[:], c_colm).then_inc(g_in, 16)
                sp.dma_start(rowm[:], c_rowm).then_inc(g_in, 16)
                for m in range(2):
                    sp.dma_start(ss_[:, :, m, :], state_gla[0].rearrange("b (m r) d e -> m (r d) b e", m=2)[m])\
                      .then_inc(g_in, 16)
                for i in range(TILES):
                    r = rows_of(i)
                    if i >= 2:
                        sp.wait_ge(mgd, i - 1)
                        sp.wait_ge(dsd, i - 1)
                        sp.wait_ge(ogd, i - 1)
                    sp.dma_start(vg[0:r, i % 2, :], val_g[i, 0:r, :]).then_inc(vg_in[i % 2], 16)
                    sp.dma_start(gg[0:r, i % 2, :], gate_g[i, 0:r, :]).then_inc(vg_in[i % 2], 16)
                sp.wait_ge(sdn, TILES + NB)
                for m in range(2):
                    sp.dma_start(s_sample[0].rearrange("b (m r) d e -> m (r d) b e", m=2)[m], ss_[:, :, m, :])\
                      .then_inc(g_out, 16)
                    sp.dma_start(s_prompt[0, 0].rearrange("(m r) d e -> m (r d) e", m=2)[m], sp_[:, m, :])\
                      .then_inc(g_out, 16)
                sp.wait_ge(g_out, 64)

            @block.tensor
            def _(pe):
                def products(i):
                    r = rows_of(i)
                    pe.wait_ge(fdone, i + 1)
                    f = ff[:, i % 2]
                    for n in levels(i):
                        if i >= 1:
                            pe.wait_ge(amask, A0(i - 1, n) + 1 if i < TILES - 1 else LV * i)
                        for h in range(H):
                            half = slice(DK * (h % 2), DK * (h % 2) + DK)
                            c0 = (n % 2) * 256 + (h // 2) * P
                            ins = pe.matmul(pA[0:r, 2 * (n // 2) + h % 2, c0:c0 + r], ff[half, i % 2, n, 1, h // 2, 0:r],
                                            ff[half, i % 2, n, 0, h // 2, 0:r], start=True, stop=True)
                        ins.then_inc(adone, 1)
                    if i >= 1:
                        pe.wait_ge(kdo, i)
                    for m in range(2):
                        ins = pe.transpose(pK[0:r, m * P:(m + 1) * P], ff[:, i % 2, LV, 1, m, 0:r], ident[:])
                    ins.then_inc(kdt, 1)

                def output(i):
                    r = rows_of(i)
                    if i < TILES - 1:
                        pe.wait_ge(atd, i + 1)
                    else:
                        pe.wait_ge(amask, LV * i + 1)
                    pe.wait_ge(vg_in[i % 2], 32 * (i // 2 + 1))
                    if i >= 1:
                        pe.wait_ge(sdn, i)
                        pe.wait_ge(ogc, i)
                    if i == TILES - 1:
                        pe.wait_ge(q8d, 1)
                    for h in range(H):
                        to = pOg[0:r, h * DV:(h + 1) * DV]
                        ins = pe.matmul(to, at[0:r, i % 2, h % 2, h // 2, 0:r], vg[0:r, i % 2, h * DV:(h + 1) * DV],
                                        start=True, stop=(i == 0))
                        if 0 < i < TILES - 1:
                            ins = pe.matmul(to, qz[:, i % 2, h % 2, h // 2, :], sp_[:, h // 2, :],
                                            start=False, stop=True)
                        if i == TILES - 1:
                            for c in range(NB + 1):
                                of = sp_[:, h // 2, :] if c == 0 else ss_[:, c - 1, h // 2, :]
                                ins = pe.matmul(to, q8[:, h % 2, h // 2, c, :], of, start=False, stop=(c == NB))
                    ins.then_inc(ogd, 1)

                def state(i):
                    r = rows_of(i)
                    pe.wait_ge(kdo, i + 1)
                    if i >= 1:
                        pe.wait_ge(sdn, i)
                    for c in range(1 if i < TILES - 1 else NB + 1):
                        if i == TILES - 1:
                            pe.wait_ge(kd8d, 1)
                            pe.wait_ge(sdn, i + c)
                        for m in range(2):
                            k = kd[:, m, :] if i < TILES - 1 else kd8[:, c, m * P:(m + 1) * P]
                            ins = pe.matmul(pdS[:, m * 256:(m + 1) * 256], k, vg[0:r, i % 2, m * 256:(m + 1) * 256],
                                            start=True, stop=True)
                        ins.then_inc(dsd, 1)

                def turn_mix(i):
                    r = rows_of(i)
                    pe.wait_ge(mgd, i + 1)
                    if i >= 1:
                        pe.wait_ge(mgo, i)
                    for k in range(H):
                        ins = pe.transpose(pM[:, k * P:k * P + r], mixg[0:r, k * P:(k + 1) * P], ident[0:r, 0:r])
                    ins.then_inc(mgt, 1)

                pe.wait_ge(g_in, 16 * 7)
                pe.wait_ge(dzero, 1)
                products(0)
                for i in range(TILES):
                    if i + 1 < TILES:
                        products(i + 1)
                    output(i)
                    state(i)
                    if i >= 1:
                        turn_mix(i - 1)
                turn_mix(TILES - 1)

            @block.scalar
            def _(act):
                link = [0]

                def linked(ins):
                    link[0] += 1
                    ins.then_inc(ach3, 1)
                    act.wait_ge(ach3, link[0])

                def decays(i):
                    r = rows_of(i)
                    act.wait_ge(dexp_in, i + 1)
                    if i >= 2:
                        act.wait_ge(ogd, i - 1)
                    n0 = 0 if i < TILES - 1 else LV - 1
                    for n in range(n0, NL):
                        linked(act.activation(ff[:, i % 2, n, :, :, 0:r], dd[:, n, :, :, 0:r], ACT.Exp))
                    if i < TILES - 1:
                        act.activation(ebl[:, i % 2, :, 0:1], bT[:, :, P * i + P - 1:P * i + P], ACT.Exp)\
                           .then_inc(dexp, 1)
                    else:
                        linked(act.activation(ebl[:, i % 2, :, 0:1], bT[:, :, P * i + TAIL - 1:P * i + TAIL], ACT.Exp))
                        act.activation(ebl[:, i % 2, :, 1:NB + 1],
                                       bT[:, :, P * i + S0:P * i + S0 + NS].rearrange("p m (b t) -> p m b t", t=TS)
                                       [:, :, :, TS - 1], ACT.Exp).then_inc(dexp, 1)

                def rest(i):
                    r = rows_of(i)
                    act.wait_ge(kdt, i + 1)
                    if i >= 1:
                        act.wait_ge(dsd, i)
                    act.activation(kd[0:r, :, :], pK[0:r, 0:2 * P].rearrange("p (m d) -> p m d", m=2), ACT.Copy)\
                       .then_inc(kdo, 1)
                    act.wait_ge(ogd, i + 1)
                    if i >= 1:
                        act.wait_ge(mgd, i)
                    act.activation(og[0:r, :], pOg[0:r, :], ACT.Copy).then_inc(ogc, 1)
                    act.wait_ge(ogc, i + 1)
                    act.activation(sqg[0:r, :], og[0:r, :], ACT.Square).then_inc(gsq, 1)
                    act.wait_ge(gms, i + 1)
                    linked(act.activation(r4g[0:r, 1, :], r4g[0:r, 0, :], ACT.Ln))
                    act.activation(r4g[0:r, 2, :], r4g[0:r, 1, :], ACT.Exp, scale=-0.5).then_inc(grr, 1)

                def mixed(i):
                    r = rows_of(i)
                    act.wait_ge(mgt, i + 1)
                    act.activation(mixT[:, H:2 * H, P * i:P * i + r],
                                   pM[:, :].rearrange("p (k t) -> p k t", k=H)[:, :, 0:r], ACT.Copy)\
                       .then_inc(mgo, 1)

                act.wait_ge(g_in, 16 * 7)
                decays(0)
                for i in range(TILES):
                    if i + 1 < TILES:
                        decays(i + 1)
                    rest(i)
                    if i >= 1:
                        mixed(i - 1)
                mixed(TILES - 1)

            @block.vector
            def _(dve):
                link = [0]

                def linked(ins):
                    link[0] += 1
                    ins.then_inc(dch3, 1)
                    dve.wait_ge(dch3, link[0])

                def exponents(i):
                    r = rows_of(i)
                    b = bT[:, :, P * i:P * i + r]
                    if i >= 1:
                        dve.wait_ge(dexp, i)
                    if i < TILES - 1:
                        for n, half in enumerate(HALVES):
                            v = lambda a: a.rearrange("p m (n two x) -> p m n two x", two=2, x=half)
                            nb = P // (2 * half)
                            to_q, to_k, bb = v(dd[:, n, 0]), v(dd[:, n, 1]), v(b)
                            if nb == 1:
                                for m in range(2):
                                    ref = b[:, m, half - 1:half].to_broadcast([P, half])
                                    dve.tensor_tensor(dd[:, n, 0, m, half:P], b[:, m, half:P], ref, ALU.subtract)
                                    dve.tensor_tensor(dd[:, n, 1, m, 0:half], ref, b[:, m, 0:half], ALU.subtract)
                                continue
                            ref = bb[:, :, :, 0, half - 1:half].to_broadcast([P, 2, nb, half])
                            dve.tensor_tensor(to_q[:, :, :, 1, :], bb[:, :, :, 1, :], ref, ALU.subtract)
                            dve.tensor_tensor(to_k[:, :, :, 0, :], ref, bb[:, :, :, 0, :], ALU.subtract)
                        v = lambda a: a.rearrange("p m (n x) -> p m n x", x=DIAG)
                        ref = v(b)[:, :, :, DIAG // 2 - 1:DIAG // 2].to_broadcast([P, 2, P // DIAG, DIAG])
                        dve.tensor_tensor(v(dd[:, LV - 1, 0]), v(b), ref, ALU.subtract)
                        linked(dve.tensor_tensor(v(dd[:, LV - 1, 1]), ref, v(b), ALU.subtract))
                        last = b[:, :, P - 1:P].to_broadcast([P, 2, P])
                        dve.tensor_tensor(dd[:, LV, 1], last, b, ALU.subtract)
                    else:
                        t, s = slice(0, TAIL), slice(S0, S0 + NS)
                        linked(dve.memset(dd[:, LV - 1:NL, :, :, 0:r], 0.0))
                        ref = b[:, :, TAIL // 2 - 1:TAIL // 2].to_broadcast([P, 2, TAIL])
                        dve.tensor_tensor(dd[:, LV - 1, 0, :, t], b[:, :, t], ref, ALU.subtract)
                        dve.tensor_tensor(dd[:, LV - 1, 1, :, t], ref, b[:, :, t], ALU.subtract)
                        dve.tensor_copy(dd[:, LV - 1, 0, :, s], b[:, :, s])
                        linked(dve.tensor_scalar(dd[:, LV - 1, 1, :, s], b[:, :, s], -1.0, None, ALU.mult))
                        dve.tensor_tensor(dd[:, LV, 1, :, t], b[:, :, TAIL - 1:TAIL].to_broadcast([P, 2, TAIL]),
                                          b[:, :, t], ALU.subtract)
                        v = lambda a: a.rearrange("p m (b t) -> p m b t", t=TS)
                        dve.tensor_tensor(v(dd[:, LV, 1, :, s]), v(b[:, :, s])[:, :, :, TS - 1:TS]
                                          .to_broadcast([P, 2, NB, TS]), v(b[:, :, s]), ALU.subtract)
                    dve.tensor_copy(dd[:, LV, 0, :, 0:r], b)
                    dve.tensor_scalar(dd[:, LV - 1, :, :, 0:r], dd[:, LV - 1, :, :, 0:r], 80.0, None, ALU.min)\
                       .then_inc(dexp_in, 1)

                def factors(i):
                    r = rows_of(i)
                    dve.wait_ge(dexp, i + 1)
                    n0 = 0 if i < TILES - 1 else LV - 1
                    t = slice(P * i, P * i + r)
                    for hh in range(2):
                        half = slice(DK * hh, DK * hh + DK)
                        dve.tensor_tensor(qz[half, i % 2, hh, :, 0:r], ff[half, i % 2, LV, 0, :, 0:r], gqT[half, :, t],
                                          ALU.mult)
                    to = ff[:, i % 2, n0:LV, 0, :, 0:r]
                    dve.tensor_tensor(to, to, gqT[:, :, t].unsqueeze(1).to_broadcast([P, LV - n0, 2, r]), ALU.mult)
                    to = ff[:, i % 2, n0:NL, 1, :, 0:r]
                    dve.tensor_tensor(to, to, gkT[:, :, t].unsqueeze(1).to_broadcast([P, NL - n0, 2, r]), ALU.mult)\
                       .then_inc(fdone, 1)
                    if i == TILES - 1:
                        dve.wait_ge(fdone, i + 1)
                        for hh in range(2):
                            for m in range(2):
                                ins = dve.tensor_tensor(q8[:, hh, m], qz[:, i % 2, hh, m, 0:r].unsqueeze(1)
                                                        .to_broadcast([P, NB + 1, r]), colm[:], ALU.mult)
                        ins.then_inc(q8d, 1)

                def masks(i):
                    r = rows_of(i)
                    dve.wait_ge(adone, A0(i, levels(i)[-1]) + 1 if i < TILES - 1 else LV * i + 1)
                    sums = at[0:r, i % 2, :, :, 0:r]
                    if i >= 2:
                        dve.wait_ge(ogd, i - 1)
                    for x, n in enumerate(levels(i)):
                        mk = (mask[:, n, :] if r == P else mask8[:, :]).unsqueeze(1).unsqueeze(1)\
                            .to_broadcast([r, 2, 2, r])
                        of = pA[0:r, 2 * (n // 2):2 * (n // 2) + 2, (n % 2) * 256:(n % 2) * 256 + 256]\
                            .rearrange("p a (m t) -> p a m t", m=2)[:, :, :, 0:r]
                        to = sums if x == 0 else am[0:r, x % 2, :, :, 0:r]
                        dve.tensor_tensor(to, of, mk, ALU.mult).then_inc(amask, 1)
                        dve.wait_ge(amask, A0(i, n) + 1 if i < TILES - 1 else LV * i + 1)
                        if x:
                            ins = dve.tensor_tensor(sums, sums, to, ALU.add)
                            if n < LV - 1:
                                linked(ins)
                            else:
                                ins.then_inc(atd, 1)

                def state(i):
                    r = rows_of(i)
                    if i == TILES - 1:
                        dve.wait_ge(kdo, i + 1)
                        dve.tensor_tensor(kd8[:], kd[0:r].rearrange("p m d -> p (m d)").unsqueeze(1)
                                          .to_broadcast([r, NB + 1, 2 * P]),
                                          rowm[:].unsqueeze(2).to_broadcast([r, NB + 1, 2 * P]), ALU.mult)\
                           .then_inc(kd8d, 1)
                        dve.wait_ge(ogd, i + 1)
                    for c in range(1 if i < TILES - 1 else NB + 1):
                        dve.wait_ge(dsd, i + c + 1)
                        if c == 0 and i >= 1:
                            dve.wait_ge(ogd, i + 1)
                        for m in range(2):
                            for hh in range(2):
                                half = slice(DK * hh, DK * hh + DK)
                                ds = pdS[half, m * 256 + hh * P:m * 256 + hh * P + P]
                                to = sp_[half, m, :] if c == 0 else ss_[half, c - 1, m, :]
                                if i == 0:
                                    ins = dve.tensor_copy(to, ds)
                                else:
                                    ins = dve.scalar_tensor_tensor(out=to, in0=to,
                                                                   scalar=ebl[half, i % 2, m, c:c + 1],
                                                                   in1=ds, op0=ALU.mult, op1=ALU.add)
                        ins.then_inc(sdn, 1)

                def norm(i):
                    r = rows_of(i)
                    h4 = lambda a: a[0:r, :].rearrange("p (h d) -> p h d", h=H)
                    dve.wait_ge(gsq, i + 1)
                    linked(dve.tensor_reduce(r4g[0:r, 0, :], h4(sqg), AX.X, ALU.add))
                    dve.tensor_scalar(r4g[0:r, 0, :], r4g[0:r, 0, :], 1.0 / DV, EPS, ALU.mult, ALU.add)\
                       .then_inc(gms, 1)
                    dve.wait_ge(vg_in[i % 2], 32 * (i // 2 + 1))
                    linked(dve.tensor_tensor(h4(sqg), gw[0:r, :].unsqueeze(1).to_broadcast([r, H, DV]),
                                             gg[0:r, i % 2, :].rearrange("p (h d) -> p h d", h=H), ALU.mult))
                    dve.wait_ge(grr, i + 1)
                    linked(dve.tensor_tensor(h4(og), h4(og), r4g[0:r, 2, :].unsqueeze(2).to_broadcast([r, H, DV]),
                                             ALU.mult))
                    if i >= 1:
                        dve.wait_ge(mgt, i)
                    dve.tensor_tensor(mixg[0:r, :], og[0:r, :], sqg[0:r, :], ALU.mult).then_inc(mgd, 1)
                    dve.wait_ge(mgd, i + 1)

                dve.wait_ge(g_in, 16 * 7)
                linked(dve.memset(dd[:], 0.0))
                dve.memset(qz[:], 0.0).then_inc(dzero, 1)
                dve.wait_ge(dzero, 1)
                exponents(0)
                factors(0)
                for i in range(TILES):
                    if i + 1 < TILES:
                        exponents(i + 1)
                    masks(i)
                    if i + 1 < TILES:
                        factors(i + 1)
                    state(i)
                    norm(i)

        with ExitStack() as st:
            wor = sb(st, "wor", [P, 2, D])
            woh = sb(st, "woh", [P, KT, D], F32R)
            wol = sb(st, "wol", [P, KT, D], F32R)
            mh = sb(st, "mh", [P, 2, KT, P], F32R)
            ml = sb(st, "ml", [P, 2, KT, P], F32R)
            xr = sb(st, "xr", [P, 2, D])
            pY = [ps(st, f"pY{n}", [P, 512]) for n in range(4)]
            wo_in = [sem(f"wo_in{n}") for n in range(2)]
            xr_in = [sem(f"xr_in{n}") for n in range(2)]
            woh_d = sem("woh_d")
            wol_d = sem("wol_d")
            mh_d = sem("mh_d")
            ml_d = sem("ml_d")
            y_done = sem("y_done")
            y_sum = sem("y_sum")
            y_out = [sem(f"y_out{n}") for n in range(2)]

            def parts(i):
                if i == 0:
                    return [(NMETA, P, x_prompt[0, 0:P - NMETA, :], y_prompt[0, 0:P - NMETA, :])]
                if i < TILES - 1:
                    rows = slice(P * i - NMETA, P * (i + 1) - NMETA)
                    return [(0, P, x_prompt[0, rows, :], y_prompt[0, rows, :])]
                return [(0, TAIL, x_prompt[0, SEQ - TAIL:SEQ, :], y_prompt[0, SEQ - TAIL:SEQ, :]),
                        (S0, S0 + NS, x_sample.rearrange("b t d -> (b t) d"),
                         y_sample.rearrange("b t d -> (b t) d"))]

            def moved(i):
                return 16 * sum(len(parts(j)) for j in range(i % 2, i + 1, 2))

            block = st.enter_context(nc.Block())
            xz = sem("xr_zero")

            @block.sync
            def _(sp):
                for k in range(KT):
                    if k >= 2:
                        sp.wait_ge(woh_d, k - 1)
                        sp.wait_ge(wol_d, k - 1)
                    sp.dma_start(wor[:, k % 2, :], w_out[0, k * P:(k + 1) * P, :]).then_inc(wo_in[k % 2], 16)
                sp.wait_ge(xz, 1)
                for i in range(TILES + 1):
                    if i < TILES:
                        if i >= 2:
                            sp.wait_ge(y_out[i % 2], moved(i - 2))
                        if i == TILES - 1:
                            sp.wait_ge(xz, 2)
                        for a, b, x, _ in parts(i):
                            sp.dma_start(xr[a:b, i % 2, :], x).then_inc(xr_in[i % 2], 16)
                    if i >= 1:
                        sp.wait_ge(y_sum, 2 * i)
                        for a, b, _, y in parts(i - 1):
                            sp.dma_start(y, xr[a:b, (i - 1) % 2, :]).then_inc(y_out[(i - 1) % 2], 16)
                sp.wait_ge(y_out[0], moved(TILES - 1))
                sp.wait_ge(y_out[1], moved(TILES - 2))

            @block.scalar
            def _(act):
                def mix_hi(i):
                    r = rows_of(i)
                    if i >= 2:
                        act.wait_ge(y_done, 2 * (i - 1))
                    act.activation(mh[:, i % 2, :, 0:r], mixT[:, :, P * i:P * i + r], ACT.Copy).then_inc(mh_d, 1)

                mix_hi(0)
                for k in range(KT):
                    act.wait_ge(wo_in[k % 2], 16 * (k // 2 + 1))
                    act.activation(woh[:, k, :], wor[:, k % 2, :], ACT.Copy).then_inc(woh_d, 1)
                for i in range(1, TILES):
                    mix_hi(i)

            @block.vector
            def _(dve):
                def mix_lo(i):
                    r = rows_of(i)
                    dve.wait_ge(mh_d, i + 1)
                    dve.tensor_tensor(ml[:, i % 2, :, 0:r], mixT[:, :, P * i:P * i + r],
                                      mh[:, i % 2, :, 0:r].bitcast(F32), ALU.subtract).then_inc(ml_d, 1)

                def add(i):
                    r = rows_of(i)
                    for n in range(2):
                        dve.wait_ge(y_done, 2 * i + n + 1)
                        dve.wait_ge(xr_in[i % 2], moved(i))
                        x = xr[0:r, i % 2, n * 512:(n + 1) * 512]
                        dve.tensor_tensor(x, x, pY[2 * (i % 2) + n][0:r, :], ALU.add).then_inc(y_sum, 1)

                dve.memset(xr[0:S0, 0, :], 0.0).then_inc(xz, 1)
                mix_lo(0)
                for k in range(KT):
                    dve.wait_ge(woh_d, k + 1)
                    dve.tensor_tensor(wol[:, k, :], wor[:, k % 2, :], woh[:, k, :].bitcast(F32), ALU.subtract)\
                       .then_inc(wol_d, 1)
                for i in range(TILES):
                    if i + 1 < TILES:
                        mix_lo(i + 1)
                    add(i)
                    if i == TILES - 3:
                        dve.wait_ge(y_out[0], moved(TILES - 3))
                        dve.memset(xr[0:S0, 0, :], 0.0).then_inc(xz, 1)

            @block.tensor
            def _(pe):
                for i in range(TILES):
                    r = rows_of(i)
                    pe.wait_ge(mh_d, i + 1)
                    pe.wait_ge(ml_d, i + 1)
                    for n in range(2):
                        if i >= 2:
                            pe.wait_ge(y_sum, 2 * (i - 2) + n + 1)
                        for k in range(KT):
                            if i == 0 and n == 0:
                                pe.wait_ge(woh_d, k + 1)
                                pe.wait_ge(wol_d, k + 1)
                            for x, (a, b) in enumerate(((mh, woh), (ml, woh), (mh, wol))):
                                ins = pe.matmul(pY[2 * (i % 2) + n][0:r, :], a[:, i % 2, k, 0:r],
                                                b[:, k, n * 512:(n + 1) * 512], start=(k == 0 and x == 0),
                                                stop=(k == KT - 1 and x == 2))
                        ins.then_inc(y_done, 1)


def shape_constants():
    import numpy as np
    f = np.float32
    c = {"c_ident": np.eye(P, dtype=f)}
    a = np.arange(P)
    c["c_cum"] = ((a[:, None] <= a[None, :]) / 16.0).astype(f)
    a8 = np.arange(LASTW)
    chunk = np.where(a8 < TAIL, 0, np.where(a8 < S0, 100 + a8, 1 + (a8 - S0) // TS))
    same = (chunk[:, None] == chunk[None, :]) & (a8[:, None] <= a8[None, :])
    c["c_cum8"] = (same / 16.0).astype(f)
    m = np.zeros((P, LV, P), f)
    s, t = a[:, None], a[None, :]
    for n, half in enumerate(HALVES):
        m[:, n, :] = (s // (2 * half) == t // (2 * half)) & (s % (2 * half) < half) & (t % (2 * half) >= half)
    m[:, LV - 1, :] = (s // DIAG == t // DIAG) & (s <= t)
    c["c_mask"] = m
    c["c_mask8"] = same.astype(f)
    n = np.arange(0, PAST + TS)
    nf = np.maximum(n, 1).astype(f)
    large = 16 + (np.log(nf / f(16)) / f(math.log(128 / 16)) * f(16)).astype(np.int32)
    bucket = np.where(n < 16, n, np.minimum(large, 31))

    def hot(n):
        o = np.zeros((32, n.size), f)
        ok = n.ravel() >= 0
        o[bucket[np.maximum(n.ravel(), 0)], np.arange(n.size)] = 1
        o[31, :] -= 1
        o[:, ~ok] = 0
        return o
    d = 255 - np.arange(384)
    c["c_oh"] = hot(d)
    c["c_negp"] = np.broadcast_to(np.where(d < 0, NEG, 0).astype(f), (H, 384)).copy()
    q = np.arange(TS)
    c["c_hotp"] = hot(PAST + q[:, None] - (PAST - PAGE + np.arange(PAGE))[None, :]).reshape(32, TS * PAGE)
    j = np.arange(NS)
    dn = np.stack([np.where((j // TS == b), q[:, None] - (j % TS)[None, :], -1) for b in range(NB)], 1)
    c["c_hotn"] = hot(dn).reshape(32, TS, NB * NS)
    row = np.arange(32)
    neg = np.where(dn < 0, NEG, 0).astype(f)
    c["c_negn"] = neg[row % TS].reshape(32, NB * NS)
    c["c_rowq"] = np.broadcast_to((row[None, :] % TS == q[:, None]).astype(f), (32, TS, 32)).copy()
    r2 = np.arange(64) % 32
    sel = np.zeros((64, NB, H, NS), f)
    for b in range(NB):
        for h in range(H):
            sel[:, b, h, :] = (r2[:, None] // 8 == h) & (b * TS + r2[:, None] % TS == np.arange(NS)[None, :])
    c["c_selT"] = sel
    c["c_m01"] = np.stack([(r2 // 4 % 2 == 0), (r2 // 4 % 2 == 1)], 1).astype(f)
    own = (chunk[None, :] == np.arange(NB + 1)[:, None]).astype(f)
    c["c_colm"] = np.broadcast_to(own, (P, NB + 1, LASTW)).copy()
    c["c_rowm"] = own.T.copy()
    return c


_INS = ["x_prompt", "x_sample", "cache_k", "cache_v", "state_gla", "page_table", "meta_tokens", "rel_bias",
        "norm_w", "w_in", "q_norm_w", "k_norm_w", "lam_q", "lam_k", "diff_norm_w", "gla_wa2", "gla_ba",
        "gla_norm_w", "w_out"]
_CONSTS = ["c_ident", "c_cum", "c_cum8", "c_mask", "c_mask8", "c_oh", "c_hotp", "c_hotn", "c_negn", "c_negp",
           "c_rowq", "c_selT", "c_colm", "c_rowm", "c_m01"]
_OUTS = [(1, SEQ, D), (NB, TS, D), (1, 1, L, H, 2 * DK), (1, 1, L, H, DV), (1, 1, H, DK, DV),
         (1, NB, TS, H, 2 * DK), (1, NB, TS, H, DV), (1, NB, H, DK, DV)]


def kernel(**inputs):
    import numpy as np
    import concourse.bacc as bacc
    from concourse.bass_utils import run_bass_kernel_spmd

    nc = bacc.Bacc("TRN2", target_bir_lowering=False, num_devices=1)
    consts = shape_constants()
    arrays, args = {}, []
    for name in _INS + _CONSTS:
        a = np.ascontiguousarray(inputs[name] if name in inputs else consts[name])
        arrays[f"in_{name}"] = a
        args.append(nc.dram_tensor(f"in_{name}", a.shape, mybir.dt.from_np(a.dtype), kind="ExternalInput").ap())
    for n, shape in enumerate(_OUTS):
        args.append(nc.dram_tensor(f"out_{n}", shape, F32, kind="ExternalOutput").ap())
    hymba_kernel(nc, *args)
    r = run_bass_kernel_spmd(nc, [arrays], core_ids=[0])
    return tuple(r.results[0][f"out_{n}"] for n in range(len(_OUTS)))
```

```python
from contextlib import ExitStack
import math

import concourse.bass as bass
from concourse import mybir

F32 = mybir.dt.float32
F32R = mybir.dt.float32r
I32 = mybir.dt.int32
ALU = mybir.AluOpType
ACT = mybir.ActivationFunctionType
AX = mybir.AxisListType

P = 128
D = 1024
KT = D // P
NMETA, SEQ = 16, 1024
L = NMETA + SEQ
NB, TS = 8, 4
NS = NB * TS
TILES = L // P + 1
TAIL = L - P * (TILES - 1)
LASTW = 64
S0 = 32
NTOK = P * (TILES - 1) + LASTW
H, DK, DV = 4, 64, 128
W = H * DV
PAGE, NPAGES, POOL = 128, 32, 320
GRP = 4
G = NPAGES // GRP
PAST = PAGE * NPAGES
DIN = 3600
CB = 256
EPS = 1e-6
LAM_INIT = 0.8 - 0.6 * math.exp(0.0)
NEG = -1e30

HALVES = (64, 32, 16)
DIAG = 16
LV = len(HALVES) + 1

KINDS = ["q", "q", "k", "k", "v", "v", "dg", "dg", "gq", "gk", "gv", "gv", "gg", "gg"]

W_AT = [CB * c for c in range(len(KINDS) + 1)]


def rows_of(i):
    return P if i < TILES - 1 else LASTW


def hymba_kernel(nc, x_prompt, x_sample, cache_k, cache_v, state_gla, page_table, meta_tokens, rel_bias,
                 norm_w, w_in, q_norm_w, k_norm_w, lam_q, lam_k, diff_norm_w, gla_wa2, gla_ba, gla_norm_w,
                 w_out, c_ident, c_cum, c_cum8, c_mask, c_mask8, c_oh, c_hotp, c_hotn, c_negn, c_negp, c_rowq, c_selT,
                 c_colm, c_rowm, c_m01,
                 y_prompt, y_sample, k_prompt, v_prompt, s_prompt, k_sample, v_sample, s_sample):
    ctx = ExitStack()
    with ctx:
        def sem(name):
            return ctx.enter_context(nc.semaphore(name))

        def sb(stack, name, shape, dt=F32):
            return stack.enter_context(nc.sbuf_tensor(name, shape, dt))

        def ps(stack, name, shape):
            return stack.enter_context(nc.psum_tensor(name, shape, F32))

        def dram(name, shape):
            return nc.dram_tensor(name, shape, F32, kind="Internal").ap()

        gate_d = dram("gate_d", (TILES, P, W))
        gate_g = dram("gate_g", (TILES, P, W))
        val_g = dram("val_g", (TILES, P, W))
        val_d = dram("val_d", (TILES, P, W))
        skew = dram("skew", (H, P * 384))

        ident = sb(ctx, "ident", [P, P])
        qT = sb(ctx, "qT", [P, H, NTOK])
        kT = sb(ctx, "kT", [P, H, NTOK])
        gqT = sb(ctx, "gqT", [P, 2, NTOK])
        gkT = sb(ctx, "gkT", [P, 2, NTOK])
        bT = sb(ctx, "bT", [P, 2, NTOK])
        lam = sb(ctx, "lam", [P, 8])
        nlam = lam[:, 7:8]
        od_s = sb(ctx, "od_s", [NS, W])

        with ExitStack() as st:
            xTh = sb(st, "xTh", [P, KT, NTOK], F32R)
            xTl = sb(st, "xTl", [P, KT, NTOK], F32R)
            xb = sb(st, "xb", [P, 2, D])
            wraw = sb(st, "wraw", [P, 2, KT, CB])
            wh = sb(st, "wh", [P, 2, KT, CB], F32R)
            wl = sb(st, "wl", [P, 2, KT, CB], F32R)
            squares = sb(st, "squares", [P, D])
            nw = sb(st, "nw", [P, KT])
            qwr = sb(st, "qwr", [P, 2, CB])
            ss = sb(st, "ss", [P, 4, TILES])
            sq = sb(st, "sq", [P, 2, CB])
            rms = sb(st, "rms", [P, 2, 3, 4])
            nrm = sb(st, "nrm", [P, CB])
            nat = sb(st, "nat", [P, 3, CB])
            gaT = sb(st, "gaT", [17, NTOK])
            wa2 = sb(st, "wa2", [17, CB])
            cum = sb(st, "cum", [P, P])
            cum8 = sb(st, "cum8", [LASTW, LASTW])
            lg = squares[:, 0:2 * CB].rearrange("p (a c) -> p a c", a=2)
            lgm = squares[:, 2 * CB:4 * CB].rearrange("p (a c) -> p a c", a=2)
            lmv = sb(st, "lmv", [P, 4, P])
            pz = [ps(st, f"pz{n}", [P, 512]) for n in range(3)]
            pt = ps(st, "pt", [P, 2, 512])
            pn = ps(st, "pn", [P, 2, 512])

            x_loaded = [sem(f"x_loaded{n}") for n in range(2)]
            x_zero = sem("x_zero")
            consts_in = sem("consts_in")
            w_loaded = [sem(f"w_loaded{n}") for n in range(2)]
            sumsq_done = sem("sumsq_done")
            meansq_done = sem("meansq_done")
            ln_done = sem("ln_done")
            rstd_done = sem("rstd_done")
            hn_done = sem("hn_done")
            xt_done = sem("xt_done")
            xhi_done = sem("xhi_done")
            xlo_done = sem("xlo_done")
            whi_done = sem("whi_done")
            wlo_done = sem("wlo_done")
            z_done = sem("z_done")
            turned_out = sem("turned_out")
            sq_done = sem("sq_done")
            ms_done = sem("ms_done")
            r_done = sem("r_done")
            nat_done = sem("nat_done")
            nt_done = sem("nt_done")
            nt_out = sem("nt_out")
            nat_stored = [sem(f"nat_stored{n}") for n in range(3)]
            dchain = sem("dchain_a")
            achain = sem("achain_a")
            ga_done = sem("ga_done")
            log_in = sem("log_in")
            lnexp_done = sem("lnexp_done")
            lg_done = sem("lg_done")
            cum_done = sem("cum_done")
            cum_out = sem("cum_out")
            lam_exp = sem("lam_exp")
            lam_sum = sem("lam_sum")

            natural = [(c, i) for c, k in enumerate(KINDS) if k not in ("gq", "gk") for i in range(TILES)]
            turned = [c for c, k in enumerate(KINDS) if k in ("gq", "gk")]
            NN = len(natural)

            def kind(s):
                return KINDS[natural[s][0]]

            def count(kinds, s):
                return sum(1 for t in range(s + 1) if kind(t) in kinds)

            ACTIVE = ("q", "k", "dg", "gg")
            CH = [(0, 512), (512, 512), (1024, LASTW)]
            uses = []
            for c, k in enumerate(KINDS):
                if k in ("gq", "gk"):
                    uses += [("t", c, m, n) for m in range(2) for n in range(3)]
                else:
                    uses += [("n", c, i) for i in range(TILES)]
            uses += [("a", n) for n in range(3)]
            uses += [("l", i) for i in range(TILES)]
            use_of = {u: n for n, u in enumerate(uses)}
            step_of = {x: n for n, x in enumerate(natural)}
            turned_uses = [u for u in uses if u[0] in "ta"]
            BLOCK_END = [1 + max(n for n, u in enumerate(uses) if u[0] in "nt" and u[1] == c)
                         for c in range(len(KINDS))]
            X_IN = [32, 16, 48, 32, 64, 48, 80, 64, 112]

            def wait_z(eng, u):
                if u < 3:
                    return
                before = uses[u - 3]
                if before[0] == "n":
                    eng.wait_ge(nat_done, step_of[before[1:]] + 1)
                elif before[0] in "ta":
                    eng.wait_ge(turned_out, turned_uses.index(before) + 1)
                else:
                    eng.wait_ge(lg_done, before[1] + 1)

            def z_at(n):
                return pz[n % 3]

            def stored(s):
                c, i = natural[s]
                k = KINDS[c]
                last = i == TILES - 1
                return {"q": 0, "k": 1 + last, "v": 2 + last}.get(k, 1)

            def stored_upto(s, slot):
                return sum(stored(t) for t in range(s + 1) if t % 3 == slot)

            block = st.enter_context(nc.Block())

            @block.sync
            def _(sp):
                sp.dma_start(ident[:], c_ident).then_inc(consts_in, 16)
                sp.dma_start(nw[:], norm_w.rearrange("a (t p) -> p (a t)", p=P), allow_slow_non_contiguous=True).then_inc(consts_in, 16)
                for m in range(2):
                    sp.dma_start(lmv[:, m, :], lam_q.rearrange("a m d -> a (m d)").to_broadcast([P, P]) if m == 0
                                 else lam_k.rearrange("a m d -> a (m d)").to_broadcast([P, P])).then_inc(consts_in, 16)
                for n, wt in enumerate((q_norm_w, k_norm_w)):
                    for h in range(2):
                        sp.dma_start(qwr[:, n, h * P:(h + 1) * P],
                                     wt.rearrange("a m d -> a (m d)").to_broadcast([P, P])).then_inc(consts_in, 16)
                sp.dma_start(cum[:], c_cum).then_inc(consts_in, 16)
                sp.dma_start(cum8[:], c_cum8).then_inc(consts_in, 16)
                sp.dma_start(wa2[0:16, :], gla_wa2[0]).then_inc(consts_in, 16)
                sp.dma_start(wa2[16:17, :], gla_ba).then_inc(consts_in, 16)

                def load_x(i):
                    if i >= 2:
                        sp.wait_ge(xt_done, 2 * (i - 1))
                    if i == 0:
                        sp.dma_start(xb[0:NMETA, 0, :], meta_tokens).then_inc(x_loaded[0], 16)
                        sp.dma_start(xb[NMETA:P, 0, :], x_prompt[0, 0:P - NMETA, :]).then_inc(x_loaded[0], 16)
                    elif i < TILES - 1:
                        sp.dma_start(xb[:, i % 2, :], x_prompt[0, P * i - NMETA:P * (i + 1) - NMETA, :])\
                          .then_inc(x_loaded[i % 2], 16)
                    else:
                        sp.wait_ge(x_zero, 1)
                        sp.dma_start(xb[0:TAIL, i % 2, :], x_prompt[0, SEQ - TAIL:SEQ, :])\
                          .then_inc(x_loaded[i % 2], 16)
                        sp.dma_start(xb[S0:S0 + NS, i % 2, :], x_sample.rearrange("b t d -> (b t) d"))\
                          .then_inc(x_loaded[i % 2], 16)

                def load_w(c):
                    if c >= 2:
                        sp.wait_ge(whi_done, KT * (c - 1))
                        sp.wait_ge(wlo_done, KT * (c - 1))
                    n = min(CB, DIN - W_AT[c])
                    sp.dma_start(wraw[:, c % 2, :, 0:n],
                                 w_in[0, :, W_AT[c]:W_AT[c] + n].rearrange("(t p) n -> p t n", p=P))\
                      .then_inc(w_loaded[c % 2], 16)

                load_x(0)
                load_x(1)
                load_w(0)
                load_w(1)
                for i in range(2, TILES):
                    load_x(i)
                stores = {"v": (val_d, 4), "gv": (val_g, 10), "dg": (gate_d, 6), "gg": (gate_g, 12)}
                nextw = 2
                for s, (c, i) in enumerate(natural):
                    if i == 0:
                        while nextw <= min(c + 2, len(W_AT) - 1):
                            load_w(nextw)
                            nextw += 1
                    k = kind(s)
                    at = nat_stored[s % 3]
                    sp.wait_ge(nat_done, s + 1)
                    r = rows_of(i)
                    if k == "q":
                        continue
                    if k in stores:
                        to, first = stores[k]
                        cols = slice((c - first) * CB, (c - first + 1) * CB)
                        sp.dma_start(to[i, 0:r, cols], nat[0:r, s % 3, :]).then_inc(at, 16)
                    if k in ("k", "v"):
                        first = 2 if k == "k" else 4
                        op, os_ = (k_prompt, k_sample) if k == "k" else (v_prompt, v_sample)
                        cols = slice((c - first) * CB, (c - first + 1) * CB)
                        dst = op.rearrange("a b l h d -> (a b l) (h d)")
                        n = P if i < TILES - 1 else TAIL
                        sp.dma_start(dst[P * i:P * i + n, cols], nat[0:n, s % 3, :]).then_inc(at, 16)
                        if i == TILES - 1:
                            dst = os_.rearrange("a b t h d -> (a b t) (h d)")
                            sp.dma_start(dst[:, cols], nat[S0:S0 + NS, s % 3, :]).then_inc(at, 16)
                while nextw < len(W_AT):
                    load_w(nextw)
                    nextw += 1
                for n in range(3):
                    sp.wait_ge(nat_stored[n], 16 * stored_upto(NN - 1, n))

            @block.gpsimd
            def _(pool):
                pass

            @block.scalar
            def _(act):
                link = [0]

                def linked(ins):
                    link[0] += 1
                    ins.then_inc(achain, 1)
                    act.wait_ge(achain, link[0])

                def x_sumsq(i):
                    r = rows_of(i)
                    act.wait_ge(x_loaded[i % 2], X_IN[i])
                    act.activation(squares[0:r, :], xb[0:r, i % 2, :], ACT.Square,
                                   accum_out=ss[0:r, 0, i:i + 1]).then_inc(sumsq_done, 1)
                    act.wait_ge(meansq_done, i + 1)
                    linked(act.activation(ss[0:r, 2, i:i + 1], ss[0:r, 1, i:i + 1], ACT.Ln))
                    act.activation(ss[0:r, 3, i:i + 1], ss[0:r, 2, i:i + 1], ACT.Exp, scale=-0.5)\
                       .then_inc(rstd_done, 1)

                def x_hi(i):
                    r = rows_of(i)
                    for half in range(2):
                        act.wait_ge(xt_done, 2 * i + half + 1)
                        for k in range(4):
                            kk = 4 * half + k
                            ins = act.activation(xTh[:, kk, P * i:P * i + r], pt[:, half, k * P:k * P + r],
                                                 ACT.Copy, scale=nw[:, kk:kk + 1])
                        ins.then_inc(xhi_done, 1)

                def w_hi(c):
                    n = min(CB, DIN - W_AT[c])
                    act.wait_ge(w_loaded[c % 2], 16 * (c // 2 + 1))
                    if c >= 2:
                        act.wait_ge(z_done, BLOCK_END[c - 2])
                    for k in range(KT):
                        act.activation(wh[:, c % 2, k, 0:n], wraw[:, c % 2, k, 0:n], ACT.Copy).then_inc(whi_done, 1)

                act.preload_act_table_set("natural_log_exp_and_others")
                act.wait_ge(consts_in, 16 * 12)
                x_sumsq(0)
                x_sumsq(1)
                x_hi(0)
                w_hi(0)
                act.wait_ge(lam_sum, 1)
                act.activation(lam[:, 2:4], lam[:, 0:2], ACT.Exp).then_inc(lam_exp, 1)

                def first(s):
                    k = kind(s)
                    if k not in ACTIVE:
                        return
                    r = rows_of(natural[s][1])
                    u = use_of[("n", *natural[s])]
                    act.wait_ge(z_done, u + 1)
                    n = count(ACTIVE, s)
                    if n > 2:
                        act.wait_ge(nat_done, last_active(s, 2) + 1)
                    if k in ("q", "k"):
                        act.activation(sq[0:r, n % 2, :], z_at(u)[0:r, 0:CB], ACT.Square).then_inc(sq_done, 1)
                    else:
                        act.activation(sq[0:r, n % 2, :], z_at(u)[0:r, 0:CB], ACT.Exp, scale=-1.0)\
                           .then_inc(sq_done, 1)

                def second(s):
                    if kind(s) not in ("q", "k"):
                        return
                    r = rows_of(natural[s][1])
                    act.wait_ge(ms_done, s + 1)
                    linked(act.activation(rms[0:r, s % 2, 1, :], rms[0:r, s % 2, 0, :], ACT.Ln))
                    act.activation(rms[0:r, s % 2, 2, :], rms[0:r, s % 2, 1, :], ACT.Exp, scale=-0.5)\
                       .then_inc(r_done, 1)

                def third(s):
                    if kind(s) not in ("q", "k"):
                        return
                    c, i = natural[s]
                    r = rows_of(i)
                    to = qT if kind(s) == "q" else kT
                    act.wait_ge(nt_done, s + 1)
                    act.activation(to[:, 2 * (c % 2):2 * (c % 2) + 2, P * i:P * i + r],
                                   pn[:, s % 2, 0:2 * P].rearrange("p (h t) -> p h t", h=2)[:, :, 0:r],
                                   ACT.Copy).then_inc(nt_out, 1)

                def last_active(s, back):
                    t = s
                    while back:
                        t -= 1
                        if kind(t) in ACTIVE:
                            back -= 1
                    return t

                def turn_out(c):
                    to, sc = (gqT, DK ** -0.5) if KINDS[c] == "gq" else (gkT, 1.0)
                    for m in range(2):
                        for n, (t0, tn) in enumerate(CH):
                            u = use_of[("t", c, m, n)]
                            act.wait_ge(z_done, u + 1)
                            act.activation(to[:, m, t0:t0 + tn], z_at(u)[:, 0:tn], ACT.Copy, scale=sc)\
                               .then_inc(turned_out, 1)

                for s in range(NN + 3):
                    if s < NN:
                        c, i = natural[s]
                        if i == 0 and c == 10:
                            w_hi(9)
                            turn_out(8)
                            w_hi(10)
                            turn_out(9)
                        if c == 0:
                            if i + 2 < TILES:
                                x_sumsq(i + 2)
                            if i + 1 < TILES:
                                x_hi(i + 1)
                        first(s)
                        if i == 3:
                            w_hi(c + 1)
                    if 1 <= s <= NN:
                        second(s - 1)
                    if s >= 3:
                        third(s - 3)
                for n, (t0, tn) in enumerate(CH):
                    u = use_of[("a", n)]
                    act.wait_ge(z_done, u + 1)
                    act.wait_ge(ga_done, 1)
                    act.activation(gaT[0:16, t0:t0 + tn], z_at(u)[0:16, 0:tn], ACT.Copy).then_inc(turned_out, 1)
                for i in range(TILES):
                    r = rows_of(i)
                    u = use_of[("l", i)]
                    act.wait_ge(z_done, u + 1)
                    linked(act.activation(lgm[0:r, i % 2, :], z_at(u)[0:r, 0:CB], ACT.Abs))
                    linked(act.activation(lg[0:r, i % 2, :], lgm[0:r, i % 2, :], ACT.Exp, scale=-1.0))
                    act.activation(lgm[0:r, i % 2, :], lg[0:r, i % 2, :], ACT.Ln, bias=1.0).then_inc(lnexp_done, 1)
                    act.wait_ge(cum_done, i + 1)
                    act.activation(bT[:, :, P * i:P * i + r],
                                   pt[:, i % 2, 0:2 * r].rearrange("p (m t) -> p m t", m=2), ACT.Copy)\
                       .then_inc(cum_out, 1)

            @block.tensor
            def _(pe):
                def x_turn(i):
                    r = rows_of(i)
                    pe.wait_ge(hn_done, i + 1)
                    for half in range(2):
                        if i >= 1:
                            pe.wait_ge(xhi_done, 2 * (i - 1) + half + 1)
                            pe.wait_ge(xlo_done, 2 * (i - 1) + half + 1)
                        for k in range(4):
                            kk = 4 * half + k
                            ins = pe.transpose(pt[:, half, k * P:k * P + r], xb[0:r, i % 2, kk * P:(kk + 1) * P],
                                               ident[0:r, 0:r])
                        ins.then_inc(xt_done, 1)

                def z_nat(c, i, lastcols=CB):
                    u = use_of[("n", c, i)]
                    r = rows_of(i)
                    wait_z(pe, u)
                    n = 0
                    for k in range(KT):
                        if i == 0:
                            pe.wait_ge(whi_done, KT * c + k + 1)
                            pe.wait_ge(wlo_done, KT * c + k + 1)
                        for a, b in ((xTh, wh), (xTl, wh), (xTh, wl)):
                            ins = pe.matmul(z_at(u)[0:r, 0:CB], a[:, k, P * i:P * i + r], b[:, c % 2, k, :],
                                            start=(n == 0), stop=(n == 3 * KT - 1))
                            n += 1
                    ins.then_inc(z_done, 1)

                def z_turned(u, c, m0, mn, t0, tn):
                    wait_z(pe, u)
                    n = 0
                    for k in range(KT):
                        pe.wait_ge(whi_done, KT * c + k + 1)
                        pe.wait_ge(wlo_done, KT * c + k + 1)
                        for a, b in ((xTh, wh), (xTl, wh), (xTh, wl)):
                            ins = pe.matmul(z_at(u)[0:mn, 0:tn], b[:, c % 2, k, m0:m0 + mn], a[:, k, t0:t0 + tn],
                                            start=(n == 0), stop=(n == 3 * KT - 1))
                            n += 1
                    ins.then_inc(z_done, 1)

                def nat_turn(s):
                    if kind(s) not in ("q", "k"):
                        return
                    r = rows_of(natural[s][1])
                    pe.wait_ge(nat_done, s + 1)
                    if s >= 2:
                        pe.wait_ge(nt_out, s - 1)
                    for h in range(2):
                        ins = pe.transpose(pn[:, s % 2, h * P:h * P + r], nat[0:r, s % 3, h * P:(h + 1) * P],
                                           ident[0:r, 0:r])
                    ins.then_inc(nt_done, 1)

                pe.wait_ge(consts_in, 16 * 12)
                x_turn(0)
                s = 0
                for c, k in enumerate(KINDS):
                    if k in ("gq", "gk"):
                        for m in range(2):
                            for n, (t0, tn) in enumerate(CH):
                                z_turned(use_of[("t", c, m, n)], c, m * P, P, t0, tn)
                        continue
                    for i in range(TILES):
                        if c == 0:
                            if i + 1 < TILES:
                                x_turn(i + 1)
                            pe.wait_ge(xhi_done, 2 * i + 2)
                            pe.wait_ge(xlo_done, 2 * i + 2)
                        z_nat(c, i)
                        if s >= 2:
                            nat_turn(s - 2)
                        s += 1
                for n, (t0, tn) in enumerate(CH):
                    z_turned(use_of[("a", n)], 14, 0, 16, t0, tn)
                for i in range(TILES + 1):
                    if i < TILES:
                        r = rows_of(i)
                        u = use_of[("l", i)]
                        wait_z(pe, u)
                        pe.wait_ge(turned_out, len(turned_uses))
                        pe.matmul(z_at(u)[0:r, 0:CB], gaT[:, P * i:P * i + r], wa2[:], start=True, stop=True)\
                          .then_inc(z_done, 1)
                    if i >= 1:
                        j = i - 1
                        r = rows_of(j)
                        pe.wait_ge(lg_done, j + 1)
                        if j >= 2:
                            pe.wait_ge(cum_out, j - 1)
                        for m in range(2):
                            ins = pe.matmul(pt[:, j % 2, m * r:(m + 1) * r], lg[0:r, j % 2, m * P:(m + 1) * P],
                                            cum[:, :] if r == P else cum8[:, :], start=True, stop=True)
                        ins.then_inc(cum_done, 1)

            @block.vector
            def _(dve):
                link = [0]

                def linked(ins):
                    link[0] += 1
                    ins.then_inc(dchain, 1)
                    dve.wait_ge(dchain, link[0])

                dve.memset(gaT[:], 1.0).then_inc(ga_done, 1)
                dve.wait_ge(consts_in, 16 * 12)
                linked(dve.tensor_tensor(lmv[:, 2, :], lmv[:, 0, :], lmv[:, 1, :], ALU.mult))
                dve.tensor_reduce(lam[:, 0:2], lmv[:, 2, :].rearrange("p (m d) -> p m d", m=2), AX.X, ALU.add)\
                   .then_inc(lam_sum, 1)
                linked(dve.tensor_scalar(qwr[:, 0, :], qwr[:, 0, :], DK ** -0.5, None, ALU.mult))

                def x_norm(i):
                    r = rows_of(i)
                    dve.wait_ge(sumsq_done, i + 1)
                    dve.tensor_scalar(ss[0:r, 1, i:i + 1], ss[0:r, 0, i:i + 1], 1.0 / D, EPS, ALU.mult, ALU.add)\
                       .then_inc(meansq_done, 1)
                    dve.wait_ge(rstd_done, i + 1)
                    dve.tensor_scalar(xb[0:r, i % 2, :], xb[0:r, i % 2, :], ss[0:r, 3, i:i + 1], None, ALU.mult)\
                       .then_inc(hn_done, 1)

                def x_lo(i):
                    r = rows_of(i)
                    for half in range(2):
                        dve.wait_ge(xhi_done, 2 * i + half + 1)
                        for k in range(4):
                            kk = 4 * half + k
                            ins = dve.scalar_tensor_tensor(
                                out=xTl[:, kk, P * i:P * i + r], in0=pt[:, half, k * P:k * P + r],
                                scalar=nw[:, kk:kk + 1], in1=xTh[:, kk, P * i:P * i + r].bitcast(F32),
                                op0=ALU.mult, op1=ALU.subtract)
                        ins.then_inc(xlo_done, 1)

                def w_lo(c):
                    n = min(CB, DIN - W_AT[c])
                    for k in range(KT):
                        dve.wait_ge(whi_done, KT * c + k + 1)
                        dve.tensor_tensor(wl[:, c % 2, k, 0:n], wraw[:, c % 2, k, 0:n],
                                          wh[:, c % 2, k, 0:n].bitcast(F32), ALU.subtract).then_inc(wlo_done, 1)

                x_norm(0)
                x_norm(1)
                x_lo(0)
                w_lo(0)
                dve.wait_ge(lam_exp, 1)
                linked(dve.tensor_tensor(lam[:, 4:5], lam[:, 3:4], lam[:, 2:3], ALU.subtract))
                dve.tensor_scalar(nlam, lam[:, 4:5], -LAM_INIT, None, ALU.add)

                def reduce_sq(s):
                    k = kind(s)
                    if k not in ACTIVE:
                        return
                    r = rows_of(natural[s][1])
                    n = count(ACTIVE, s)
                    dve.wait_ge(sq_done, n)
                    if k in ("q", "k"):
                        linked(dve.tensor_reduce(rms[0:r, s % 2, 0, :],
                                                 sq[0:r, n % 2, :].rearrange("p (g d) -> p g d", g=4),
                                                 AX.X, ALU.add))
                        dve.tensor_scalar(rms[0:r, s % 2, 0, :], rms[0:r, s % 2, 0, :], 1.0 / DK, EPS,
                                          ALU.mult, ALU.add).then_inc(ms_done, 1)
                    else:
                        linked(dve.tensor_scalar(sq[0:r, n % 2, :], sq[0:r, n % 2, :], 1.0, None, ALU.add))
                        linked(dve.reciprocal(sq[0:r, n % 2, :], sq[0:r, n % 2, :]))

                def finish(s):
                    c, i = natural[s]
                    r = rows_of(i)
                    k = kind(s)
                    n = count(ACTIVE, s)
                    u = use_of[("n", c, i)]
                    z = z_at(u)[0:r, 0:CB]
                    to = nat[0:r, s % 3, :]
                    if s >= 3:
                        if stored_upto(s - 3, s % 3):
                            dve.wait_ge(nat_stored[s % 3], 16 * stored_upto(s - 3, s % 3))
                        if kind(s - 3) in ("q", "k"):
                            dve.wait_ge(nt_done, s - 2)
                    if k in ("q", "k"):
                        dve.wait_ge(r_done, s + 1)
                        g4 = lambda a: a.rearrange("p (g d) -> p g d", g=4)
                        linked(dve.tensor_tensor(g4(nrm[0:r, :]), g4(z),
                                                 rms[0:r, s % 2, 2, :].unsqueeze(2).to_broadcast([r, 4, DK]),
                                                 ALU.mult))
                        dve.tensor_tensor(to, nrm[0:r, :], qwr[0:r, 0 if k == "q" else 1, :], ALU.mult)\
                           .then_inc(nat_done, 1)
                        dve.wait_ge(nat_done, s + 1)
                    elif k in ("dg", "gg"):
                        dve.tensor_tensor(to, z, sq[0:r, n % 2, :], ALU.mult).then_inc(nat_done, 1)
                        dve.wait_ge(nat_done, s + 1)
                    else:
                        dve.wait_ge(z_done, u + 1)
                        dve.tensor_copy(to, z).then_inc(nat_done, 1)
                        dve.wait_ge(nat_done, s + 1)

                for s in range(NN + 1):
                    if s < NN:
                        c, i = natural[s]
                        if i == 0 and c == 10:
                            finish(s - 1)
                            w_lo(9)
                            w_lo(10)
                            reduce_sq(s)
                            continue
                        if c == 0:
                            if i + 2 == TILES - 1:
                                dve.wait_ge(xt_done, 2 * i + 2)
                                dve.memset(xb[0:S0, i % 2, :], 0.0).then_inc(x_zero, 1)
                            if i + 2 < TILES:
                                x_norm(i + 2)
                            if i + 1 < TILES:
                                x_lo(i + 1)
                        reduce_sq(s)
                        if i == 3:
                            finish(s - 1)
                            w_lo(c + 1)
                            continue
                    if s >= 1:
                        finish(s - 1)
                for i in range(TILES):
                    r = rows_of(i)
                    u = use_of[("l", i)]
                    dve.wait_ge(lnexp_done, i + 1)
                    dve.scalar_tensor_tensor(out=lg[0:r, i % 2, :], in0=z_at(u)[0:r, 0:CB], scalar=0.0,
                                             in1=lgm[0:r, i % 2, :], op0=ALU.min, op1=ALU.subtract)\
                       .then_inc(lg_done, 1)
                    dve.wait_ge(lg_done, i + 1)

        with ExitStack() as st:
            KR, VR = 4, 4
            R = 2 * H * TS
            kraw = sb(st, "kraw", [P, KR, GRP, W])
            vraw = sb(st, "vraw", [P, VR, GRP, W])
            kt = sb(st, "kt", [P, 2, H, GRP * PAGE])
            sc = sb(st, "sc", [P, G + 1, PAGE])
            pr = sb(st, "pr", [P, 2, PAGE])
            pT = sb(st, "pT", [P, 2, P])
            pages = sb(st, "pages", [1, NB * NPAGES], I32)
            qq = sb(st, "qq", [P, 160])
            kn = sb(st, "kn", [P, H, NS])
            vn = sb(st, "vn", [P, W])
            relb = sb(st, "relb", [32, H])
            rowq = sb(st, "rowq", [32, TS, 32])
            relq = sb(st, "relq", [32, TS, 32])
            staged = kt[0:32].rearrange("k a h x -> k (a h x)")
            oh, negp = staged[:, 0:384], staged[0:H, 512:896]
            hotp = staged[:, 1024:1024 + TS * PAGE].rearrange("k (q j) -> k q j", q=TS)
            hotn = staged[:, 2048:2048 + TS * NB * NS].rearrange("k (q j) -> k q j", q=TS)
            dlast = sb(st, "dlast", [P, PAGE])
            dnew = sb(st, "dnew", [32, NB * NS])
            band = sb(st, "band", [H, 384])
            selT = sb(st, "selT", [P, NB, H, NS])
            selc = sb(st, "selc", [P, H, P])
            m01 = sb(st, "m01", [R, 2])
            mx = sb(st, "mx", [P, G + 1])
            lsum = sb(st, "lsum", [P, G + 1])
            stat = sb(st, "stat", [P, 8])
            by_page = sb(st, "by_page", [R, GRP])
            osb = sb(st, "osb", [P, W])
            pk = [ps(st, f"pk{n}", [P, 512]) for n in range(H)]
            psc = [ps(st, f"psc{n}", [P, 512]) for n in range(2)]
            ppt = ps(st, "ppt", [P, 512])
            po = ps(st, "po", [P, 512])
            pod = ppt
            negmax, coef, partial = stat[:, 0:1], stat[:, 1:2], stat[:, 2:3]
            row_stat, sign_lam = stat[0:R, 3:4], stat[0:R, 4:5]
            c_in = sem("c_in")
            pages_in = sem("pages_in")
            k_in = [sem(f"k_in{n}") for n in range(KR)]
            v_in = [sem(f"v_in{n}") for n in range(VR)]
            setup = sem("setup_c")
            rel_done = sem("rel_done")
            band_out = sem("band_out")
            kt_done = sem("kt_done")
            kt_act = sem("kt_act")
            kt_dve = sem("kt_dve")
            sc_done = sem("sc_done")
            sc_out = sem("sc_out")
            max_done = sem("max_done")
            negmax_done = sem("negmax_done")
            exp_done = sem("exp_done")
            pt_done = sem("pt_done")
            pt_out = sem("pt_out")
            pv_done = sem("pv_done")
            o_out = sem("o_out")
            qq_done = sem("qq_done")
            sel_done = sem("sel_done")
            od_done = sem("od_done")
            od_added = sem("od_added")
            bias_done = sem("bias_done")
            dch = sem("dchain_c")
            NCONST = 10

            block = st.enter_context(nc.Block())

            @block.sync
            def _(sp):
                sp.dma_start(pages[:], page_table.rearrange("(o b) n -> o (b n)", o=1)).then_inc(pages_in, 16)
                sp.dma_start(vn[0:NS, :], v_sample.rearrange("a b t h d -> (a b t) (h d)")).then_inc(c_in, 16)
                for to, of in ((relb[:], rel_bias), (rowq[:], c_rowq), (hotp, c_hotp.rearrange("k (q j) -> k q j", q=TS)),
                               (hotn, c_hotn), (dnew[:], c_negn), (oh, c_oh), (negp, c_negp), (selT[:], c_selT),
                               (m01[:], c_m01)):
                    sp.dma_start(to, of).then_inc(c_in, 16)
                sp.wait_ge(pages_in, 16)

                def load_keys(kb, peeled):
                    for g in range(G):
                        if not (peeled and g < KR):
                            sp.wait_ge(kt_done, kb * (4 * G) + 4 * (g - KR + 1))
                        for n in range(GRP):
                            page = sp.value_load(pages[0:1, bass.ds(kb * NPAGES + GRP * g + n, 1)],
                                                 min_val=0, max_val=POOL - 1)
                            sp.dma_start(kraw[:, g % KR, n, :],
                                         cache_k.rearrange("a n p h d -> (a n) p (h d)")[bass.ds(page, 1)]
                                         .rearrange("o p c -> (o p) c")).then_inc(k_in[g % KR], 16)

                load_keys(0, True)
                with sp.Fori(1, NB) as kb:
                    load_keys(kb, False)
                sp.wait_ge(band_out, 1)
                for h in range(H):
                    sp.dma_start(skew[h:h + 1].rearrange("o (q x) -> o q x", q=P),
                                 band[h:h + 1, :].unsqueeze(1).to_broadcast([1, P, 384])).then_inc(c_in, 16)
                sp.wait_ge(c_in, 16 * (NCONST + H))

            @block.gpsimd
            def _(pool):
                pool.wait_ge(pages_in, 16)

                def load_values(b, peeled):
                    for g in range(G):
                        if not (peeled and g < VR):
                            pool.wait_ge(pv_done, b * (G + 1) + (g - VR + 1 if g >= VR else g - VR))
                        for n in range(GRP):
                            page = pool.value_load(pages[0:1, bass.ds(b * NPAGES + GRP * g + n, 1)],
                                                   min_val=0, max_val=POOL - 1)
                            pool.dma_start(vraw[:, g % VR, n, :],
                                           cache_v.rearrange("a n p h d -> (a n) p (h d)")[bass.ds(page, 1)]
                                           .rearrange("o p c -> (o p) c")).then_inc(v_in[g % VR], 16)

                load_values(0, True)
                with pool.Fori(1, NB) as b:
                    load_values(b, False)

            def first(b):
                return isinstance(b, int) and b == 0

            def copy_keys(eng, copied, kb, g, h):
                eng.wait_ge(kt_done, kb * (4 * G) + 4 * g + h + 1)
                if not (first(kb) and g < 2):
                    eng.wait_ge(sc_done, kb * (G + 1) + (g - 1 if g >= 2 else g - 2))
                if eng is nc.scalar:
                    ins = eng.activation(kt[:, g % 2, h, :], pk[h][:], ACT.Copy)
                else:
                    ins = eng.tensor_copy(kt[:, g % 2, h, :], pk[h][:])
                ins.then_inc(copied, 1)

            @block.scalar
            def _(act):
                def scores_out(kb, g):
                    act.wait_ge(sc_done, kb * (G + 1) + g + 1)
                    if g < G:
                        act.activation(sc[:, g, :], psc[g % 2][:, 0:PAGE], ACT.Copy).then_inc(sc_out, 1)
                    else:
                        act.activation(sc[0:R, g, 0:NS], psc[g % 2][0:R, 0:NS], ACT.Copy).then_inc(sc_out, 1)

                def expo(b, g):
                    if g == 0:
                        act.wait_ge(negmax_done, b + 1)
                    if not (first(b) and g < 2):
                        act.wait_ge(pt_done, b * (G + 1) + max(g - 1, 0))
                    rows, n = (R, NS) if g == G else (P, PAGE)
                    act.activation(pr[0:rows, g % 2, 0:n], sc[0:rows, g, 0:n], ACT.Exp, bias=negmax[0:rows],
                                   accum_out=lsum[0:rows, g:g + 1]).then_inc(exp_done, 1)

                def row(kb, b):
                    for g in range(G):
                        if b is not None:
                            expo(b, g)
                        if kb is not None:
                            if g >= 1:
                                scores_out(kb, g - 1)
                            copy_keys(act, kt_act, kb, g, 0)
                            copy_keys(act, kt_act, kb, g, 1)
                    if b is not None:
                        expo(b, G)
                    if kb is not None:
                        scores_out(kb, G - 1)
                        scores_out(kb, G)
                    if b is not None:
                        act.wait_ge(pv_done, b * (G + 1) + G + 1)
                        if not first(b):
                            act.wait_ge(od_done, b + 0)
                        act.activation(osb[:], po[:, :], ACT.Copy).then_inc(o_out, 1)

                row(0, None)
                row(1, 0)
                with act.Fori(1, NB - 1) as b:
                    row(b + 1, b)
                row(None, NB - 1)

            @block.tensor
            def _(pe):
                def turn_keys(kb, g, h):
                    if h == 0:
                        pe.wait_ge(k_in[g % KR], kb * 128 + 64 * (g // KR + 1))
                    if not (first(kb) and g == 0):
                        pe.wait_ge(kt_act if h < 2 else kt_dve, kb * (2 * G) + 2 * (g - 1) + h % 2 + 1)
                    for n in range(GRP):
                        ins = pe.transpose(pk[h][:, n * PAGE:(n + 1) * PAGE],
                                           kraw[:, g % KR, n, h * P:(h + 1) * P], ident[:])
                    ins.then_inc(kt_done, 1)

                def scores(kb, g):
                    if g == 0:
                        pe.wait_ge(qq_done, 2 * (kb + 1))
                    if g >= 2:
                        pe.wait_ge(sc_out, kb * (G + 1) + g - 1)
                    elif not first(kb):
                        pe.wait_ge(sc_out, kb * (G + 1))
                    for h in range(H):
                        pe.wait_ge(kt_act if h < 2 else kt_dve, kb * (2 * G) + 2 * g + h % 2 + 1)
                        for n in range(GRP):
                            ins = pe.matmul(psc[g % 2][R * n:R * (n + 1), 0:PAGE], qq[:, 32 * h:32 * h + R],
                                            kt[:, g % 2, h, n * PAGE:(n + 1) * PAGE], start=(h == 0),
                                            stop=(h == H - 1), tile_position=(0, R * n))
                    ins.then_inc(sc_done, 1)

                def new_scores(kb):
                    pe.wait_ge(sc_out, kb * (G + 1) + G - 1)
                    for h in range(H):
                        ins = pe.matmul(psc[G % 2][0:R, 0:NS], qq[:, 32 * h:32 * h + R], kn[:, h, :],
                                        start=(h == 0), stop=(h == H - 1))
                    ins.then_inc(sc_done, 1)

                def turn_probs(b, g):
                    pe.wait_ge(exp_done, b * (G + 1) + g + 1)
                    if not (first(b) and g == 0):
                        pe.wait_ge(pt_out, b * (G + 1) + g)
                        if g == 0:
                            pe.wait_ge(od_added, b + 0)
                    pe.transpose(ppt[:, 0:P], pr[:, g % 2, :], ident[:]).then_inc(pt_done, 1)

                def values(b, g):
                    pe.wait_ge(pt_out, b * (G + 1) + g + 1)
                    if g < G:
                        pe.wait_ge(v_in[g % VR], b * 128 + 64 * (g // VR + 1))
                    if g == 0 and not first(b):
                        pe.wait_ge(o_out, b + 0)
                    if g < G:
                        for n in range(GRP):
                            ins = pe.matmul(po[R * n:R * (n + 1), :], pT[:, g % 2, R * n:R * (n + 1)],
                                            vraw[:, g % VR, n, :], start=(g == 0), stop=(n > 0 and g == G - 1),
                                            tile_position=(0, R * n))
                    else:
                        ins = pe.matmul(po[0:R, :], pT[:, g % 2, 0:R], vn[:], start=False, stop=True)
                    ins.then_inc(pv_done, 1)

                def row(kb, b):
                    for g in range(G):
                        if kb is not None:
                            for h in range(H):
                                turn_keys(kb, g, h)
                        if b is not None:
                            if g >= 1:
                                values(b, g - 1)
                            turn_probs(b, g)
                        if kb is not None:
                            scores(kb, g)
                    if b is not None:
                        values(b, G - 1)
                        turn_probs(b, G)
                    if kb is not None:
                        new_scores(kb)
                    if b is not None:
                        values(b, G)
                        pe.wait_ge(o_out, b + 1)
                        pe.wait_ge(sel_done, b + 1)
                        for h in range(H):
                            ins = pe.matmul(pod[:, h * DV:(h + 1) * DV], selc[:, h, :], osb[:, h * DV:(h + 1) * DV],
                                            start=True, stop=True)
                        ins.then_inc(od_done, 1)

                pe.wait_ge(setup, 1)
                for q in range(TS):
                    pe.matmul(pk[0][0:32, 0:PAGE], relq[:, q, :], hotp[:, q, :], start=(q == 0), stop=(q == TS - 1))
                for q in range(TS):
                    pe.matmul(pk[1][0:32, 0:NB * NS], relq[:, q, :], hotn[:, q, :], start=(q == 0),
                              stop=(q == TS - 1))
                pe.matmul(pk[2][0:H, 0:384], relb[:], oh, start=True, stop=True).then_inc(rel_done, 1)
                pe.wait_ge(band_out, 1)
                row(0, None)
                row(1, 0)
                with pe.Fori(1, NB - 1) as b:
                    row(b + 1, b)
                row(None, NB - 1)

            @block.vector
            def _(dve):
                link = [0]

                def linked(ins):
                    link[0] += 1
                    ins.then_inc(dch, 1)
                    dve.wait_ge(dch, link[0])

                dve.wait_ge(c_in, 16 * NCONST)
                linked(dve.tensor_tensor(
                    relq[:].rearrange("k q (h x) -> k q h x", h=H),
                    rowq[:].rearrange("k q (h x) -> k q h x", h=H),
                    relb[:].unsqueeze(1).unsqueeze(3).to_broadcast([32, TS, H, 8]), ALU.mult))
                dve.memset(od_s[:], 0.0)
                dve.memset(selc[:], 0.0)
                dve.memset(vn[NS:2 * NS, :], 0.0)
                dve.memset(vn[2 * NS:P, :], 0.0)
                dve.memset(lsum[:], 0.0)
                dve.memset(mx[:], NEG)
                dve.memset(qq[:], 0.0).then_inc(setup, 1)
                dve.wait_ge(setup, 1)
                new = slice(P * (TILES - 1) + S0, P * (TILES - 1) + S0 + NS)
                dve.tensor_copy(kn[:], kT[:, :, new])
                dve.scalar_tensor_tensor(out=sign_lam, in0=m01[:, 1:2], scalar=nlam[0:R], in1=m01[:, 0:1],
                                         op0=ALU.mult, op1=ALU.add)
                dve.wait_ge(rel_done, 1)
                dve.tensor_copy(dlast[P - R:P, :], pk[0][0:R, 0:PAGE])
                dve.tensor_tensor(dnew[:], dnew[:], pk[1][0:32, 0:NB * NS], ALU.add)
                dve.tensor_tensor(band[:], negp, pk[2][0:H, 0:384], ALU.add).then_inc(band_out, 1)
                dve.wait_ge(band_out, 1)
                SETUP = link[0]
                LINKS = 9
                at = [0]

                def rowlinked(ins, b):
                    at[0] += 1
                    ins.then_inc(dch, 1)
                    dve.wait_ge(dch, b * LINKS + SETUP + at[0])

                def queries(kb):
                    if not first(kb):
                        dve.wait_ge(sc_done, kb * (G + 1))
                    for m in range(2):
                        half = slice(DK * m, DK * m + DK)
                        of = qT[half, :, bass.ds(kb * TS + P * (TILES - 1) + S0, TS)]
                        dve.tensor_copy(qq[half, :].rearrange("p (h x) -> p h x", h=H)[:, :, TS * m:TS * m + TS], of)\
                           .then_inc(qq_done, 1)

                def group_max(kb, g):
                    dve.wait_ge(sc_out, kb * (G + 1) + g + 1)
                    rows, n = (R, NS) if g == G else (P, PAGE)
                    if g == G - 1:
                        last = sc[P - R:P, g, :]
                        dve.tensor_tensor(last, last, dlast[P - R:P, :], ALU.add).then_inc(bias_done, 1)
                        dve.wait_ge(bias_done, 2 * kb + 1)
                    if g == G:
                        new = sc[0:R, g, 0:NS]
                        dve.tensor_tensor(new, new, dnew[:, bass.ds(kb * NS, NS)], ALU.add).then_inc(bias_done, 1)
                        dve.wait_ge(bias_done, 2 * kb + 2)
                    dve.tensor_reduce(mx[0:rows, g:g + 1], sc[0:rows, g, 0:n], AX.X, ALU.max).then_inc(max_done, 1)

                def over_pages(of, op, b, negate=False):
                    rowlinked(dve.tensor_reduce(partial, of, AX.X, op), b)
                    for n in range(GRP):
                        ins = dve.tensor_copy(by_page[:, n:n + 1], partial[R * n:R * (n + 1)])
                    rowlinked(ins, b)
                    rowlinked(dve.tensor_reduce(row_stat, by_page[:], AX.X, op, negate=negate), b)

                def row_max(b):
                    at[0] = 0
                    dve.wait_ge(max_done, b * (G + 1) + G + 1)
                    over_pages(mx[:], ALU.max, b, negate=True)
                    for n in range(GRP):
                        ins = dve.tensor_copy(negmax[R * n:R * (n + 1)], row_stat)
                    ins.then_inc(negmax_done, 1)
                    dve.wait_ge(negmax_done, b + 1)

                def coefficients(b):
                    dve.wait_ge(exp_done, b * (G + 1) + G + 1)
                    over_pages(lsum[:], ALU.add, b)
                    rowlinked(dve.reciprocal(row_stat, row_stat), b)
                    rowlinked(dve.tensor_tensor(row_stat, row_stat, sign_lam, ALU.mult), b)
                    for n in range(GRP):
                        ins = dve.tensor_copy(coef[R * n:R * (n + 1)], row_stat)
                    rowlinked(ins, b)
                    if not first(b):
                        dve.wait_ge(od_done, b + 0)
                    dve.tensor_scalar(selc[:, :, 0:NS], selT[:, bass.ds(b, 1), :, :].rearrange("p o h t -> p (o h) t"),
                                      coef, None, ALU.mult).then_inc(sel_done, 1)
                    assert at[0] == LINKS

                def turned_probs(b, g):
                    dve.wait_ge(pt_done, b * (G + 1) + g + 1)
                    if not (first(b) and g < 2):
                        dve.wait_ge(pv_done, b * (G + 1) + max(g - 1, 0))
                    dve.tensor_copy(pT[:, g % 2, :], ppt[:, 0:P]).then_inc(pt_out, 1)

                def row(kb, b):
                    if b is not None:
                        row_max(b)
                    if kb is not None:
                        queries(kb)
                    for g in range(G):
                        if kb is not None:
                            copy_keys(dve, kt_dve, kb, g, 2)
                            copy_keys(dve, kt_dve, kb, g, 3)
                        if b is not None:
                            turned_probs(b, g)
                        if kb is not None and g >= 1:
                            group_max(kb, g - 1)
                    if kb is not None:
                        group_max(kb, G - 1)
                    if b is not None:
                        turned_probs(b, G)
                        coefficients(b)
                    if kb is not None:
                        group_max(kb, G)
                    if b is not None:
                        dve.wait_ge(od_done, b + 1)
                        dve.tensor_tensor(od_s[:], od_s[:], pod[0:NS, :], ALU.add).then_inc(od_added, 1)
                        dve.wait_ge(od_added, b + 1)

                row(0, None)
                row(1, 0)
                with dve.Fori(1, NB - 1) as b:
                    row(b + 1, b)
                row(None, NB - 1)

        mixT = sb(ctx, "mixT", [P, 2 * H, NTOK])

        with ExitStack() as st:
            vd = sb(st, "vd", [P, TILES, W])
            gd = sb(st, "gd", [P, 2, W])
            dw = sb(st, "dw", [P, DV])
            ks = sb(st, "ks", [P, 2, H, L], F32R)
            qs = sb(st, "qs", [P, 2, 2, 2, H, P], F32R)
            bh = sb(st, "bh", [P, H, 2 * P], F32R)
            bl = sb(st, "bl", [P, H, 2 * P], F32R)
            identr = sb(st, "identr", [P, P], F32R)
            e = sb(st, "e", [P, 2, 2, L])
            pT = sb(st, "pT_b", [P, TILES, P])
            ob = sb(st, "ob", [P, W])
            mix = sb(st, "mix_b", [P, W])
            squares_b = sb(st, "squares_b", [P, DV])
            r4 = sb(st, "r4", [P, 3, 4])
            inv = sb(st, "inv", [P, 2, H])
            eps = sb(st, "eps_b", [P, 1])
            sm = sb(st, "sm", [P, 2, 8])
            pS = ps(st, "pS", [P, 6 * 512])
            pT6 = ps(st, "pT6", [P, 512])
            pO = ps(st, "pO", [P, 512])
            turn_banks = [pS[:, 2 * 512:3 * 512], pS[:, 5 * 512:6 * 512], pT6[:, :]]
            b_in = sem("b_in")
            band_in = sem("band_in")
            gd_in = [sem(f"gd_in{n}") for n in range(2)]
            bandhi_done = sem("bandhi_done")
            bandlo_done = sem("bandlo_done")
            dw_scaled = sem("dw_scaled")
            khi_done = sem("b_khi_done")
            klo_done = sem("b_klo_done")
            qhi_done = sem("b_qhi_done")
            qlo_done = sem("b_qlo_done")
            scores_done = sem("b_scores_done")
            max_done = sem("b_max_done")
            exp_done = sem("b_exp_done")
            probs_done = sem("b_probs_done")
            turned_done = sem("b_turned_done")
            turned_copied = sem("b_turned_copied")
            out_done = sem("b_out_done")
            out_copied = sem("b_out_copied")
            root_done = sem("root_done")
            gate_done = sem("gate_done")
            mix_done = sem("mix_done")
            tail_ready = sem("tail_ready")
            pool_chain = sem("pool_chain_b")
            dch2 = sem("dchain_b")
            ach2 = sem("achain_b")
            units = [(i, h) for i in range(TILES) for h in range(H)]
            NU = len(units)
            LAST0 = H * (TILES - 1)
            PAIRS = (TILES + 1) // 2

            def rq(i):
                return P if i < TILES - 1 else TAIL

            def keys(i):
                return P * i + rq(i)

            turns, bank_of = [], []
            for u in range(NU + 1):
                if u >= 1:
                    i, h = units[u - 1]
                    new = [("p", u - 1, j0, min(j0 + 4, i + 1)) for j0 in range(0, i + 1, 4)]
                    if h == 1 and i >= 1:
                        new.append(("m", i - 1))
                    for x in new:
                        turns.append(x)
                        bank_of.append(len(turns) % 3 if u < LAST0 else 2)
            turns.append(("m", TILES - 1))
            bank_of.append(2)
            turn_no = {x: n for n, x in enumerate(turns)}

            def batches(u):
                return [x for x in turns if x[0] == "p" and x[1] == u]

            def last_batch(u):
                return turn_no[batches(u)[-1]]

            def wait_bank(eng, n):
                before = [m for m in range(n) if bank_of[m] == bank_of[n]]
                if before:
                    eng.wait_ge(turned_copied, before[-1] + 1)

            block = st.enter_context(nc.Block())

            @block.sync
            def _(sp):
                sp.dma_start(dw[:], diff_norm_w.to_broadcast([P, DV])).then_inc(band_in, 16)
                for h in range(H):
                    sp.dma_start(pT[:, 2 * h:2 * h + 2, :].rearrange("p a x -> p (a x)"),
                                 skew[h, P - 1:P - 1 + P * 383].rearrange("(q x) -> q x", x=383)
                                 [:, 0:2 * P]).then_inc(band_in, 16)
                for i in range(TILES):
                    sp.dma_start(vd[0:rows_of(i), i, :], val_d[i, 0:rows_of(i), :]).then_inc(b_in, 16)
                for i in range(TILES):
                    if i >= 2:
                        sp.wait_ge(mix_done, i - 1)
                    sp.dma_start(gd[0:rows_of(i), i % 2, :], gate_d[i, 0:rows_of(i), :]).then_inc(gd_in[i % 2], 16)

            own = [slice(0, DK), slice(DK, P)]

            def key_lo(eng, p, m):
                k = slice(2 * P * p, min(2 * P * (p + 1), L))
                return eng.tensor_tensor(ks[own[1 - m], m, :, k], kT[own[m], :, k],
                                         ks[own[m], m, :, k].bitcast(F32), ALU.subtract)

            def query_lo(eng, i, m, to):
                nq = rq(i)
                return eng.tensor_tensor(qs[to, i % 2, m, 1, :, 0:nq], qT[own[m], :, P * i:P * i + nq],
                                         qs[own[m], i % 2, m, 0, :, 0:nq].bitcast(F32), ALU.subtract)

            @block.gpsimd
            def _(pool):
                link = [0]

                def linked(ins):
                    link[0] += 1
                    ins.then_inc(pool_chain, 1)
                    pool.wait_ge(pool_chain, link[0])

                def split_lo(i):
                    if i % 2 == 0 and i > 0:
                        pool.wait_ge(khi_done, i // 2 + 1)
                        linked(key_lo(pool, i // 2, 0))
                        key_lo(pool, i // 2, 1).then_inc(klo_done, 1)
                        pool.wait_ge(klo_done, i // 2 + 1)
                    pool.wait_ge(qhi_done, i + 1)
                    linked(query_lo(pool, i, 0, own[0]))
                    linked(query_lo(pool, i, 0, own[1]))
                    linked(query_lo(pool, i, 1, own[0]))
                    query_lo(pool, i, 1, own[1]).then_inc(qlo_done, 1)
                    pool.wait_ge(qlo_done, i + 1)

                split_lo(0)
                pool.wait_ge(dw_scaled, 1)
                for i in range(TILES):
                    if i + 1 < TILES:
                        split_lo(i + 1)
                    r = rows_of(i)
                    pool.wait_ge(gd_in[i % 2], 16 * (i // 2 + 1))
                    g = gd[0:r, i % 2, :].rearrange("p (h d) -> p h d", h=H)
                    pool.tensor_tensor(g, g, dw[0:r, :].unsqueeze(1).to_broadcast([r, H, DV]), ALU.mult)\
                        .then_inc(gate_done, 1)
                    pool.wait_ge(gate_done, i + 1)

            @block.tensor
            def _(pe):
                def scores(u):
                    i, h = units[u]
                    nq, nk = rq(i), keys(i)
                    last = i == TILES - 1
                    if h == 0:
                        pe.wait_ge(khi_done, i // 2 + 1)
                        pe.wait_ge(klo_done, i // 2 + 1)
                        pe.wait_ge(qhi_done, i + 1)
                        pe.wait_ge(qlo_done, i + 1)
                    if u == LAST0:
                        pe.wait_ge(turned_copied, 1 + max(n for n, b in enumerate(bank_of) if b < 2))
                    w = min(nk, P + nq)
                    d0 = P - (w - nq)
                    for m in range(2):
                        if u >= 1:
                            pe.wait_ge(exp_done, 2 * (u - 1) + m + 1)
                        width = nk if last else 2 * P * (i // 2 + 1)
                        for k0 in range(0, width, 512):
                            k1 = min(k0 + 512, width)
                            def product(x):
                                return pe.matmul(pS[0:nq, 1536 * m + k0:1536 * m + k1],
                                                 qs[:, i % 2, m, x, h, 0:nq], ks[:, m, h, k0:k1],
                                                 start=(x == 0), stop=(x == 1))

                            product(0)
                            n0, n1 = max(nk - w, k0), min(nk, k1)
                            if n0 < n1:
                                c = slice(d0 + n0 - (nk - w), d0 + n1 - (nk - w))
                                for band in (bh, bl):
                                    pe.matmul(pS[0:nq, 1536 * m + n0:1536 * m + n1], identr[:, 0:nq],
                                              band[:, h, c], start=False, stop=False)
                            ins = product(1)
                        ins.then_inc(scores_done, 1)

                def weigh(u):
                    i, h = units[u]
                    nq = rq(i)
                    pe.wait_ge(probs_done, u + 1)
                    for b in batches(u):
                        n = turn_no[b]
                        wait_bank(pe, n)
                        for j in range(b[2], b[3]):
                            kn = P if j < i else nq
                            at = (j - b[2]) * P
                            ins = pe.transpose(turn_banks[bank_of[n]][0:kn, at:at + nq],
                                               e[0:nq, u % 2, 0, P * j:P * j + kn], ident[0:nq, 0:nq])
                        ins.then_inc(turned_done, 1)
                    if u == 0:
                        pe.wait_ge(b_in, 16 * TILES)
                    if h == 0 and i >= 1:
                        pe.wait_ge(out_copied, i)
                    for b in batches(u):
                        pe.wait_ge(turned_copied, turn_no[b] + 1)
                        for j in range(b[2], b[3]):
                            kn = P if j < i else nq
                            ins = pe.matmul(pO[0:nq, h * DV:(h + 1) * DV], pT[0:kn, j, 0:nq],
                                            vd[0:kn, j, h * DV:(h + 1) * DV], start=(j == 0), stop=(j == i))
                    ins.then_inc(out_done, 1)

                def turn_mix(i):
                    r = rows_of(i)
                    n = turn_no[("m", i)]
                    pe.wait_ge(mix_done, i + 1)
                    wait_bank(pe, n)
                    for k in range(H):
                        ins = pe.transpose(turn_banks[bank_of[n]][:, k * P:k * P + r], mix[0:r, k * P:(k + 1) * P],
                                           ident[0:r, 0:r])
                    ins.then_inc(turned_done, 1)

                pe.wait_ge(bandhi_done, 2)
                pe.wait_ge(bandlo_done, 1)
                for u in range(NU + 1):
                    if u < NU:
                        scores(u)
                    if u >= 1:
                        weigh(u - 1)
                        if units[u - 1][1] == 1 and units[u - 1][0] >= 1:
                            turn_mix(units[u - 1][0] - 1)
                turn_mix(TILES - 1)

            @block.scalar
            def _(act):
                link = [0]

                def linked(ins):
                    link[0] += 1
                    ins.then_inc(ach2, 1)
                    act.wait_ge(ach2, link[0])

                def split_hi(p, i):
                    if p is not None:
                        k = slice(2 * P * p, min(2 * P * (p + 1), L))
                        for m in range(2):
                            ins = act.activation(ks[own[m], m, :, k], kT[own[m], :, k], ACT.Copy)
                        ins.then_inc(khi_done, 1)
                    nq = rq(i)
                    if i >= 2:
                        act.wait_ge(scores_done, 2 * H * (i - 1))
                    for m in range(2):
                        for to in own:
                            ins = act.activation(qs[to, i % 2, m, 0, :, 0:nq], qT[own[m], :, P * i:P * i + nq],
                                                 ACT.Copy)
                    ins.then_inc(qhi_done, 1)

                def expo(u, m):
                    i, h = units[u]
                    nq, nk = rq(i), keys(i)
                    act.wait_ge(max_done, 2 * u + m + 1)
                    if u >= 2:
                        act.wait_ge(probs_done, u - 1)
                        act.wait_ge(turned_done, last_batch(u - 2) + 1)
                    act.activation(e[0:nq, u % 2, m, 0:nk], pS[0:nq, 1536 * m:1536 * m + nk], ACT.Exp,
                                   bias=sm[0:nq, u % 2, m:m + 1], accum_out=sm[0:nq, u % 2, 2 + m:3 + m])\
                       .then_inc(exp_done, 1)

                def turned(b):
                    _, u, j0, j1 = b
                    i, h = units[u]
                    nq = rq(i)
                    n = turn_no[b]
                    bank = turn_banks[bank_of[n]]
                    act.wait_ge(turned_done, n + 1)
                    if u >= 1:
                        act.wait_ge(out_done, u)
                    full = [j for j in range(j0, j1) if j < i or nq == P]
                    if full:
                        ins = act.activation(pT[:, j0:j0 + len(full), 0:nq],
                                             bank[:, 0:len(full) * P].rearrange("p (j q) -> p j q", q=P)[:, :, 0:nq],
                                             ACT.Copy)
                    if len(full) < j1 - j0:
                        ins = act.activation(pT[0:nq, i, 0:nq], bank[0:nq, (i - j0) * P:(i - j0) * P + nq], ACT.Copy)
                    ins.then_inc(turned_copied, 1)

                def out(i):
                    nq, r = rq(i), rows_of(i)
                    act.wait_ge(out_done, 4 * i + 4)
                    if i >= 1:
                        act.wait_ge(mix_done, i)
                    if i == TILES - 1:
                        act.wait_ge(tail_ready, 1)
                    for h in range(H):
                        c = slice(h * DV, (h + 1) * DV)
                        ins = act.activation(ob[0:nq, c], pO[0:nq, c], ACT.Copy, scale=inv[0:nq, i % 2, h:h + 1])
                    ins.then_inc(out_copied, 1)
                    act.wait_ge(out_copied, i + 1)
                    for h in range(H):
                        ins = act.activation(squares_b[0:r, :], ob[0:r, h * DV:(h + 1) * DV], ACT.Square,
                                             accum_out=r4[0:r, 0, h:h + 1])
                        if h < H - 1:
                            linked(ins)
                    linked(ins)
                    linked(act.activation(r4[0:r, 1, :], r4[0:r, 0, :], ACT.Ln, scale=1.0 / DV, bias=eps[0:r, :]))
                    act.activation(r4[0:r, 2, :], r4[0:r, 1, :], ACT.Exp, scale=-0.5).then_inc(root_done, 1)

                def mixed(i):
                    r = rows_of(i)
                    n = turn_no[("m", i)]
                    act.wait_ge(turned_done, n + 1)
                    act.activation(mixT[:, 0:H, P * i:P * i + r],
                                   turn_banks[bank_of[n]].rearrange("p (k t) -> p k t", k=H)[:, :, 0:r], ACT.Copy)\
                       .then_inc(turned_copied, 1)

                split_hi(0, 0)
                act.activation(identr[:], ident[:], ACT.Copy).then_inc(bandhi_done, 1)
                act.wait_ge(band_in, 16 * (1 + H))
                act.activation(bh[:].rearrange("p h x -> p (h x)"), pT[:, 0:2 * H, :].rearrange("p j x -> p (j x)"),
                               ACT.Copy).then_inc(bandhi_done, 1)
                for u in range(NU + 1):
                    before = batches(u - 1) if u >= 1 else []
                    if before:
                        turned(before[0])
                    if u < NU:
                        expo(u, 0)
                    if len(before) > 1:
                        turned(before[1])
                    if u < NU:
                        expo(u, 1)
                    if len(before) > 2:
                        turned(before[2])
                    if u < NU and units[u][1] == 0 and units[u][0] + 1 < TILES:
                        i = units[u][0] + 1
                        split_hi(i // 2 if i % 2 == 0 else None, i)
                    if u >= 1:
                        i, h = units[u - 1]
                        if h == 3:
                            out(i)
                        if h == 1 and i >= 1:
                            mixed(i - 1)
                mixed(TILES - 1)

            @block.vector
            def _(dve):
                link = [0]

                def linked(ins):
                    link[0] += 1
                    ins.then_inc(dch2, 1)
                    dve.wait_ge(dch2, link[0])

                def maxima(u):
                    i, h = units[u]
                    nq, nk = rq(i), keys(i)
                    for m in range(2):
                        dve.wait_ge(scores_done, 2 * u + m + 1)
                        dve.tensor_reduce(sm[0:nq, u % 2, m:m + 1], pS[0:nq, 1536 * m:1536 * m + nk], AX.X, ALU.max,
                                          negate=True).then_inc(max_done, 1)

                def combine(u):
                    i, h = units[u]
                    nq, nk = rq(i), keys(i)
                    s = sm[0:nq, u % 2, :]
                    dve.wait_ge(exp_done, 2 * u + 2)
                    if h == 0 and i >= 2:
                        dve.wait_ge(out_copied, i - 1)
                    dve.reciprocal(inv[0:nq, i % 2, h:h + 1], s[:, 2:3])
                    linked(dve.reciprocal(s[:, 4:5], s[:, 3:4]))
                    linked(dve.scalar_tensor_tensor(out=s[:, 5:6], in0=s[:, 4:5], scalar=nlam[0:nq], in1=s[:, 2:3],
                                                    op0=ALU.mult, op1=ALU.mult))
                    e0, e1 = e[0:nq, u % 2, 0, 0:nk], e[0:nq, u % 2, 1, 0:nk]
                    dve.scalar_tensor_tensor(out=e0, in0=e1, scalar=s[:, 5:6], in1=e0, op0=ALU.mult, op1=ALU.add)\
                       .then_inc(probs_done, 1)

                def norm(i):
                    r = rows_of(i)
                    dve.wait_ge(gate_done, i + 1)
                    dve.wait_ge(root_done, i + 1)
                    if i >= 1:
                        dve.wait_ge(turned_done, turn_no[("m", i - 1)] + 1)
                    for h in range(H):
                        c = slice(h * DV, (h + 1) * DV)
                        ins = dve.scalar_tensor_tensor(out=mix[0:r, c], in0=ob[0:r, c], scalar=r4[0:r, 2, h:h + 1],
                                                       in1=gd[0:r, i % 2, c], op0=ALU.mult, op1=ALU.mult)
                    ins.then_inc(mix_done, 1)

                dve.memset(eps[:], EPS)
                dve.wait_ge(band_in, 16 * (1 + H))
                dve.tensor_scalar(dw[:], dw[:], 1.0 - LAM_INIT, None, ALU.mult).then_inc(dw_scaled, 1)
                dve.wait_ge(khi_done, 1)
                key_lo(dve, 0, 0)
                key_lo(dve, 0, 1).then_inc(klo_done, 1)
                dve.wait_ge(bandhi_done, 2)
                dve.tensor_tensor(bl[:].rearrange("p h x -> p (h x)"), pT[:, 0:2 * H, :].rearrange("p j x -> p (j x)"),
                                  bh[:].rearrange("p h x -> p (h x)").bitcast(F32), ALU.subtract)\
                   .then_inc(bandlo_done, 1)
                for u in range(NU + 1):
                    if u >= 1:
                        combine(u - 1)
                    if u < NU:
                        maxima(u)
                    if u >= 2 and units[u - 2][1] == 3:
                        norm(units[u - 2][0])
                        if units[u - 2][0] == TILES - 2:
                            dve.wait_ge(mix_done, TILES - 1)
                            linked(dve.memset(ob[0:S0, :], 0.0))
                            dve.tensor_copy(ob[S0:S0 + NS, :], od_s[:]).then_inc(tail_ready, 1)
                norm(TILES - 1)
        with ExitStack() as st:
            NL = LV + 1
            vg = sb(st, "vg", [P, 2, W])
            gg = sb(st, "gg", [P, 2, W])
            gw = sb(st, "gw", [P, DV])
            mask = sb(st, "mask", [P, P])
            mask8 = sb(st, "mask8", [LASTW, LASTW])
            colm = sb(st, "colm", [P, NB + 1, LASTW])
            rowm = sb(st, "rowm", [LASTW, NB + 1])
            dd = sb(st, "dd", [P, 2, NL, 2, 2, P])
            ff = sb(st, "ff", [P, 3, NL, 2, 2, P])
            ebl = sb(st, "ebl", [P, 3, 2, NB + 1])
            at = sb(st, "at", [P, 2, 2, 2, P])
            kd = sb(st, "kd", [P, 2, P])
            kd8 = sb(st, "kd8", [LASTW, NB + 1, 2 * P])
            q8 = sb(st, "q8", [P, 2, 2, NB + 1, LASTW])
            sp_ = sb(st, "state_p", [P, 2, DV])
            ss_ = sb(st, "state_s", [P, NB, 2, DV])
            og = sb(st, "og", [P, W])
            squares_g = sb(st, "squares_g", [P, DV])
            eps_g = sb(st, "eps_g", [P, 1])
            mixg = sb(st, "mix_g", [P, W])
            r4g = sb(st, "r4g", [P, 3, 4])
            pA = ps(st, "pA", [P, 4, 512])
            qz = sb(st, "qz", [P, 3, 2, 2, P])
            pOg = ps(st, "pOg", [P, 512])
            pK = ps(st, "pK", [P, 512])
            pdS = ps(st, "pdS", [P, 512])
            pM = ps(st, "pM", [P, 512])
            g_in = sem("g_in")
            vg_in = [sem(f"vg_in{n}") for n in range(2)]
            dzero = sem("dzero")
            dexp_in = sem("dexp_in")
            dexp = sem("dexp")
            fdone = sem("fdone")
            adone = sem("adone")
            amask = sem("amask")
            diag_done = sem("diag_done")
            ogd = sem("ogd")
            ogc = sem("ogc")
            kdt = sem("kdt")
            kdo = sem("kdo")
            kd8d = sem("kd8d")
            q8d = sem("q8d")
            dsd = sem("dsd")
            sdn = sem("state_done")
            ggd = sem("ggd")
            grr = sem("grr")
            mgd = sem("mgd")
            mgt = sem("mgt")
            mgo = sem("mgo")
            g_out = sem("g_out")
            pch3 = sem("pchain_g")
            ach3 = sem("achain_g")
            def level_groups(i):
                return [[LV - 1, LV - 2], list(range(LV - 2))] if i < TILES - 1 else [[LV - 1]]

            def groups_done(i, g):
                return 2 * i + g + 1

            block = st.enter_context(nc.Block())

            @block.sync
            def _(sp):
                sp.dma_start(gw[:], gla_norm_w.to_broadcast([P, DV])).then_inc(g_in, 16)
                sp.dma_start(mask[:], c_mask).then_inc(g_in, 16)
                sp.dma_start(mask8[:], c_mask8).then_inc(g_in, 16)
                sp.dma_start(colm[:], c_colm).then_inc(g_in, 16)
                sp.dma_start(rowm[:], c_rowm).then_inc(g_in, 16)
                for m in range(2):
                    sp.dma_start(ss_[:, :, m, :], state_gla[0].rearrange("b (m r) d e -> m (r d) b e", m=2)[m])\
                      .then_inc(g_in, 16)
                for i in range(TILES):
                    r = rows_of(i)
                    if i >= 2:
                        sp.wait_ge(mgd, i - 1)
                        sp.wait_ge(dsd, i - 1)
                        sp.wait_ge(ogd, i - 1)
                    sp.dma_start(vg[0:r, i % 2, :], val_g[i, 0:r, :]).then_inc(vg_in[i % 2], 16)
                    sp.dma_start(gg[0:r, i % 2, :], gate_g[i, 0:r, :]).then_inc(vg_in[i % 2], 16)
                sp.wait_ge(sdn, TILES + NB)
                for m in range(2):
                    sp.dma_start(s_sample[0].rearrange("b (m r) d e -> m (r d) b e", m=2)[m], ss_[:, :, m, :])\
                      .then_inc(g_out, 16)
                    sp.dma_start(s_prompt[0, 0].rearrange("(m r) d e -> m (r d) e", m=2)[m], sp_[:, m, :])\
                      .then_inc(g_out, 16)
                sp.wait_ge(g_out, 64)

            @block.tensor
            def _(pe):
                def products(i):
                    r = rows_of(i)
                    pe.wait_ge(fdone, i + 1)
                    for g, group in enumerate(level_groups(i)):
                        if i >= 1:
                            pe.wait_ge(amask, groups_done(i - 1, g))
                        for n in group:
                            s1, t0 = (HALVES[0], HALVES[0]) if n == 0 else (r, 0)
                            for h in range(H):
                                half = slice(DK * (h % 2), DK * (h % 2) + DK)
                                c0 = (n % 2) * 256 + (h // 2) * P
                                ins = pe.matmul(pA[0:s1, 2 * (n // 2) + h % 2, c0 + t0:c0 + r],
                                                ff[half, i % 3, n, 1, h // 2, 0:s1],
                                                ff[half, i % 3, n, 0, h // 2, t0:r], start=True, stop=True)
                        ins.then_inc(adone, 1)
                    if i >= 1:
                        pe.wait_ge(kdo, i)
                    for m in range(2):
                        ins = pe.transpose(pK[0:r, m * P:(m + 1) * P], ff[:, i % 3, LV, 1, m, 0:r], ident[:])
                    ins.then_inc(kdt, 1)

                def output(i):
                    r = rows_of(i)
                    pe.wait_ge(amask, groups_done(i, len(level_groups(i)) - 1))
                    pe.wait_ge(vg_in[i % 2], 32 * (i // 2 + 1))
                    if i >= 1:
                        pe.wait_ge(sdn, i)
                        pe.wait_ge(ogc, i)
                    if i == TILES - 1:
                        pe.wait_ge(q8d, 1)
                    for h in range(H):
                        to = pOg[0:r, h * DV:(h + 1) * DV]
                        ins = pe.matmul(to, at[0:r, i % 2, h % 2, h // 2, 0:r], vg[0:r, i % 2, h * DV:(h + 1) * DV],
                                        start=True, stop=(i == 0))
                        if 0 < i < TILES - 1:
                            ins = pe.matmul(to, qz[:, i % 3, h % 2, h // 2, :], sp_[:, h // 2, :],
                                            start=False, stop=True)
                        if i == TILES - 1:
                            for c in range(NB + 1):
                                of = sp_[:, h // 2, :] if c == 0 else ss_[:, c - 1, h // 2, :]
                                ins = pe.matmul(to, q8[:, h % 2, h // 2, c, :], of, start=False, stop=(c == NB))
                    ins.then_inc(ogd, 1)

                def state(i):
                    r = rows_of(i)
                    pe.wait_ge(kdo, i + 1)
                    if i >= 1:
                        pe.wait_ge(sdn, i)
                    for c in range(1 if i < TILES - 1 else NB + 1):
                        if i == TILES - 1:
                            pe.wait_ge(kd8d, 1)
                            pe.wait_ge(sdn, i + c)
                        for m in range(2):
                            k = kd[:, m, :] if i < TILES - 1 else kd8[:, c, m * P:(m + 1) * P]
                            ins = pe.matmul(pdS[:, m * 256:(m + 1) * 256], k, vg[0:r, i % 2, m * 256:(m + 1) * 256],
                                            start=True, stop=True)
                        ins.then_inc(dsd, 1)

                def turn_mix(i):
                    r = rows_of(i)
                    pe.wait_ge(mgd, i + 1)
                    if i >= 1:
                        pe.wait_ge(mgo, i)
                    for k in range(H):
                        ins = pe.transpose(pM[:, k * P:k * P + r], mixg[0:r, k * P:(k + 1) * P], ident[0:r, 0:r])
                    ins.then_inc(mgt, 1)

                pe.wait_ge(g_in, 16 * 7)
                pe.wait_ge(dzero, 1)
                products(0)
                for i in range(TILES):
                    if i + 1 < TILES:
                        products(i + 1)
                    output(i)
                    state(i)
                    if i >= 1:
                        turn_mix(i - 1)
                turn_mix(TILES - 1)

            @block.scalar
            def _(act):
                link = [0]

                def linked(ins):
                    link[0] += 1
                    ins.then_inc(ach3, 1)
                    act.wait_ge(ach3, link[0])

                def decays(i):
                    r = rows_of(i)
                    act.wait_ge(dexp_in, i + 1)
                    if i >= 3:
                        act.wait_ge(sdn, i - 2)
                    n0 = 0 if i < TILES - 1 else LV - 1
                    for n in range(n0, NL):
                        act.activation(ff[:, i % 3, n, :, :, 0:r], dd[:, i % 2, n, :, :, 0:r], ACT.Exp)
                    if i < TILES - 1:
                        act.activation(ebl[:, i % 3, :, 0:1], bT[:, :, P * i + P - 1:P * i + P], ACT.Exp)\
                           .then_inc(dexp, 1)
                    else:
                        act.activation(ebl[:, i % 3, :, 0:1], bT[:, :, P * i + TAIL - 1:P * i + TAIL], ACT.Exp)
                        act.activation(ebl[:, i % 3, :, 1:NB + 1],
                                       bT[:, :, P * i + S0:P * i + S0 + NS].rearrange("p m (b t) -> p m b t", t=TS)
                                       [:, :, :, TS - 1], ACT.Exp).then_inc(dexp, 1)

                def turned_k(i):
                    r = rows_of(i)
                    act.wait_ge(kdt, i + 1)
                    if i >= 1:
                        act.wait_ge(dsd, i)
                    act.activation(kd[0:r, :, :], pK[0:r, 0:2 * P].rearrange("p (m d) -> p m d", m=2), ACT.Copy)\
                       .then_inc(kdo, 1)

                def out(i):
                    r = rows_of(i)
                    act.wait_ge(ogd, i + 1)
                    if i >= 1:
                        act.wait_ge(mgd, i)
                    act.activation(og[0:r, :], pOg[0:r, :], ACT.Copy).then_inc(ogc, 1)
                    act.wait_ge(ogc, i + 1)
                    for h in range(H):
                        linked(act.activation(squares_g[0:r, :], og[0:r, h * DV:(h + 1) * DV], ACT.Square,
                                              accum_out=r4g[0:r, 0, h:h + 1]))
                    linked(act.activation(r4g[0:r, 1, :], r4g[0:r, 0, :], ACT.Ln, scale=1.0 / DV, bias=eps_g[0:r, :]))
                    act.activation(r4g[0:r, 2, :], r4g[0:r, 1, :], ACT.Exp, scale=-0.5).then_inc(grr, 1)

                def mixed(i):
                    r = rows_of(i)
                    act.wait_ge(mgt, i + 1)
                    act.activation(mixT[:, H:2 * H, P * i:P * i + r],
                                   pM[:, :].rearrange("p (k t) -> p k t", k=H)[:, :, 0:r], ACT.Copy)\
                       .then_inc(mgo, 1)

                act.wait_ge(dzero, 1)
                decays(0)
                decays(1)
                turned_k(0)
                for i in range(TILES):
                    if i + 2 < TILES:
                        decays(i + 2)
                    out(i)
                    if i + 1 < TILES:
                        turned_k(i + 1)
                    if i >= 1:
                        mixed(i - 1)
                mixed(TILES - 1)

            @block.gpsimd
            def _(pool):
                link = [0]

                def linked(ins):
                    link[0] += 1
                    ins.then_inc(pch3, 1)
                    pool.wait_ge(pch3, link[0])

                def exponents(i):
                    r = rows_of(i)
                    b = bT[:, :, P * i:P * i + r]
                    if i >= 2:
                        pool.wait_ge(dexp, i - 1)
                    if i < TILES - 1:
                        for n, half in enumerate(HALVES):
                            v = lambda a: a.rearrange("p m (n two x) -> p m n two x", two=2, x=half)
                            nb = P // (2 * half)
                            to_q, to_k, bb = v(dd[:, i % 2, n, 0]), v(dd[:, i % 2, n, 1]), v(b)
                            if nb == 1:
                                for m in range(2):
                                    ref = b[:, m, half - 1:half].to_broadcast([P, half])
                                    pool.tensor_tensor(dd[:, i % 2, n, 0, m, half:P], b[:, m, half:P], ref, ALU.subtract)
                                    pool.tensor_tensor(dd[:, i % 2, n, 1, m, 0:half], ref, b[:, m, 0:half], ALU.subtract)
                                continue
                            ref = bb[:, :, :, 0, half - 1:half].to_broadcast([P, 2, nb, half])
                            pool.tensor_tensor(to_q[:, :, :, 1, :], bb[:, :, :, 1, :], ref, ALU.subtract)
                            pool.tensor_tensor(to_k[:, :, :, 0, :], ref, bb[:, :, :, 0, :], ALU.subtract)
                        v = lambda a: a.rearrange("p m (n x) -> p m n x", x=DIAG)
                        ref = v(b)[:, :, :, DIAG // 2 - 1:DIAG // 2].to_broadcast([P, 2, P // DIAG, DIAG])
                        pool.tensor_tensor(v(dd[:, i % 2, LV - 1, 0]), v(b), ref, ALU.subtract)
                        linked(pool.tensor_tensor(v(dd[:, i % 2, LV - 1, 1]), ref, v(b), ALU.subtract))
                        last = b[:, :, P - 1:P].to_broadcast([P, 2, P])
                        pool.tensor_tensor(dd[:, i % 2, LV, 1], last, b, ALU.subtract)
                    else:
                        t, s = slice(0, TAIL), slice(S0, S0 + NS)
                        linked(pool.memset(dd[:, i % 2, LV - 1:NL, :, :, 0:r], 0.0))
                        ref = b[:, :, TAIL // 2 - 1:TAIL // 2].to_broadcast([P, 2, TAIL])
                        pool.tensor_tensor(dd[:, i % 2, LV - 1, 0, :, t], b[:, :, t], ref, ALU.subtract)
                        pool.tensor_tensor(dd[:, i % 2, LV - 1, 1, :, t], ref, b[:, :, t], ALU.subtract)
                        pool.tensor_copy(dd[:, i % 2, LV - 1, 0, :, s], b[:, :, s])
                        linked(pool.tensor_scalar(dd[:, i % 2, LV - 1, 1, :, s], b[:, :, s], -1.0, None, ALU.mult))
                        pool.tensor_tensor(dd[:, i % 2, LV, 1, :, t], b[:, :, TAIL - 1:TAIL].to_broadcast([P, 2, TAIL]),
                                          b[:, :, t], ALU.subtract)
                        v = lambda a: a.rearrange("p m (b t) -> p m b t", t=TS)
                        pool.tensor_tensor(v(dd[:, i % 2, LV, 1, :, s]), v(b[:, :, s])[:, :, :, TS - 1:TS]
                                          .to_broadcast([P, 2, NB, TS]), v(b[:, :, s]), ALU.subtract)
                    pool.tensor_copy(dd[:, i % 2, LV, 0, :, 0:r], b)
                    pool.tensor_scalar(dd[:, i % 2, LV - 1, :, :, 0:r], dd[:, i % 2, LV - 1, :, :, 0:r], 80.0, None, ALU.min)\
                       .then_inc(dexp_in, 1)

                def gate(i):
                    r = rows_of(i)
                    pool.wait_ge(vg_in[i % 2], 32 * (i // 2 + 1))
                    g = gg[0:r, i % 2, :].rearrange("p (h d) -> p h d", h=H)
                    pool.tensor_tensor(g, g, gw[0:r, :].unsqueeze(1).to_broadcast([r, H, DV]), ALU.mult)\
                        .then_inc(ggd, 1)

                linked(pool.memset(dd[:], 0.0))
                exponents(0)
                exponents(1)
                pool.wait_ge(g_in, 16 * 7)
                for i in range(TILES):
                    if i + 2 < TILES:
                        exponents(i + 2)
                    gate(i)

            @block.vector
            def _(dve):
                def factors(i):
                    r = rows_of(i)
                    dve.wait_ge(dexp, i + 1)
                    n0 = 0 if i < TILES - 1 else LV - 1
                    t = slice(P * i, P * i + r)
                    for hh in range(2):
                        half = slice(DK * hh, DK * hh + DK)
                        dve.tensor_tensor(qz[half, i % 3, hh, :, 0:r], ff[half, i % 3, LV, 0, :, 0:r], gqT[half, :, t],
                                          ALU.mult)
                    to = ff[:, i % 3, n0:LV, 0, :, 0:r]
                    dve.tensor_tensor(to, to, gqT[:, :, t].unsqueeze(1).to_broadcast([P, LV - n0, 2, r]), ALU.mult)
                    to = ff[:, i % 3, n0:NL, 1, :, 0:r]
                    dve.tensor_tensor(to, to, gkT[:, :, t].unsqueeze(1).to_broadcast([P, NL - n0, 2, r]), ALU.mult)\
                       .then_inc(fdone, 1)
                    if i == TILES - 1:
                        dve.wait_ge(fdone, i + 1)
                        for hh in range(2):
                            for m in range(2):
                                ins = dve.tensor_tensor(q8[:, hh, m], qz[:, i % 3, hh, m, 0:r].unsqueeze(1)
                                                        .to_broadcast([P, NB + 1, r]), colm[:], ALU.mult)
                        ins.then_inc(q8d, 1)

                def masks(i):
                    r = rows_of(i)
                    if i >= 2:
                        dve.wait_ge(ogd, i - 1)

                    def sums(n, s, t):
                        return pA[s, 2 * (n // 2):2 * (n // 2) + 2, (n % 2) * 256:(n % 2) * 256 + 256]\
                            .rearrange("p a (m t) -> p a m t", m=2)[:, :, :, t]

                    for g, group in enumerate(level_groups(i)):
                        dve.wait_ge(adone, groups_done(i, g))
                        for n in group:
                            if n == LV - 1:
                                mk = (mask if r == P else mask8)[:, :].unsqueeze(1).unsqueeze(1)\
                                    .to_broadcast([r, 2, 2, r])
                                every = slice(0, r)
                                ins = dve.tensor_tensor(at[0:r, i % 2, :, :, 0:r], sums(n, every, every), mk, ALU.mult)
                                if i < TILES - 1:
                                    ins.then_inc(diag_done, 1)
                                    dve.wait_ge(diag_done, i + 1)
                                continue
                            half = HALVES[n]
                            for s0 in range(0, P, 2 * half):
                                s, t = slice(s0, s0 + half), slice(s0 + half, s0 + 2 * half)
                                ins = dve.tensor_copy(at[s, i % 2, :, :, t], sums(n, s, t))
                        ins.then_inc(amask, 1)

                def state(i):
                    r = rows_of(i)
                    if i == TILES - 1:
                        dve.wait_ge(kdo, i + 1)
                        dve.tensor_tensor(kd8[:], kd[0:r].rearrange("p m d -> p (m d)").unsqueeze(1)
                                          .to_broadcast([r, NB + 1, 2 * P]),
                                          rowm[:].unsqueeze(2).to_broadcast([r, NB + 1, 2 * P]), ALU.mult)\
                           .then_inc(kd8d, 1)
                        dve.wait_ge(ogd, i + 1)
                    for c in range(1 if i < TILES - 1 else NB + 1):
                        dve.wait_ge(dsd, i + c + 1)
                        if c == 0 and i >= 1:
                            dve.wait_ge(ogd, i + 1)
                        for m in range(2):
                            for hh in range(2):
                                half = slice(DK * hh, DK * hh + DK)
                                ds = pdS[half, m * 256 + hh * P:m * 256 + hh * P + P]
                                to = sp_[half, m, :] if c == 0 else ss_[half, c - 1, m, :]
                                if i == 0:
                                    ins = dve.tensor_copy(to, ds)
                                else:
                                    ins = dve.scalar_tensor_tensor(out=to, in0=to,
                                                                   scalar=ebl[half, i % 3, m, c:c + 1],
                                                                   in1=ds, op0=ALU.mult, op1=ALU.add)
                        ins.then_inc(sdn, 1)

                def norm(i):
                    r = rows_of(i)
                    dve.wait_ge(ggd, i + 1)
                    dve.wait_ge(grr, i + 1)
                    if i >= 1:
                        dve.wait_ge(mgt, i)
                    for h in range(H):
                        c = slice(h * DV, (h + 1) * DV)
                        ins = dve.scalar_tensor_tensor(out=mixg[0:r, c], in0=og[0:r, c], scalar=r4g[0:r, 2, h:h + 1],
                                                       in1=gg[0:r, i % 2, c], op0=ALU.mult, op1=ALU.mult)
                    ins.then_inc(mgd, 1)

                dve.memset(eps_g[:], EPS)
                dve.memset(qz[:], 0.0).then_inc(dzero, 1)
                dve.wait_ge(dzero, 1)
                dve.wait_ge(g_in, 16 * 7)
                factors(0)
                factors(1)
                for i in range(TILES):
                    if i >= 1:
                        state(i - 1)
                    masks(i)
                    if i >= 1:
                        norm(i - 1)
                    if i + 2 < TILES:
                        factors(i + 2)
                state(TILES - 1)
                norm(TILES - 1)

        with ExitStack() as st:
            wor = sb(st, "wor", [P, 2, D])
            woh = sb(st, "woh", [P, KT, D], F32R)
            wol = sb(st, "wol", [P, KT, D], F32R)
            mh = sb(st, "mh", [P, 2, KT, P], F32R)
            ml = sb(st, "ml", [P, 2, KT, P], F32R)
            xr = sb(st, "xr", [P, 2, D])
            pY = [ps(st, f"pY{n}", [P, 512]) for n in range(4)]
            wo_in = [sem(f"wo_in{n}") for n in range(2)]
            xr_in = [sem(f"xr_in{n}") for n in range(2)]
            woh_d = sem("woh_d")
            wol_d = sem("wol_d")
            mh_d = sem("mh_d")
            ml_d = sem("ml_d")
            y_done = sem("y_done")
            y_sum = sem("y_sum")
            y_out = [sem(f"y_out{n}") for n in range(2)]

            def parts(i):
                if i == 0:
                    return [(NMETA, P, x_prompt[0, 0:P - NMETA, :], y_prompt[0, 0:P - NMETA, :])]
                if i < TILES - 1:
                    rows = slice(P * i - NMETA, P * (i + 1) - NMETA)
                    return [(0, P, x_prompt[0, rows, :], y_prompt[0, rows, :])]
                return [(0, TAIL, x_prompt[0, SEQ - TAIL:SEQ, :], y_prompt[0, SEQ - TAIL:SEQ, :]),
                        (S0, S0 + NS, x_sample.rearrange("b t d -> (b t) d"),
                         y_sample.rearrange("b t d -> (b t) d"))]

            def moved(i):
                return 16 * sum(len(parts(j)) for j in range(i % 2, i + 1, 2))

            block = st.enter_context(nc.Block())
            xz = sem("xr_zero")

            @block.sync
            def _(sp):
                for k in range(KT):
                    if k >= 2:
                        sp.wait_ge(woh_d, k - 1)
                        sp.wait_ge(wol_d, k - 1)
                    sp.dma_start(wor[:, k % 2, :], w_out[0, k * P:(k + 1) * P, :]).then_inc(wo_in[k % 2], 16)
                sp.wait_ge(xz, 1)
                for i in range(TILES + 1):
                    if i < TILES:
                        if i >= 2:
                            sp.wait_ge(y_out[i % 2], moved(i - 2))
                        if i == TILES - 1:
                            sp.wait_ge(xz, 2)
                        for a, b, x, _ in parts(i):
                            sp.dma_start(xr[a:b, i % 2, :], x).then_inc(xr_in[i % 2], 16)
                    if i >= 1:
                        sp.wait_ge(y_sum, 2 * i)
                        for a, b, _, y in parts(i - 1):
                            sp.dma_start(y, xr[a:b, (i - 1) % 2, :]).then_inc(y_out[(i - 1) % 2], 16)
                sp.wait_ge(y_out[0], moved(TILES - 1))
                sp.wait_ge(y_out[1], moved(TILES - 2))

            @block.scalar
            def _(act):
                def mix_hi(i):
                    r = rows_of(i)
                    if i >= 2:
                        act.wait_ge(y_done, 2 * (i - 1))
                    act.activation(mh[:, i % 2, :, 0:r], mixT[:, :, P * i:P * i + r], ACT.Copy).then_inc(mh_d, 1)

                mix_hi(0)
                for k in range(KT):
                    act.wait_ge(wo_in[k % 2], 16 * (k // 2 + 1))
                    act.activation(woh[:, k, :], wor[:, k % 2, :], ACT.Copy).then_inc(woh_d, 1)
                for i in range(1, TILES):
                    mix_hi(i)

            @block.vector
            def _(dve):
                def mix_lo(i):
                    r = rows_of(i)
                    dve.wait_ge(mh_d, i + 1)
                    dve.tensor_tensor(ml[:, i % 2, :, 0:r], mixT[:, :, P * i:P * i + r],
                                      mh[:, i % 2, :, 0:r].bitcast(F32), ALU.subtract).then_inc(ml_d, 1)

                def add(i):
                    r = rows_of(i)
                    for n in range(2):
                        dve.wait_ge(y_done, 2 * i + n + 1)
                        dve.wait_ge(xr_in[i % 2], moved(i))
                        x = xr[0:r, i % 2, n * 512:(n + 1) * 512]
                        dve.tensor_tensor(x, x, pY[2 * (i % 2) + n][0:r, :], ALU.add).then_inc(y_sum, 1)

                dve.memset(xr[0:S0, 0, :], 0.0).then_inc(xz, 1)
                mix_lo(0)
                for k in range(KT):
                    dve.wait_ge(woh_d, k + 1)
                    dve.tensor_tensor(wol[:, k, :], wor[:, k % 2, :], woh[:, k, :].bitcast(F32), ALU.subtract)\
                       .then_inc(wol_d, 1)
                for i in range(TILES):
                    if i + 1 < TILES:
                        mix_lo(i + 1)
                    add(i)
                    if i == TILES - 3:
                        dve.wait_ge(y_out[0], moved(TILES - 3))
                        dve.memset(xr[0:S0, 0, :], 0.0).then_inc(xz, 1)

            @block.tensor
            def _(pe):
                for i in range(TILES):
                    r = rows_of(i)
                    pe.wait_ge(mh_d, i + 1)
                    pe.wait_ge(ml_d, i + 1)
                    for n in range(2):
                        if i >= 2:
                            pe.wait_ge(y_sum, 2 * (i - 2) + n + 1)
                        for k in range(KT):
                            if i == 0 and n == 0:
                                pe.wait_ge(woh_d, k + 1)
                                pe.wait_ge(wol_d, k + 1)
                            for x, (a, b) in enumerate(((mh, woh), (ml, woh), (mh, wol))):
                                ins = pe.matmul(pY[2 * (i % 2) + n][0:r, :], a[:, i % 2, k, 0:r],
                                                b[:, k, n * 512:(n + 1) * 512], start=(k == 0 and x == 0),
                                                stop=(k == KT - 1 and x == 2))
                        ins.then_inc(y_done, 1)


def shape_constants():
    import numpy as np
    f = np.float32
    c = {"c_ident": np.eye(P, dtype=f)}
    a = np.arange(P)
    c["c_cum"] = ((a[:, None] <= a[None, :]) / 16.0).astype(f)
    a8 = np.arange(LASTW)
    chunk = np.where(a8 < TAIL, 0, np.where(a8 < S0, 100 + a8, 1 + (a8 - S0) // TS))
    same = (chunk[:, None] == chunk[None, :]) & (a8[:, None] <= a8[None, :])
    c["c_cum8"] = (same / 16.0).astype(f)
    s, t = a[:, None], a[None, :]
    c["c_mask"] = ((s // DIAG == t // DIAG) & (s <= t)).astype(f)
    c["c_mask8"] = same.astype(f)
    n = np.arange(0, PAST + TS)
    nf = np.maximum(n, 1).astype(f)
    large = 16 + (np.log(nf / f(16)) / f(math.log(128 / 16)) * f(16)).astype(np.int32)
    bucket = np.where(n < 16, n, np.minimum(large, 31))

    def hot(n):
        o = np.zeros((32, n.size), f)
        ok = n.ravel() >= 0
        o[bucket[np.maximum(n.ravel(), 0)], np.arange(n.size)] = 1
        o[31, :] -= 1
        o[:, ~ok] = 0
        return o
    d = 255 - np.arange(384)
    c["c_oh"] = hot(d)
    c["c_negp"] = np.broadcast_to(np.where(d < 0, NEG, 0).astype(f), (H, 384)).copy()
    q = np.arange(TS)
    c["c_hotp"] = hot(PAST + q[:, None] - (PAST - PAGE + np.arange(PAGE))[None, :]).reshape(32, TS * PAGE)
    j = np.arange(NS)
    dn = np.stack([np.where((j // TS == b), q[:, None] - (j % TS)[None, :], -1) for b in range(NB)], 1)
    c["c_hotn"] = hot(dn).reshape(32, TS, NB * NS)
    row = np.arange(32)
    neg = np.where(dn < 0, NEG, 0).astype(f)
    c["c_negn"] = neg[row % TS].reshape(32, NB * NS)
    c["c_rowq"] = np.broadcast_to((row[None, :] % TS == q[:, None]).astype(f), (32, TS, 32)).copy()
    pr = np.arange(P) % 32
    sel = np.zeros((P, NB, H, NS), f)
    for b in range(NB):
        for h in range(H):
            sel[:, b, h, :] = (pr[:, None] // 8 == h) & (b * TS + pr[:, None] % TS == np.arange(NS)[None, :])
    c["c_selT"] = sel
    c["c_m01"] = np.stack([(row // 4 % 2 == 0), (row // 4 % 2 == 1)], 1).astype(f)
    own = (chunk[None, :] == np.arange(NB + 1)[:, None]).astype(f)
    c["c_colm"] = np.broadcast_to(own, (P, NB + 1, LASTW)).copy()
    c["c_rowm"] = own.T.copy()
    return c


_INS = ["x_prompt", "x_sample", "cache_k", "cache_v", "state_gla", "page_table", "meta_tokens", "rel_bias",
        "norm_w", "w_in", "q_norm_w", "k_norm_w", "lam_q", "lam_k", "diff_norm_w", "gla_wa2", "gla_ba",
        "gla_norm_w", "w_out"]
_CONSTS = ["c_ident", "c_cum", "c_cum8", "c_mask", "c_mask8", "c_oh", "c_hotp", "c_hotn", "c_negn", "c_negp",
           "c_rowq", "c_selT", "c_colm", "c_rowm", "c_m01"]
_OUTS = [(1, SEQ, D), (NB, TS, D), (1, 1, L, H, 2 * DK), (1, 1, L, H, DV), (1, 1, H, DK, DV),
         (1, NB, TS, H, 2 * DK), (1, NB, TS, H, DV), (1, NB, H, DK, DV)]


def kernel(**inputs):
    import numpy as np
    import concourse.bacc as bacc
    from concourse.bass_utils import run_bass_kernel_spmd

    nc = bacc.Bacc("TRN2", target_bir_lowering=False, num_devices=1)
    consts = shape_constants()
    arrays, args = {}, []
    for name in _INS + _CONSTS:
        a = np.ascontiguousarray(inputs[name] if name in inputs else consts[name])
        arrays[f"in_{name}"] = a
        args.append(nc.dram_tensor(f"in_{name}", a.shape, mybir.dt.from_np(a.dtype), kind="ExternalInput").ap())
    for n, shape in enumerate(_OUTS):
        args.append(nc.dram_tensor(f"out_{n}", shape, F32, kind="ExternalOutput").ap())
    hymba_kernel(nc, *args)
    r = run_bass_kernel_spmd(nc, [arrays], core_ids=[0])
    return tuple(r.results[0][f"out_{n}"] for n in range(len(_OUTS)))
```

```python
from contextlib import ExitStack
import math

import concourse.bass as bass
from concourse import mybir

F32 = mybir.dt.float32
F32R = mybir.dt.float32r
I32 = mybir.dt.int32
ALU = mybir.AluOpType
ACT = mybir.ActivationFunctionType
AX = mybir.AxisListType

P = 128
D = 1024
KT = D // P
NMETA, SEQ = 16, 1024
L = NMETA + SEQ
NB, TS = 8, 4
NS = NB * TS
TILES = L // P + 1
TAIL = L - P * (TILES - 1)
LASTW = 64
S0 = 32
NTOK = P * (TILES - 1) + LASTW
H, DK, DV = 4, 64, 128
W = H * DV
PAGE, NPAGES, POOL = 128, 32, 320
GRP = 4
G = NPAGES // GRP
PAST = PAGE * NPAGES
DIN = 3600
CB = 256
EPS = 1e-6
LAM_INIT = 0.8 - 0.6 * math.exp(0.0)
NEG = -1e30

HALVES = (64, 32, 16)
DIAG = 16
LV = len(HALVES) + 1

KINDS = ["q", "q", "k", "k", "v", "v", "dg", "dg", "gq", "gk", "ga", "gv", "gv", "gg", "gg"]
GA = KINDS.index("ga")
W_AT = [CB * c for c in range(GA)] + [DIN - 16] + [CB * c for c in range(GA, len(KINDS) - 1)]
W_N = [16 if k == "ga" else CB for k in KINDS]
NZ = 4


def rows_of(i):
    return P if i < TILES - 1 else LASTW


def hymba_kernel(nc, x_prompt, x_sample, cache_k, cache_v, state_gla, page_table, meta_tokens, rel_bias,
                 norm_w, w_in, q_norm_w, k_norm_w, lam_q, lam_k, diff_norm_w, gla_wa2, gla_ba, gla_norm_w,
                 w_out, c_ident, c_cum, c_cum8, c_mask, c_mask8, c_oh, c_hotp, c_hotn, c_negn, c_negp, c_rowq, c_selT,
                 c_colm, c_rowm, c_m01,
                 y_prompt, y_sample, k_prompt, v_prompt, s_prompt, k_sample, v_sample, s_sample):
    ctx = ExitStack()
    with ctx:
        def sem(name):
            return ctx.enter_context(nc.semaphore(name))

        def sb(stack, name, shape, dt=F32):
            return stack.enter_context(nc.sbuf_tensor(name, shape, dt))

        def ps(stack, name, shape):
            return stack.enter_context(nc.psum_tensor(name, shape, F32))

        def dram(name, shape):
            return nc.dram_tensor(name, shape, F32, kind="Internal").ap()

        gate_d = dram("gate_d", (TILES, P, W))
        gate_g = dram("gate_g", (TILES, P, W))
        val_g = dram("val_g", (TILES, P, W))
        val_d = dram("val_d", (TILES, P, W))
        skew = dram("skew", (H, P * 384))

        ident = sb(ctx, "ident", [P, P])
        qT = sb(ctx, "qT", [P, H, NTOK])
        kT = sb(ctx, "kT", [P, H, NTOK])
        gqT = sb(ctx, "gqT", [P, 2, NTOK])
        gkT = sb(ctx, "gkT", [P, 2, NTOK])
        bT = sb(ctx, "bT", [P, 2, NTOK])
        lam = sb(ctx, "lam", [P, 8])
        nlam = lam[:, 7:8]
        od_s = sb(ctx, "od_s", [NS, W])
        pages = sb(ctx, "pages", [1, NB * NPAGES], I32)
        nat = sb(ctx, "nat", [P, 3, CB])
        nat_stored = [sem(f"nat_stored{n}") for n in range(3)]

        with ExitStack() as st:
            xTh = sb(st, "xTh", [P, KT, NTOK], F32R)
            xTl = sb(st, "xTl", [P, KT, NTOK], F32R)
            xb = sb(st, "xb", [P, 2, D])
            wraw = sb(st, "wraw", [P, 2, KT, CB])
            wh = sb(st, "wh", [P, 2, KT, CB], F32R)
            wl = sb(st, "wl", [P, 2, KT, CB], F32R)
            squares = sb(st, "squares", [P, D])
            nw = sb(st, "nw", [P, KT])
            qwr = sb(st, "qwr", [P, 2, CB])
            ss = sb(st, "ss", [P, 4, TILES])
            sq = sb(st, "sq", [P, 2, CB])
            rms = sb(st, "rms", [P, 2, 3, 4])
            nrm = sb(st, "nrm", [P, CB])
            gaT = sb(st, "gaT", [48, NTOK])
            wa2 = sb(st, "wa2", [48, CB])
            cum = sb(st, "cum", [P, P])
            cum8 = sb(st, "cum8", [LASTW, LASTW])
            lg = squares[:, 0:2 * CB].rearrange("p (a c) -> p a c", a=2)
            lgm = squares[:, 2 * CB:4 * CB].rearrange("p (a c) -> p a c", a=2)
            lmv = sb(st, "lmv", [P, 4, P])
            pz = [ps(st, f"pz{n}", [P, 512]) for n in range(NZ)]
            pt = ps(st, "pt", [P, 2, 512])
            pn = ps(st, "pn", [P, 2, 512])

            x_loaded = [sem(f"x_loaded{n}") for n in range(2)]
            ident_in = sem("ident_in")
            pages_in = sem("pages_in")
            nw_in = sem("nw_in")
            consts_in = sem("consts_in")
            w_loaded = [sem(f"w_loaded{n}") for n in range(2)]
            sumsq_done = sem("sumsq_done")
            meansq_done = sem("meansq_done")
            ln_done = sem("ln_done")
            rstd_done = sem("rstd_done")
            hn_done = sem("hn_done")
            xt_done = sem("xt_done")
            xhi_done = sem("xhi_done")
            xlo_done = sem("xlo_done")
            whi_done = sem("whi_done")
            wlo_done = sem("wlo_done")
            z_done = sem("z_done")
            turned_out = sem("turned_out")
            sq_done = sem("sq_done")
            ms_done = sem("ms_done")
            r_done = sem("r_done")
            nat_done = sem("nat_done")
            nt_done = sem("nt_done")
            nt_out = sem("nt_out")
            dchain = sem("dchain_a")
            achain = sem("achain_a")
            ga_done = sem("ga_done")
            log_in = sem("log_in")
            lnexp_done = sem("lnexp_done")
            lg_done = sem("lg_done")
            cum_done = sem("cum_done")
            cum_out = sem("cum_out")
            lam_exp = sem("lam_exp")
            lam_sum = sem("lam_sum")

            natural = [(c, i) for c, k in enumerate(KINDS) if k not in ("gq", "gk", "ga") for i in range(TILES)]
            turned = [c for c, k in enumerate(KINDS) if k in ("gq", "gk")]
            NN = len(natural)

            def kind(s):
                return KINDS[natural[s][0]]

            def count(kinds, s):
                return sum(1 for t in range(s + 1) if kind(t) in kinds)

            ACTIVE = ("q", "k", "dg", "gg")
            LOGS = GA + 1
            CH = [(0, 384), (384, 384), (768, NTOK - 768)]
            uses = []
            for c, k in enumerate(KINDS):
                if k in ("gq", "gk"):
                    uses += [("t", c, m, n) for m in range(2) for n in range(3)]
                elif k == "ga":
                    uses += [("a", c, n) for n in range(3)]
                else:
                    for i in range(TILES):
                        uses.append(("n", c, i))
                        if c == LOGS:
                            uses.append(("l", i))
            use_of = {u: n for n, u in enumerate(uses)}
            step_of = {x: n for n, x in enumerate(natural)}
            turned_uses = [u for u in uses if u[0] in "ta"]
            BLOCK_END = [1 + max(n for n, u in enumerate(uses) if u[0] in "nta" and u[1] == c)
                         for c in range(len(KINDS))]
            X_IN = [32, 16, 48, 32, 64, 48, 80, 64, 128]

            def wait_z(eng, u):
                if u < NZ:
                    return
                before = uses[u - NZ]
                if before[0] == "n":
                    eng.wait_ge(nat_done, step_of[before[1:]] + 1)
                elif before[0] in "ta":
                    eng.wait_ge(turned_out, turned_uses.index(before) + 1)
                else:
                    eng.wait_ge(lg_done, before[1] + 1)

            def z_at(n):
                return pz[n % NZ]

            def stored(s):
                c, i = natural[s]
                k = KINDS[c]
                last = i == TILES - 1
                return {"q": 0, "k": 1 + last, "v": 2 + last}.get(k, 1)

            def stored_upto(s, slot):
                return sum(stored(t) for t in range(s + 1) if t % 3 == slot)

            all_stored = [16 * stored_upto(NN - 1, n) for n in range(3)]
            block = st.enter_context(nc.Block())

            @block.sync
            def _(sp):
                def load_x(i):
                    if i >= 2:
                        sp.wait_ge(xt_done, 2 * (i - 1))
                    if i == 0:
                        sp.dma_start(xb[0:NMETA, 0, :], meta_tokens).then_inc(x_loaded[0], 16)
                        sp.dma_start(xb[NMETA:P, 0, :], x_prompt[0, 0:P - NMETA, :]).then_inc(x_loaded[0], 16)
                    elif i < TILES - 1:
                        sp.dma_start(xb[:, i % 2, :], x_prompt[0, P * i - NMETA:P * (i + 1) - NMETA, :])\
                          .then_inc(x_loaded[i % 2], 16)
                    else:
                        for r in (0, TAIL):
                            sp.dma_start(xb[r:r + TAIL, i % 2, :], x_prompt[0, SEQ - TAIL:SEQ, :])\
                              .then_inc(x_loaded[i % 2], 16)
                        sp.dma_start(xb[S0:S0 + NS, i % 2, :], x_sample.rearrange("b t d -> (b t) d"))\
                          .then_inc(x_loaded[i % 2], 16)

                def load_w(c):
                    if c >= 2:
                        sp.wait_ge(whi_done, KT * (c - 1))
                        sp.wait_ge(wlo_done, KT * (c - 1))
                        if c == GA + 2:
                            sp.wait_ge(z_done, BLOCK_END[GA])
                    n = W_N[c]
                    sp.dma_start(wraw[:, c % 2, :, 0:n],
                                 w_in[0, :, W_AT[c]:W_AT[c] + n].rearrange("(t p) n -> p t n", p=P))\
                      .then_inc(w_loaded[c % 2], 16)

                load_x(0)
                sp.dma_start(ident[:], c_ident).then_inc(ident_in, 16)
                load_w(0)
                sp.dma_start(nw[:], norm_w.rearrange("a (t p) -> p (a t)", p=P), allow_slow_non_contiguous=True)\
                  .then_inc(nw_in, 16)
                load_x(1)
                for m in range(2):
                    sp.dma_start(lmv[:, m, :], lam_q.rearrange("a m d -> a (m d)").to_broadcast([P, P]) if m == 0
                                 else lam_k.rearrange("a m d -> a (m d)").to_broadcast([P, P])).then_inc(consts_in, 16)
                for n, wt in enumerate((q_norm_w, k_norm_w)):
                    for h in range(2):
                        sp.dma_start(qwr[:, n, h * P:(h + 1) * P],
                                     wt.rearrange("a m d -> a (m d)").to_broadcast([P, P])).then_inc(consts_in, 16)
                sp.dma_start(cum[:], c_cum).then_inc(consts_in, 16)
                sp.dma_start(cum8[:], c_cum8).then_inc(consts_in, 16)
                sp.wait_ge(ga_done, 1)
                sp.dma_start(wa2[0:16, :], gla_wa2[0]).then_inc(consts_in, 16)
                sp.dma_start(wa2[16:17, :], gla_ba).then_inc(consts_in, 16)
                sp.dma_start(wa2[32:48, :], gla_wa2[0]).then_inc(consts_in, 16)
                sp.dma_start(pages[:], page_table.rearrange("(o b) n -> o (b n)", o=1)).then_inc(pages_in, 16)
                load_w(1)
                for i in range(2, TILES):
                    load_x(i)
                stores = {k: (to, KINDS.index(k)) for k, to in
                          (("v", val_d), ("gv", val_g), ("dg", gate_d), ("gg", gate_g))}
                nextw = 2
                for s, (c, i) in enumerate(natural):
                    if i == 0:
                        while nextw <= min(c + 2, len(KINDS) - 1):
                            load_w(nextw)
                            nextw += 1
                    k = kind(s)
                    at = nat_stored[s % 3]
                    sp.wait_ge(nat_done, s + 1)
                    r = rows_of(i)
                    if k == "q":
                        continue
                    if k in stores:
                        to, first = stores[k]
                        cols = slice((c - first) * CB, (c - first + 1) * CB)
                        sp.dma_start(to[i, 0:r, cols], nat[0:r, s % 3, :]).then_inc(at, 16)
                    if k in ("k", "v"):
                        first = 2 if k == "k" else 4
                        op, os_ = (k_prompt, k_sample) if k == "k" else (v_prompt, v_sample)
                        cols = slice((c - first) * CB, (c - first + 1) * CB)
                        dst = op.rearrange("a b l h d -> (a b l) (h d)")
                        n = P if i < TILES - 1 else TAIL
                        sp.dma_start(dst[P * i:P * i + n, cols], nat[0:n, s % 3, :]).then_inc(at, 16)
                        if i == TILES - 1:
                            dst = os_.rearrange("a b t h d -> (a b t) (h d)")
                            sp.dma_start(dst[:, cols], nat[S0:S0 + NS, s % 3, :]).then_inc(at, 16)
                while nextw < len(KINDS):
                    load_w(nextw)
                    nextw += 1
                for n in range(3):
                    sp.wait_ge(nat_stored[n], 16 * stored_upto(NN - TILES - 1, n))
                sp.wait_ge(pages_in, 16)

            @block.gpsimd
            def _(pool):
                pass

            @block.scalar
            def _(act):
                link = [0]

                def linked(ins):
                    link[0] += 1
                    ins.then_inc(achain, 1)
                    act.wait_ge(achain, link[0])

                def x_sumsq(i):
                    r = rows_of(i)
                    act.wait_ge(x_loaded[i % 2], X_IN[i])
                    act.activation(squares[0:r, :], xb[0:r, i % 2, :], ACT.Square,
                                   accum_out=ss[0:r, 0, i:i + 1]).then_inc(sumsq_done, 1)
                    act.wait_ge(meansq_done, i + 1)
                    linked(act.activation(ss[0:r, 2, i:i + 1], ss[0:r, 1, i:i + 1], ACT.Ln))
                    act.activation(ss[0:r, 3, i:i + 1], ss[0:r, 2, i:i + 1], ACT.Exp, scale=-0.5)\
                       .then_inc(rstd_done, 1)

                def x_hi(i):
                    r = rows_of(i)
                    for half in range(2):
                        act.wait_ge(xt_done, 2 * i + half + 1)
                        act.activation(xTh[:, 4 * half:4 * half + 4, P * i:P * i + r],
                                       pt[:, half, :].rearrange("p (k t) -> p k t", k=4)[:, :, 0:r], ACT.Copy)\
                           .then_inc(xhi_done, 1)

                def w_hi(c, ks=range(KT)):
                    n = W_N[c]
                    if ks[0] == 0:
                        act.wait_ge(w_loaded[c % 2], 16 * (c // 2 + 1))
                        if c >= 2:
                            act.wait_ge(z_done, BLOCK_END[c - 2])
                    for k in ks:
                        act.activation(wh[:, c % 2, k, 0:n], wraw[:, c % 2, k, 0:n], ACT.Copy, scale=nw[:, k:k + 1])\
                           .then_inc(whi_done, 1)

                act.preload_act_table_set("natural_log_exp_and_others")
                x_sumsq(0)
                act.wait_ge(nw_in, 16)
                w_hi(0, range(2))
                x_hi(0)
                w_hi(0, range(2, KT))
                x_sumsq(1)

                def first(s):
                    k = kind(s)
                    if k not in ACTIVE:
                        return
                    r = rows_of(natural[s][1])
                    u = use_of[("n", *natural[s])]
                    act.wait_ge(z_done, u + 1)
                    n = count(ACTIVE, s)
                    if n > 2:
                        act.wait_ge(nat_done, last_active(s, 2) + 1)
                    if k in ("q", "k"):
                        act.activation(sq[0:r, n % 2, :], z_at(u)[0:r, 0:CB], ACT.Square).then_inc(sq_done, 1)
                    else:
                        to = sq[0:r, n % 2, :]
                        linked(act.activation(to, z_at(u)[0:r, 0:CB], ACT.Exp, scale=-1.0))
                        linked(act.activation(to, to, ACT.Ln, bias=1.0))
                        act.activation(to, to, ACT.Exp, scale=-1.0).then_inc(sq_done, 1)

                def second(s):
                    if kind(s) not in ("q", "k"):
                        return
                    r = rows_of(natural[s][1])
                    act.wait_ge(ms_done, s + 1)
                    linked(act.activation(rms[0:r, s % 2, 1, :], rms[0:r, s % 2, 0, :], ACT.Ln))
                    act.activation(rms[0:r, s % 2, 2, :], rms[0:r, s % 2, 1, :], ACT.Exp, scale=-0.5)\
                       .then_inc(r_done, 1)

                def third(s):
                    if kind(s) not in ("q", "k"):
                        return
                    c, i = natural[s]
                    r = rows_of(i)
                    to = qT if kind(s) == "q" else kT
                    act.wait_ge(nt_done, s + 1)
                    act.activation(to[:, 2 * (c % 2):2 * (c % 2) + 2, P * i:P * i + r],
                                   pn[:, s % 2, 0:2 * P].rearrange("p (h t) -> p h t", h=2)[:, :, 0:r],
                                   ACT.Copy).then_inc(nt_out, 1)

                def last_active(s, back):
                    t = s
                    while back:
                        t -= 1
                        if kind(t) in ACTIVE:
                            back -= 1
                    return t

                def turn_out(c):
                    to, sc = (gqT, DK ** -0.5) if KINDS[c] == "gq" else (gkT, 1.0)
                    for m in range(2):
                        for n, (t0, tn) in enumerate(CH):
                            u = use_of[("t", c, m, n)]
                            act.wait_ge(z_done, u + 1)
                            act.activation(to[:, m, t0:t0 + tn], z_at(u)[:, 0:tn], ACT.Copy, scale=sc)\
                               .then_inc(turned_out, 1)

                def logs(i):
                    r = rows_of(i)
                    u = use_of[("l", i)]
                    act.wait_ge(z_done, u + 1)
                    if i >= 2:
                        act.wait_ge(cum_done, i - 1)
                    linked(act.activation(lgm[0:r, i % 2, :], z_at(u)[0:r, 0:CB], ACT.Abs))
                    linked(act.activation(lg[0:r, i % 2, :], lgm[0:r, i % 2, :], ACT.Exp, scale=-1.0))
                    act.activation(lgm[0:r, i % 2, :], lg[0:r, i % 2, :], ACT.Ln, bias=1.0).then_inc(lnexp_done, 1)

                def sums_out(i):
                    r = rows_of(i)
                    act.wait_ge(cum_done, i + 1)
                    act.activation(bT[:, :, P * i:P * i + r],
                                   pt[:, i % 2, 0:2 * r].rearrange("p (m t) -> p m t", m=2), ACT.Copy)\
                       .then_inc(cum_out, 1)

                for s in range(NN + 3):
                    if s < NN:
                        c, i = natural[s]
                        if i == 0 and c == LOGS:
                            w_hi(GA - 1)
                            turn_out(GA - 2)
                            w_hi(GA)
                            turn_out(GA - 1)
                            w_hi(LOGS)
                            act.wait_ge(ga_done, 1)
                            for n, (t0, tn) in enumerate(CH):
                                u = use_of[("a", GA, n)]
                                act.wait_ge(z_done, u + 1)
                                for part in range(2):
                                    to, of = 32 * part, 64 * (n % 2) + 32 * part
                                    ins = act.activation(gaT[to:to + 16, t0:t0 + tn], z_at(u)[of:of + 16, 0:tn],
                                                         ACT.Copy)
                                ins.then_inc(turned_out, 1)
                        if c == 0:
                            if i + 2 < TILES:
                                x_sumsq(i + 2)
                            if i + 1 < TILES:
                                x_hi(i + 1)
                        if c == 0 and i == 2:
                            act.wait_ge(lam_sum, 1)
                            act.activation(lam[:, 2:4], lam[:, 0:2], ACT.Exp).then_inc(lam_exp, 1)
                        first(s)
                        if i < KT and c + 1 < len(KINDS):
                            w_hi(c + 1, range(i, i + 1))
                        if c == LOGS:
                            if i >= 1:
                                logs(i - 1)
                            if i >= 2:
                                sums_out(i - 2)
                        if c == LOGS + 1 and i == 0:
                            logs(TILES - 1)
                            sums_out(TILES - 2)
                        if c == LOGS + 1 and i == 1:
                            sums_out(TILES - 1)
                    if 1 <= s <= NN:
                        second(s - 1)
                    if s >= 3:
                        third(s - 3)

            @block.tensor
            def _(pe):
                def x_turn(i):
                    r = rows_of(i)
                    pe.wait_ge(hn_done, i + 1)
                    for half in range(2):
                        if i >= 1:
                            pe.wait_ge(xhi_done, 2 * (i - 1) + half + 1)
                            pe.wait_ge(xlo_done, 2 * (i - 1) + half + 1)
                        for k in range(4):
                            kk = 4 * half + k
                            ins = pe.transpose(pt[:, half, k * P:k * P + r], xb[0:r, i % 2, kk * P:(kk + 1) * P],
                                               ident[0:r, 0:r])
                        ins.then_inc(xt_done, 1)

                def z_nat(c, i):
                    u = use_of[("n", c, i)]
                    r = rows_of(i)
                    wait_z(pe, u)
                    n = 0
                    for k in range(KT):
                        if i == 0:
                            pe.wait_ge(whi_done, KT * c + k + 1)
                            pe.wait_ge(wlo_done, KT * c + k + 1)
                        for a, b in ((xTh, wh), (xTl, wh), (xTh, wl)):
                            ins = pe.matmul(z_at(u)[0:r, 0:CB], a[:, k, P * i:P * i + r], b[:, c % 2, k, :],
                                            start=(n == 0), stop=(n == 3 * KT - 1))
                            n += 1
                    ins.then_inc(z_done, 1)

                def z_turned(u, c, m0, mn, t0, tn):
                    wait_z(pe, u)
                    n = 0
                    for k in range(KT):
                        pe.wait_ge(whi_done, KT * c + k + 1)
                        pe.wait_ge(wlo_done, KT * c + k + 1)
                        for a, b in ((xTh, wh), (xTl, wh), (xTh, wl)):
                            ins = pe.matmul(z_at(u)[0:mn, 0:tn], b[:, c % 2, k, m0:m0 + mn], a[:, k, t0:t0 + tn],
                                            start=(n == 0), stop=(n == 3 * KT - 1))
                            n += 1
                    ins.then_inc(z_done, 1)

                def nat_turn(s):
                    if kind(s) not in ("q", "k"):
                        return
                    r = rows_of(natural[s][1])
                    pe.wait_ge(nat_done, s + 1)
                    if s >= 2:
                        pe.wait_ge(nt_out, s - 1)
                    for h in range(2):
                        ins = pe.transpose(pn[:, s % 2, h * P:h * P + r], nat[0:r, s % 3, h * P:(h + 1) * P],
                                           ident[0:r, 0:r])
                    ins.then_inc(nt_done, 1)

                def logits(i):
                    r = rows_of(i)
                    u = use_of[("l", i)]
                    wait_z(pe, u)
                    if i == 0:
                        pe.wait_ge(turned_out, len(turned_uses))
                        pe.wait_ge(consts_in, 16 * 11)
                    pe.matmul(z_at(u)[0:r, 0:CB], gaT[:, P * i:P * i + r], wa2[:], start=True, stop=True)\
                      .then_inc(z_done, 1)

                def running_sum(i):
                    r = rows_of(i)
                    pe.wait_ge(lg_done, i + 1)
                    if i >= 2:
                        pe.wait_ge(cum_out, i - 1)
                    for m in range(2):
                        ins = pe.matmul(pt[:, i % 2, m * r:(m + 1) * r], lg[0:r, i % 2, m * P:(m + 1) * P],
                                        cum[:, :] if r == P else cum8[:, :], start=True, stop=True)
                    ins.then_inc(cum_done, 1)

                pe.wait_ge(ident_in, 16)
                x_turn(0)
                s = 0
                for c, k in enumerate(KINDS):
                    if k in ("gq", "gk"):
                        for m in range(2):
                            for n, (t0, tn) in enumerate(CH):
                                z_turned(use_of[("t", c, m, n)], c, m * P, P, t0, tn)
                        continue
                    if k == "ga":
                        for n in range(3):
                            wait_z(pe, use_of[("a", c, n)])
                        pe.wait_ge(wlo_done, KT * (c + 1))
                        for k in range(KT):
                            for n, (t0, tn) in enumerate(CH):
                                for part, a in enumerate((xTh, xTl)):
                                    at = 64 * (n % 2) + 32 * part
                                    ins = pe.matmul(z_at(use_of[("a", c, n)])[at:at + 16, 0:tn],
                                                    wraw[:, c % 2, k, 0:16], a[:, k, t0:t0 + tn].bitcast(F32),
                                                    start=(k == 0), stop=(k == KT - 1), tile_position=(0, at))
                                if k == KT - 1:
                                    ins.then_inc(z_done, 1)
                        continue
                    for i in range(TILES):
                        if c == 0:
                            if i + 1 < TILES:
                                x_turn(i + 1)
                            pe.wait_ge(xhi_done, 2 * i + 2)
                            pe.wait_ge(xlo_done, 2 * i + 2)
                        z_nat(c, i)
                        if c == LOGS:
                            logits(i)
                            if i >= 2:
                                running_sum(i - 2)
                        if c == LOGS + 1 and i < 2:
                            running_sum(TILES - 2 + i)
                        if s >= 2:
                            nat_turn(s - 2)
                        s += 1

            @block.vector
            def _(dve):
                link = [0]

                def linked(ins):
                    link[0] += 1
                    ins.then_inc(dchain, 1)
                    dve.wait_ge(dchain, link[0])

                dve.memset(gaT[:], 1.0)
                dve.memset(wa2[:], 0.0).then_inc(ga_done, 1)

                def x_norm(i):
                    r = rows_of(i)
                    dve.wait_ge(sumsq_done, i + 1)
                    dve.tensor_scalar(ss[0:r, 1, i:i + 1], ss[0:r, 0, i:i + 1], 1.0 / D, EPS, ALU.mult, ALU.add)\
                       .then_inc(meansq_done, 1)
                    dve.wait_ge(rstd_done, i + 1)
                    dve.tensor_scalar(xb[0:r, i % 2, :], xb[0:r, i % 2, :], ss[0:r, 3, i:i + 1], None, ALU.mult)\
                       .then_inc(hn_done, 1)

                def x_lo(i):
                    r = rows_of(i)
                    for half in range(2):
                        dve.wait_ge(xhi_done, 2 * i + half + 1)
                        to = slice(4 * half, 4 * half + 4), slice(P * i, P * i + r)
                        dve.tensor_tensor(xTl[:, to[0], to[1]],
                                          pt[:, half, :].rearrange("p (k t) -> p k t", k=4)[:, :, 0:r],
                                          xTh[:, to[0], to[1]].bitcast(F32), ALU.subtract).then_inc(xlo_done, 1)

                def w_lo(c, ks=range(KT)):
                    n = W_N[c]
                    for k in ks:
                        dve.wait_ge(whi_done, KT * c + k + 1)
                        if c == GA:
                            w = wraw[:, c % 2, k, 0:n]
                            dve.tensor_scalar(w, w, nw[:, k:k + 1], None, ALU.mult).then_inc(wlo_done, 1)
                            continue
                        dve.scalar_tensor_tensor(out=wl[:, c % 2, k, 0:n], in0=wraw[:, c % 2, k, 0:n],
                                                 scalar=nw[:, k:k + 1], in1=wh[:, c % 2, k, 0:n].bitcast(F32),
                                                 op0=ALU.mult, op1=ALU.subtract).then_inc(wlo_done, 1)

                x_norm(0)
                w_lo(0, range(2))
                x_lo(0)
                w_lo(0, range(2, KT))
                x_norm(1)
                dve.wait_ge(consts_in, 16 * 11)
                linked(dve.tensor_tensor(lmv[:, 2, :], lmv[:, 0, :], lmv[:, 1, :], ALU.mult))
                dve.tensor_reduce(lam[:, 0:2], lmv[:, 2, :].rearrange("p (m d) -> p m d", m=2), AX.X, ALU.add)\
                   .then_inc(lam_sum, 1)
                linked(dve.tensor_scalar(qwr[:, 0, :], qwr[:, 0, :], DK ** -0.5, None, ALU.mult))

                def reduce_sq(s):
                    if kind(s) not in ("q", "k"):
                        return
                    r = rows_of(natural[s][1])
                    n = count(ACTIVE, s)
                    dve.wait_ge(sq_done, n)
                    linked(dve.tensor_reduce(rms[0:r, s % 2, 0, :],
                                             sq[0:r, n % 2, :].rearrange("p (g d) -> p g d", g=4),
                                             AX.X, ALU.add))
                    dve.tensor_scalar(rms[0:r, s % 2, 0, :], rms[0:r, s % 2, 0, :], 1.0 / DK, EPS,
                                      ALU.mult, ALU.add).then_inc(ms_done, 1)

                def finish(s):
                    c, i = natural[s]
                    r = rows_of(i)
                    k = kind(s)
                    n = count(ACTIVE, s)
                    u = use_of[("n", c, i)]
                    z = z_at(u)[0:r, 0:CB]
                    to = nat[0:r, s % 3, :]
                    if s >= 3:
                        if stored_upto(s - 3, s % 3):
                            dve.wait_ge(nat_stored[s % 3], 16 * stored_upto(s - 3, s % 3))
                        if kind(s - 3) in ("q", "k"):
                            dve.wait_ge(nt_done, s - 2)
                    if k in ("q", "k"):
                        dve.wait_ge(r_done, s + 1)
                        g4 = lambda a: a.rearrange("p (g d) -> p g d", g=4)
                        linked(dve.tensor_tensor(g4(nrm[0:r, :]), g4(z),
                                                 rms[0:r, s % 2, 2, :].unsqueeze(2).to_broadcast([r, 4, DK]),
                                                 ALU.mult))
                        dve.tensor_tensor(to, nrm[0:r, :], qwr[0:r, 0 if k == "q" else 1, :], ALU.mult)\
                           .then_inc(nat_done, 1)
                        dve.wait_ge(nat_done, s + 1)
                    elif k in ("dg", "gg"):
                        dve.wait_ge(sq_done, n)
                        dve.tensor_tensor(to, z, sq[0:r, n % 2, :], ALU.mult).then_inc(nat_done, 1)
                        dve.wait_ge(nat_done, s + 1)
                    else:
                        dve.wait_ge(z_done, u + 1)
                        dve.tensor_copy(to, z).then_inc(nat_done, 1)
                        dve.wait_ge(nat_done, s + 1)

                def log_decay(i):
                    r = rows_of(i)
                    u = use_of[("l", i)]
                    dve.wait_ge(lnexp_done, i + 1)
                    dve.scalar_tensor_tensor(out=lg[0:r, i % 2, :], in0=z_at(u)[0:r, 0:CB], scalar=0.0,
                                             in1=lgm[0:r, i % 2, :], op0=ALU.min, op1=ALU.subtract)\
                       .then_inc(lg_done, 1)
                    dve.wait_ge(lg_done, i + 1)

                for s in range(NN + 1):
                    if s < NN:
                        c, i = natural[s]
                        if i == 0 and c == LOGS:
                            finish(s - 1)
                            for b in (GA - 1, GA, LOGS):
                                w_lo(b)
                        if c == 0:
                            if i + 2 < TILES:
                                x_norm(i + 2)
                            if i + 1 < TILES:
                                x_lo(i + 1)
                        reduce_sq(s)
                        if s == TILES:
                            dve.wait_ge(lam_exp, 1)
                            linked(dve.tensor_tensor(lam[:, 4:5], lam[:, 3:4], lam[:, 2:3], ALU.subtract))
                            dve.tensor_scalar(nlam, lam[:, 4:5], -LAM_INIT, None, ALU.add)
                        if c == LOGS and i > 0:
                            finish(s - 1)
                        if i < KT and c + 1 < len(KINDS):
                            w_lo(c + 1, range(i, i + 1))
                    if s >= 1 and not (s < NN and c == LOGS):
                        finish(s - 1)
                    if s < NN and c == LOGS and i >= 1:
                        log_decay(i - 1)
                    if s < NN and (c, i) == (LOGS + 1, 0):
                        log_decay(TILES - 1)

        with ExitStack() as st:
            KR, VR = 4, 8
            R = 2 * H * TS
            kraw = sb(st, "kraw", [P, KR, GRP, W])
            vraw = sb(st, "vraw", [P, VR, GRP, W])
            kt = sb(st, "kt", [P, 2, H, GRP * PAGE])
            sc = sb(st, "sc", [P, G + 1, PAGE])
            pr = sb(st, "pr", [P, 2, PAGE])
            pT = sb(st, "pT", [P, 2, P])
            qq = sb(st, "qq", [P, 160])
            kn = sb(st, "kn", [P, H, NS])
            vn = sb(st, "vn", [P, W])
            relb = sb(st, "relb", [32, H])
            rowq = sb(st, "rowq", [32, TS, 32])
            relq = sb(st, "relq", [32, TS, 32])
            staged = vraw[0:32, VR - 2:VR].rearrange("k a n x -> k (a n x)")
            oh, negp = staged[:, 0:384], staged[0:H, 512:896]
            hotp = staged[:, 1024:1024 + TS * PAGE].rearrange("k (q j) -> k q j", q=TS)
            hotn = staged[:, 2048:2048 + TS * NB * NS].rearrange("k (q j) -> k q j", q=TS)
            dlast = sb(st, "dlast", [P, PAGE])
            dnew = sb(st, "dnew", [32, NB * NS])
            band = sb(st, "band", [H, 384])
            selT = sb(st, "selT", [P, NB, H, NS])
            selc = sb(st, "selc", [P, H, P])
            m01 = sb(st, "m01", [R, 2])
            mx = sb(st, "mx", [P, G + 1])
            lsum = sb(st, "lsum", [P, G + 1])
            stat = sb(st, "stat", [P, 8])
            by_page = sb(st, "by_page", [R, GRP])
            osb = sb(st, "osb", [P, W])
            pk = [ps(st, f"pk{n}", [P, 512]) for n in range(H)]
            psc = [ps(st, f"psc{n}", [P, 512]) for n in range(2)]
            ppt = ps(st, "ppt", [P, 512])
            po = ps(st, "po", [P, 512])
            pod = ppt
            negmax, coef, partial = stat[:, 0:1], stat[:, 1:2], stat[:, 2:3]
            row_stat, sign_lam = stat[0:R, 3:4], stat[0:R, 4:5]
            c_in = sem("c_in")
            k_in = [sem(f"k_in{n}") for n in range(KR)]
            v_in = [sem(f"v_in{n}") for n in range(VR)]
            setup = sem("setup_c")
            relq_done = sem("relq_done")
            rel_done = sem("rel_done")
            band_out = sem("band_out")
            kt_done = sem("kt_done")
            kt_act = sem("kt_act")
            kt_dve = sem("kt_dve")
            sc_done = sem("sc_done")
            sc_out = sem("sc_out")
            max_done = sem("max_done")
            negmax_done = sem("negmax_done")
            exp_done = sem("exp_done")
            pt_done = sem("pt_done")
            pt_out = sem("pt_out")
            pv_done = sem("pv_done")
            o_out = sem("o_out")
            qq_done = sem("qq_done")
            sel_done = sem("sel_done")
            od_done = sem("od_done")
            od_added = sem("od_added")
            bias_done = sem("bias_done")
            dch = sem("dchain_c")
            NCONST = 10

            block = st.enter_context(nc.Block())

            @block.sync
            def _(sp):
                def load_keys(kb, peeled):
                    for g in range(G):
                        if not (peeled and g < KR):
                            sp.wait_ge(kt_done, kb * (4 * G) + 4 * (g - KR + 1))
                        for n in range(GRP):
                            page = sp.value_load(pages[0:1, bass.ds(kb * NPAGES + GRP * g + n, 1)],
                                                 min_val=0, max_val=POOL - 1)
                            sp.dma_start(kraw[:, g % KR, n, :],
                                         cache_k.rearrange("a n p h d -> (a n) p (h d)")[bass.ds(page, 1)]
                                         .rearrange("o p c -> (o p) c")).then_inc(k_in[g % KR], 16)

                load_keys(0, True)
                with sp.Fori(1, NB) as kb:
                    load_keys(kb, False)
                sp.wait_ge(band_out, 1)
                for h in range(H):
                    sp.dma_start(skew[h:h + 1].rearrange("o (q x) -> o q x", q=P),
                                 band[h:h + 1, :].unsqueeze(1).to_broadcast([1, P, 384])).then_inc(c_in, 16)
                sp.wait_ge(c_in, 16 * (NCONST + H))
                for n in range(3):
                    sp.wait_ge(nat_stored[n], all_stored[n])

            @block.gpsimd
            def _(pool):
                def load_values(b, peeled):
                    for g in range(G):
                        if not (peeled and g < VR):
                            pool.wait_ge(pv_done, b * (G + 1) + (g - VR + 1 if g >= VR else g - VR))
                        if peeled and g == VR - 2:
                            pool.wait_ge(band_out, 1)
                        for n in range(GRP):
                            page = pool.value_load(pages[0:1, bass.ds(b * NPAGES + GRP * g + n, 1)],
                                                   min_val=0, max_val=POOL - 1)
                            pool.dma_start(vraw[:, g % VR, n, :],
                                           cache_v.rearrange("a n p h d -> (a n) p (h d)")[bass.ds(page, 1)]
                                           .rearrange("o p c -> (o p) c")).then_inc(v_in[g % VR], 16)

                load_values(0, True)
                with pool.Fori(1, NB) as b:
                    load_values(b, False)

            def first(b):
                return isinstance(b, int) and b == 0

            def copy_keys(eng, copied, kb, g, h):
                eng.wait_ge(kt_done, kb * (4 * G) + 4 * g + h + 1)
                if not (first(kb) and g < 2):
                    eng.wait_ge(sc_done, kb * (G + 1) + (g - 1 if g >= 2 else g - 2))
                if eng is nc.scalar:
                    ins = eng.activation(kt[:, g % 2, h, :], pk[h][:], ACT.Copy)
                else:
                    ins = eng.tensor_copy(kt[:, g % 2, h, :], pk[h][:])
                ins.then_inc(copied, 1)

            @block.scalar
            def _(act):
                def scores_out(kb, g):
                    act.wait_ge(sc_done, kb * (G + 1) + g + 1)
                    if g < G:
                        act.activation(sc[:, g, :], psc[g % 2][:, 0:PAGE], ACT.Copy).then_inc(sc_out, 1)
                    else:
                        act.activation(sc[0:R, g, 0:NS], psc[g % 2][0:R, 0:NS], ACT.Copy).then_inc(sc_out, 1)

                def expo(b, g):
                    if g == 0:
                        act.wait_ge(negmax_done, b + 1)
                    if not (first(b) and g < 2):
                        act.wait_ge(pt_done, b * (G + 1) + max(g - 1, 0))
                    rows, n = (R, NS) if g == G else (P, PAGE)
                    act.activation(pr[0:rows, g % 2, 0:n], sc[0:rows, g, 0:n], ACT.Exp, bias=negmax[0:rows],
                                   accum_out=lsum[0:rows, g:g + 1]).then_inc(exp_done, 1)

                def row(kb, b):
                    for g in range(G):
                        if b is not None:
                            expo(b, g)
                        if kb is not None:
                            if g >= 1:
                                scores_out(kb, g - 1)
                            copy_keys(act, kt_act, kb, g, 0)
                            copy_keys(act, kt_act, kb, g, 1)
                    if b is not None:
                        expo(b, G)
                    if kb is not None:
                        scores_out(kb, G - 1)
                        scores_out(kb, G)
                    if b is not None:
                        act.wait_ge(pv_done, b * (G + 1) + G + 1)
                        if not first(b):
                            act.wait_ge(od_done, b + 0)
                        act.activation(osb[:], po[:, :], ACT.Copy).then_inc(o_out, 1)

                act.dma_start(vn[0:NS, :], v_sample.rearrange("a b t h d -> (a b t) (h d)")).then_inc(c_in, 16)
                for to, of in ((relb[:], rel_bias), (rowq[:], c_rowq), (hotp, c_hotp.rearrange("k (q j) -> k q j", q=TS)),
                               (hotn, c_hotn), (dnew[:], c_negn), (oh, c_oh), (negp, c_negp), (selT[:], c_selT),
                               (m01[:], c_m01)):
                    act.dma_start(to, of).then_inc(c_in, 16)

                row(0, None)
                row(1, 0)
                with act.Fori(1, NB - 1) as b:
                    row(b + 1, b)
                row(None, NB - 1)

            @block.tensor
            def _(pe):
                def turn_keys(kb, g, h):
                    if h == 0:
                        pe.wait_ge(k_in[g % KR], kb * 128 + 64 * (g // KR + 1))
                    if not (first(kb) and g == 0):
                        pe.wait_ge(kt_act if h < 2 else kt_dve, kb * (2 * G) + 2 * (g - 1) + h % 2 + 1)
                    for n in range(GRP):
                        ins = pe.transpose(pk[h][:, n * PAGE:(n + 1) * PAGE],
                                           kraw[:, g % KR, n, h * P:(h + 1) * P], ident[:])
                    ins.then_inc(kt_done, 1)

                def scores(kb, g):
                    if g == 0:
                        pe.wait_ge(qq_done, 2 * (kb + 1))
                    if g >= 2:
                        pe.wait_ge(sc_out, kb * (G + 1) + g - 1)
                    elif not first(kb):
                        pe.wait_ge(sc_out, kb * (G + 1))
                    for h in range(H):
                        pe.wait_ge(kt_act if h < 2 else kt_dve, kb * (2 * G) + 2 * g + h % 2 + 1)
                        for n in range(GRP):
                            ins = pe.matmul(psc[g % 2][R * n:R * (n + 1), 0:PAGE], qq[:, 32 * h:32 * h + R],
                                            kt[:, g % 2, h, n * PAGE:(n + 1) * PAGE], start=(h == 0),
                                            stop=(h == H - 1), tile_position=(0, R * n))
                    ins.then_inc(sc_done, 1)

                def new_scores(kb):
                    pe.wait_ge(sc_out, kb * (G + 1) + G - 1)
                    for h in range(H):
                        ins = pe.matmul(psc[G % 2][0:R, 0:NS], qq[:, 32 * h:32 * h + R], kn[:, h, :],
                                        start=(h == 0), stop=(h == H - 1))
                    ins.then_inc(sc_done, 1)

                def turn_probs(b, g):
                    pe.wait_ge(exp_done, b * (G + 1) + g + 1)
                    if not (first(b) and g == 0):
                        pe.wait_ge(pt_out, b * (G + 1) + g)
                        if g == 0:
                            pe.wait_ge(od_added, b + 0)
                    pe.transpose(ppt[:, 0:P], pr[:, g % 2, :], ident[:]).then_inc(pt_done, 1)

                def values(b, g):
                    pe.wait_ge(pt_out, b * (G + 1) + g + 1)
                    if g < G:
                        pe.wait_ge(v_in[g % VR], b * (64 * G // VR) + 64 * (g // VR + 1))
                    if g == 0 and not first(b):
                        pe.wait_ge(o_out, b + 0)
                    if g < G:
                        for n in range(GRP):
                            ins = pe.matmul(po[R * n:R * (n + 1), :], pT[:, g % 2, R * n:R * (n + 1)],
                                            vraw[:, g % VR, n, :], start=(g == 0), stop=(n > 0 and g == G - 1),
                                            tile_position=(0, R * n))
                    else:
                        ins = pe.matmul(po[0:R, :], pT[:, g % 2, 0:R], vn[:], start=False, stop=True)
                    ins.then_inc(pv_done, 1)

                def row(kb, b):
                    for g in range(G):
                        if kb is not None:
                            for h in range(H):
                                turn_keys(kb, g, h)
                        if b is not None:
                            turn_probs(b, g)
                            if g >= 1:
                                values(b, g - 1)
                        if kb is not None:
                            scores(kb, g)
                        if b is None and g == 2:
                            biases()
                    if b is not None:
                        turn_probs(b, G)
                        values(b, G - 1)
                    if kb is not None:
                        new_scores(kb)
                    if b is not None:
                        values(b, G)
                        pe.wait_ge(o_out, b + 1)
                        pe.wait_ge(sel_done, b + 1)
                        for h in range(H):
                            ins = pe.matmul(pod[:, h * DV:(h + 1) * DV], selc[:, h, :], osb[:, h * DV:(h + 1) * DV],
                                            start=True, stop=True)
                        ins.then_inc(od_done, 1)

                def biases():
                    pe.wait_ge(relq_done, 1)
                    for q in range(TS):
                        pe.matmul(po[0:32, 0:PAGE], relq[:, q, :], hotp[:, q, :], start=(q == 0), stop=(q == TS - 1))
                    for q in range(TS):
                        pe.matmul(po[0:32, PAGE:PAGE + NB * NS], relq[:, q, :], hotn[:, q, :], start=(q == 0),
                                  stop=(q == TS - 1))
                    pe.matmul(ppt[0:H, 0:384], relb[:], oh, start=True, stop=True).then_inc(rel_done, 1)

                row(0, None)
                pe.wait_ge(band_out, 1)
                row(1, 0)
                with pe.Fori(1, NB - 1) as b:
                    row(b + 1, b)
                row(None, NB - 1)

            @block.vector
            def _(dve):
                def bias_inputs():
                    dve.wait_ge(c_in, 16 * NCONST)
                    dve.tensor_tensor(
                        relq[:].rearrange("k q (h x) -> k q h x", h=H),
                        rowq[:].rearrange("k q (h x) -> k q h x", h=H),
                        relb[:].unsqueeze(1).unsqueeze(3).to_broadcast([32, TS, H, 8]), ALU.mult).then_inc(relq_done, 1)
                    dve.scalar_tensor_tensor(out=sign_lam, in0=m01[:, 1:2], scalar=nlam[0:R], in1=m01[:, 0:1],
                                             op0=ALU.mult, op1=ALU.add)

                def biases_out():
                    dve.wait_ge(rel_done, 1)
                    dve.tensor_copy(dlast[P - R:P, :], po[0:R, 0:PAGE])
                    dve.tensor_tensor(dnew[:], dnew[:], po[0:32, PAGE:PAGE + NB * NS], ALU.add)
                    dve.tensor_tensor(band[:], negp, ppt[0:H, 0:384], ALU.add).then_inc(band_out, 1)
                    dve.wait_ge(band_out, 1)

                dve.memset(qq[:], 0.0)
                dve.memset(mx[:], NEG)
                dve.memset(lsum[:], 0.0)
                new = slice(P * (TILES - 1) + S0, P * (TILES - 1) + S0 + NS)
                dve.tensor_copy(kn[:], kT[:, :, new])
                dve.memset(od_s[:], 0.0)
                dve.memset(selc[:], 0.0)
                dve.memset(vn[NS:2 * NS, :], 0.0)
                dve.memset(vn[2 * NS:P, :], 0.0).then_inc(setup, 1)
                dve.wait_ge(setup, 1)
                LINKS = 9
                at = [0]

                def rowlinked(ins, b):
                    at[0] += 1
                    ins.then_inc(dch, 1)
                    dve.wait_ge(dch, b * LINKS + at[0])

                def queries(kb):
                    if not first(kb):
                        dve.wait_ge(sc_done, kb * (G + 1))
                    for m in range(2):
                        half = slice(DK * m, DK * m + DK)
                        of = qT[half, :, bass.ds(kb * TS + P * (TILES - 1) + S0, TS)]
                        dve.tensor_copy(qq[half, :].rearrange("p (h x) -> p h x", h=H)[:, :, TS * m:TS * m + TS], of)\
                           .then_inc(qq_done, 1)

                def group_max(kb, g):
                    dve.wait_ge(sc_out, kb * (G + 1) + g + 1)
                    rows, n = (R, NS) if g == G else (P, PAGE)
                    if g == G - 1:
                        last = sc[P - R:P, g, :]
                        dve.tensor_tensor(last, last, dlast[P - R:P, :], ALU.add).then_inc(bias_done, 1)
                        dve.wait_ge(bias_done, 2 * kb + 1)
                    if g == G:
                        new = sc[0:R, g, 0:NS]
                        dve.tensor_tensor(new, new, dnew[:, bass.ds(kb * NS, NS)], ALU.add).then_inc(bias_done, 1)
                        dve.wait_ge(bias_done, 2 * kb + 2)
                    dve.tensor_reduce(mx[0:rows, g:g + 1], sc[0:rows, g, 0:n], AX.X, ALU.max).then_inc(max_done, 1)

                def over_pages(of, op, b, negate=False):
                    rowlinked(dve.tensor_reduce(partial, of, AX.X, op), b)
                    for n in range(GRP):
                        ins = dve.tensor_copy(by_page[:, n:n + 1], partial[R * n:R * (n + 1)])
                    rowlinked(ins, b)
                    rowlinked(dve.tensor_reduce(row_stat, by_page[:], AX.X, op, negate=negate), b)

                def row_max(b):
                    at[0] = 0
                    dve.wait_ge(max_done, b * (G + 1) + G + 1)
                    over_pages(mx[:], ALU.max, b, negate=True)
                    for n in range(GRP):
                        ins = dve.tensor_copy(negmax[R * n:R * (n + 1)], row_stat)
                    ins.then_inc(negmax_done, 1)
                    dve.wait_ge(negmax_done, b + 1)

                def coefficients(b):
                    dve.wait_ge(exp_done, b * (G + 1) + G + 1)
                    over_pages(lsum[:], ALU.add, b)
                    rowlinked(dve.reciprocal(row_stat, row_stat), b)
                    rowlinked(dve.tensor_tensor(row_stat, row_stat, sign_lam, ALU.mult), b)
                    for n in range(GRP):
                        ins = dve.tensor_copy(coef[R * n:R * (n + 1)], row_stat)
                    rowlinked(ins, b)
                    if not first(b):
                        dve.wait_ge(od_done, b + 0)
                    dve.tensor_scalar(selc[:, :, 0:NS], selT[:, bass.ds(b, 1), :, :].rearrange("p o h t -> p (o h) t"),
                                      coef, None, ALU.mult).then_inc(sel_done, 1)
                    assert at[0] == LINKS

                def turned_probs(b, g):
                    dve.wait_ge(pt_done, b * (G + 1) + g + 1)
                    if not (first(b) and g < 2):
                        dve.wait_ge(pv_done, b * (G + 1) + max(g - 1, 0))
                    dve.tensor_copy(pT[:, g % 2, :], ppt[:, 0:P]).then_inc(pt_out, 1)

                def row(kb, b):
                    if b is not None:
                        row_max(b)
                    if kb is not None:
                        queries(kb)
                    for g in range(G):
                        if kb is not None:
                            copy_keys(dve, kt_dve, kb, g, 2)
                            copy_keys(dve, kt_dve, kb, g, 3)
                        if b is not None:
                            turned_probs(b, g)
                        if kb is not None and g >= 1:
                            group_max(kb, g - 1)
                        if b is None and g == 1:
                            bias_inputs()
                        if b is None and g == 3:
                            biases_out()
                    if kb is not None:
                        group_max(kb, G - 1)
                    if b is not None:
                        turned_probs(b, G)
                        coefficients(b)
                    if kb is not None:
                        group_max(kb, G)
                    if b is not None:
                        dve.wait_ge(od_done, b + 1)
                        dve.tensor_tensor(od_s[:], od_s[:], pod[0:NS, :], ALU.add).then_inc(od_added, 1)
                        dve.wait_ge(od_added, b + 1)

                row(0, None)
                row(1, 0)
                with dve.Fori(1, NB - 1) as b:
                    row(b + 1, b)
                row(None, NB - 1)

        mixT = sb(ctx, "mixT", [P, 2 * H, NTOK])

        with ExitStack() as st:
            vd = sb(st, "vd", [P, TILES, W])
            gd = sb(st, "gd", [P, 2, W])
            dw = sb(st, "dw", [P, DV])
            ks = sb(st, "ks", [P, 2, H, L], F32R)
            qs = sb(st, "qs", [P, 2, 2, 2, H, P], F32R)
            bh = sb(st, "bh", [P, H, 2 * P], F32R)
            bl = sb(st, "bl", [P, H, 2 * P], F32R)
            identr = sb(st, "identr", [P, P], F32R)
            e = sb(st, "e", [P, 2, 2, L])
            pT = sb(st, "pT_b", [P, TILES, P])
            ob = sb(st, "ob", [P, W])
            mix = sb(st, "mix_b", [P, W])
            squares_b = sb(st, "squares_b", [P, W])
            r4 = sb(st, "r4", [P, 3, 4])
            inv = sb(st, "inv", [P, 2, H])
            eps = sb(st, "eps_b", [P, 1])
            sm = sb(st, "sm", [P, 2, 8])
            pS = ps(st, "pS", [P, 6 * 512])
            pT6 = ps(st, "pT6", [P, 512])
            pO = ps(st, "pO", [P, 512])
            turn_banks = [pS[:, 2 * 512:3 * 512], pS[:, 5 * 512:6 * 512], pT6[:, :]]
            b_in = sem("b_in")
            band_in = sem("band_in")
            gd_in = [sem(f"gd_in{n}") for n in range(2)]
            bandhi_done = sem("bandhi_done")
            bandlo_done = sem("bandlo_done")
            dw_scaled = sem("dw_scaled")
            khi_done = sem("b_khi_done")
            klo_done = sem("b_klo_done")
            qhi_done = sem("b_qhi_done")
            qlo0_done = sem("qlo0_done")
            qlo1_done = sem("qlo1_done")
            scores_done = sem("b_scores_done")
            max_done = sem("b_max_done")
            exp_done = sem("b_exp_done")
            probs_done = sem("b_probs_done")
            turned_done = sem("b_turned_done")
            turned_copied = sem("b_turned_copied")
            out_done = sem("b_out_done")
            out_copied = sem("b_out_copied")
            root_done = sem("root_done")
            gate_done = sem("gate_done")
            mix_done = sem("mix_done")
            tail_ready = sem("tail_ready")
            pool_chain = sem("pool_chain_b")
            dch2 = sem("dchain_b")
            ach2 = sem("achain_b")
            units = [(i, h) for i in range(TILES - 1) for h in range(H)] + [(TILES - 1, H - 1)]
            NU = len(units)
            LAST0 = H * (TILES - 1)
            PAIRS = (TILES + 1) // 2

            def rq(i):
                return P if i < TILES - 1 else TAIL

            def tail(u):
                return units[u][0] == TILES - 1

            def begins(u):
                return units[u][1] == 0 or tail(u)

            def mix_after(u):
                i, h = units[u]
                return i - 1 if (h == 1 and i >= 1) or tail(u) else None

            def keys(i):
                return P * i + rq(i)

            def small(u):
                return keys(units[u][0]) <= 512

            def s_at(u, m):
                return 1536 * m + (512 * (u % 2) if small(u) else 0)

            turns, bank_of = [], []
            for u in range(NU + 1):
                if u >= 1:
                    i, h = units[u - 1]
                    new = [("p", u - 1, j0, min(j0 + 4, i + 1)) for j0 in range(0, i + 1, 4)]
                    if mix_after(u - 1) is not None:
                        new.append(("m", mix_after(u - 1)))
                    for x in new:
                        turns.append(x)
                        bank_of.append(len(turns) % 3 if u < LAST0 else 2)
            turns.append(("m", TILES - 1))
            bank_of.append(2)
            turn_no = {x: n for n, x in enumerate(turns)}

            def batches(u):
                return [x for x in turns if x[0] == "p" and x[1] == u]

            def last_batch(u):
                return turn_no[batches(u)[-1]]

            def wait_bank(eng, n):
                before = [m for m in range(n) if bank_of[m] == bank_of[n]]
                if before:
                    eng.wait_ge(turned_copied, before[-1] + 1)

            block = st.enter_context(nc.Block())

            @block.sync
            def _(sp):
                sp.dma_start(dw[:], diff_norm_w.to_broadcast([P, DV])).then_inc(band_in, 16)
                for h in range(H):
                    sp.dma_start(pT[:, 2 * h:2 * h + 2, :].rearrange("p a x -> p (a x)"),
                                 skew[h, P - 1:P - 1 + P * 383].rearrange("(q x) -> q x", x=383)
                                 [:, 0:2 * P]).then_inc(band_in, 16)
                for i in range(TILES):
                    sp.dma_start(vd[0:rows_of(i), i, :], val_d[i, 0:rows_of(i), :]).then_inc(b_in, 16)
                for i in range(TILES):
                    if i >= 2:
                        sp.wait_ge(mix_done, i - 1)
                    sp.dma_start(gd[0:rows_of(i), i % 2, :], gate_d[i, 0:rows_of(i), :]).then_inc(gd_in[i % 2], 16)

            own = [slice(0, DK), slice(DK, P)]

            def copied(eng, to, of):
                return eng.activation(to, of, ACT.Copy) if eng is nc.scalar else eng.tensor_copy(to, of)

            def key_hi(eng, p, m):
                k = slice(2 * P * p, min(2 * P * (p + 1), L))
                return copied(eng, ks[own[m], m, :, k], kT[own[m], :, k])

            def query_hi(eng, i, m, to):
                nq = P if i < TILES - 1 else P // H
                return copied(eng, qs[to, i % 2, m, 0, :, 0:nq], qT[own[m], :, P * i:P * i + nq])

            def key_lo(eng, p, m):
                k = slice(2 * P * p, min(2 * P * (p + 1), L))
                return eng.tensor_tensor(ks[own[1 - m], m, :, k], kT[own[m], :, k],
                                         ks[own[m], m, :, k].bitcast(F32), ALU.subtract)

            def query_lo(eng, i, m, to):
                nq = P if i < TILES - 1 else P // H
                return eng.tensor_tensor(qs[to, i % 2, m, 1, :, 0:nq], qT[own[m], :, P * i:P * i + nq],
                                         qs[own[m], i % 2, m, 0, :, 0:nq].bitcast(F32), ALU.subtract)

            @block.gpsimd
            def _(pool):
                link = [0]

                def linked(ins):
                    link[0] += 1
                    ins.then_inc(pool_chain, 1)
                    pool.wait_ge(pool_chain, link[0])

                def split_lo(i):
                    pool.wait_ge(qhi_done, i + 2)
                    linked(query_lo(pool, i, 0, own[0]))
                    query_lo(pool, i, 0, own[1]).then_inc(qlo0_done, 1)
                    pool.wait_ge(qlo0_done, i + 1)

                split_lo(0)
                pool.wait_ge(dw_scaled, 1)
                for i in range(TILES):
                    if i + 1 < TILES:
                        split_lo(i + 1)
                    r = rows_of(i)
                    pool.wait_ge(gd_in[i % 2], 16 * (i // 2 + 1))
                    g = gd[0:r, i % 2, :].rearrange("p (h d) -> p h d", h=H)
                    pool.tensor_tensor(g, g, dw[0:r, :].unsqueeze(1).to_broadcast([r, H, DV]), ALU.mult)\
                        .then_inc(gate_done, 1)
                    pool.wait_ge(gate_done, i + 1)

            @block.tensor
            def _(pe):
                def scores(u):
                    i, h = units[u]
                    nk = keys(i)
                    if begins(u):
                        pe.wait_ge(khi_done, i // 2 + 2)
                        pe.wait_ge(klo_done, i // 2 + 1)
                        pe.wait_ge(qhi_done, i + 2)
                        pe.wait_ge(qlo0_done, i + 1)
                        pe.wait_ge(qlo1_done, i + 1)
                    if u == LAST0:
                        pe.wait_ge(turned_copied, 1 + max(n for n, b in enumerate(bank_of) if b < 2))
                    w = min(nk, P + rq(i))
                    d0 = P - (w - rq(i))
                    for m in range(2):
                        back = 2 if small(u) else 1
                        if u >= back:
                            pe.wait_ge(exp_done, 2 * (u - back) + m + 1)
                        width = nk if tail(u) else 2 * P * (i // 2 + 1)
                        for k0 in range(0, width, 512):
                            k1 = min(k0 + 512, width)
                            n0, n1 = max(nk - w, k0), min(nk, k1)
                            c = slice(d0 + n0 - (nk - w), d0 + n1 - (nk - w))
                            for hh in range(H) if tail(u) else [h]:
                                rows = slice(32 * hh, 32 * hh + 32) if tail(u) else slice(0, P)
                                nq = rows.stop - rows.start
                                typed = (lambda a: a.bitcast(F32)) if tail(u) else (lambda a: a)
                                at = (0, rows.start)

                                def product(x):
                                    return pe.matmul(pS[rows, s_at(u, m) + k0:s_at(u, m) + k1],
                                                     typed(qs[:, i % 2, m, x, hh, 0:nq]),
                                                     typed(ks[:, m, hh, k0:k1]),
                                                     start=(x == 0), stop=(x == 1), tile_position=at)

                                product(0)
                                if n0 < n1:
                                    for band in (bh, bl):
                                        pe.matmul(pS[rows, s_at(u, m) + n0:s_at(u, m) + n1],
                                                  typed(identr[:, 0:nq]), typed(band[:, hh, c]),
                                                  start=False, stop=False, tile_position=at)
                                ins = product(1)
                        ins.then_inc(scores_done, 1)

                def weigh(u):
                    i, h = units[u]
                    pe.wait_ge(probs_done, u + 1)
                    for b in batches(u):
                        n = turn_no[b]
                        wait_bank(pe, n)
                        for j in range(b[2], b[3]):
                            kn = P if j < i else rq(i)
                            at = (j - b[2]) * P
                            ins = pe.transpose(turn_banks[bank_of[n]][0:kn, at:at + P],
                                               e[:, u % 2, 0, P * j:P * j + kn], ident[:])
                        ins.then_inc(turned_done, 1)
                    if u == 0:
                        pe.wait_ge(b_in, 16 * TILES)
                    if begins(u) and i >= 1:
                        pe.wait_ge(out_copied, i)
                    for b in batches(u):
                        pe.wait_ge(turned_copied, turn_no[b] + 1)
                        for j in range(b[2], b[3]):
                            kn = P if j < i else rq(i)
                            for hh in range(H) if tail(u) else [h]:
                                q = slice(32 * hh, 32 * hh + 32) if tail(u) else slice(0, P)
                                ins = pe.matmul(pO[q, hh * DV:(hh + 1) * DV], pT[0:kn, j, q],
                                                vd[0:kn, j, hh * DV:(hh + 1) * DV], start=(j == 0), stop=(j == i),
                                                tile_position=(0, q.start))
                    ins.then_inc(out_done, 1)

                def turn_mix(i):
                    r = rows_of(i)
                    n = turn_no[("m", i)]
                    pe.wait_ge(mix_done, i + 1)
                    wait_bank(pe, n)
                    for k in range(H):
                        ins = pe.transpose(turn_banks[bank_of[n]][:, k * P:k * P + r], mix[0:r, k * P:(k + 1) * P],
                                           ident[0:r, 0:r])
                    ins.then_inc(turned_done, 1)

                pe.wait_ge(bandhi_done, 2)
                pe.wait_ge(bandlo_done, 1)
                for u in range(NU + 1):
                    if u < NU:
                        scores(u)
                    if u >= 1:
                        weigh(u - 1)
                        if mix_after(u - 1) is not None:
                            turn_mix(mix_after(u - 1))
                turn_mix(TILES - 1)

            @block.scalar
            def _(act):
                link = [0]

                def linked(ins):
                    link[0] += 1
                    ins.then_inc(ach2, 1)
                    act.wait_ge(ach2, link[0])

                def queries_hi(i):
                    if i >= 2:
                        act.wait_ge(scores_done, 2 * H * (i - 1))
                    for m in range(1 if i == 0 else 2):
                        for to in own:
                            ins = query_hi(act, i, m, to)
                    ins.then_inc(qhi_done, 1)

                def keys_hi(p):
                    for m in range(1 if p == 0 else 2):
                        ins = key_hi(act, p, m)
                    ins.then_inc(khi_done, 1)

                def expo(u, m):
                    nk = keys(units[u][0])
                    act.wait_ge(max_done, 2 * u + m + 1)
                    if u >= 2:
                        act.wait_ge(probs_done, u - 1)
                        act.wait_ge(turned_done, last_batch(u - 2) + 1)
                    act.activation(e[:, u % 2, m, 0:nk], pS[:, s_at(u, m):s_at(u, m) + nk], ACT.Exp,
                                   bias=sm[:, u % 2, m:m + 1], accum_out=sm[:, u % 2, 2 + m:3 + m])\
                       .then_inc(exp_done, 1)

                def turned(b):
                    _, u, j0, j1 = b
                    i = units[u][0]
                    n = turn_no[b]
                    bank = turn_banks[bank_of[n]]
                    act.wait_ge(turned_done, n + 1)
                    if u >= 1:
                        act.wait_ge(out_done, u)
                    full = j1 - j0 - (1 if tail(u) and j1 == i + 1 else 0)
                    if full:
                        ins = act.activation(pT[:, j0:j0 + full, :],
                                             bank[:, 0:full * P].rearrange("p (j q) -> p j q", q=P), ACT.Copy)
                    if full < j1 - j0:
                        kn = rq(i)
                        ins = act.activation(pT[0:kn, i, :], bank[0:kn, (i - j0) * P:(i - j0 + 1) * P], ACT.Copy)
                    ins.then_inc(turned_copied, 1)

                def out(i):
                    nq, r = rq(i), rows_of(i)
                    act.wait_ge(out_done, min(H * (i + 1), NU))
                    if i >= 1:
                        act.wait_ge(mix_done, i)
                    if i == TILES - 1:
                        act.wait_ge(tail_ready, 1)
                    for h in range(H):
                        c = slice(h * DV, (h + 1) * DV)
                        if i < TILES - 1:
                            ins = act.activation(ob[:, c], pO[:, c], ACT.Copy, scale=inv[:, i % 2, h:h + 1])
                        else:
                            ins = act.activation(ob[0:nq, c], pO[32 * h:32 * h + nq, c], ACT.Copy)
                    ins.then_inc(out_copied, 1)
                    act.wait_ge(out_copied, i + 1)
                    for h in range(H):
                        c = slice(h * DV, (h + 1) * DV)
                        ins = act.activation(squares_b[0:r, c], ob[0:r, c], ACT.Square, accum_out=r4[0:r, 0, h:h + 1])
                    linked(ins)
                    linked(act.activation(r4[0:r, 1, :], r4[0:r, 0, :], ACT.Ln, scale=1.0 / DV, bias=eps[0:r, :]))
                    act.activation(r4[0:r, 2, :], r4[0:r, 1, :], ACT.Exp, scale=-0.5).then_inc(root_done, 1)

                def mixed(i):
                    r = rows_of(i)
                    n = turn_no[("m", i)]
                    act.wait_ge(turned_done, n + 1)
                    act.activation(mixT[:, 0:H, P * i:P * i + r],
                                   turn_banks[bank_of[n]].rearrange("p (k t) -> p k t", k=H)[:, :, 0:r], ACT.Copy)\
                       .then_inc(turned_copied, 1)

                queries_hi(0)
                keys_hi(0)
                act.activation(identr[:], ident[:], ACT.Copy).then_inc(bandhi_done, 1)
                act.wait_ge(band_in, 16 * (1 + H))
                act.activation(bh[:].rearrange("p h x -> p (h x)"), pT[:, 0:2 * H, :].rearrange("p j x -> p (j x)"),
                               ACT.Copy).then_inc(bandhi_done, 1)
                for u in range(NU + 1):
                    before = batches(u - 1) if u >= 1 else []
                    if before:
                        turned(before[0])
                    if u < NU:
                        expo(u, 0)
                    if len(before) > 1:
                        turned(before[1])
                    if u < NU:
                        expo(u, 1)
                    if len(before) > 2:
                        turned(before[2])
                    if u >= 1:
                        i, h = units[u - 1]
                        if h == H - 1:
                            out(i)
                        if mix_after(u - 1) is not None:
                            mixed(mix_after(u - 1))
                    if u < NU and units[u][1] == 1 and units[u][0] + 1 < TILES:
                        queries_hi(units[u][0] + 1)
                    if u < NU and units[u][1] == 2 and units[u][0] % 2 == 0 and units[u][0] + 2 <= TILES - 1:
                        keys_hi(units[u][0] // 2 + 1)
                mixed(TILES - 1)

            @block.vector
            def _(dve):
                link = [0]

                def linked(ins):
                    link[0] += 1
                    ins.then_inc(dch2, 1)
                    dve.wait_ge(dch2, link[0])

                def maxima(u):
                    nk = keys(units[u][0])
                    for m in range(2):
                        dve.wait_ge(scores_done, 2 * u + m + 1)
                        dve.tensor_reduce(sm[:, u % 2, m:m + 1], pS[:, s_at(u, m):s_at(u, m) + nk], AX.X, ALU.max,
                                          negate=True).then_inc(max_done, 1)

                def combine(u):
                    i, h = units[u]
                    nk = keys(i)
                    s = sm[:, u % 2, :]
                    dve.wait_ge(exp_done, 2 * u + 2)
                    if begins(u) and i >= 2:
                        dve.wait_ge(out_copied, i - 1)
                    dve.reciprocal(inv[:, i % 2, h:h + 1], s[:, 2:3])
                    linked(dve.reciprocal(s[:, 4:5], s[:, 3:4]))
                    linked(dve.scalar_tensor_tensor(out=s[:, 5:6], in0=s[:, 4:5], scalar=nlam, in1=s[:, 2:3],
                                                    op0=ALU.mult, op1=ALU.mult))
                    e0, e1 = e[:, u % 2, 0, 0:nk], e[:, u % 2, 1, 0:nk]
                    ins = dve.scalar_tensor_tensor(out=e0, in0=e1, scalar=s[:, 5:6], in1=e0, op0=ALU.mult, op1=ALU.add)
                    if tail(u):
                        linked(ins)
                        ins = dve.tensor_scalar(e0, e0, inv[:, i % 2, h:h + 1], None, ALU.mult)
                    ins.then_inc(probs_done, 1)

                def norm(i):
                    r = rows_of(i)
                    dve.wait_ge(gate_done, i + 1)
                    dve.wait_ge(root_done, i + 1)
                    if i >= 1:
                        dve.wait_ge(turned_done, turn_no[("m", i - 1)] + 1)
                    for h in range(H):
                        c = slice(h * DV, (h + 1) * DV)
                        ins = dve.scalar_tensor_tensor(out=mix[0:r, c], in0=ob[0:r, c], scalar=r4[0:r, 2, h:h + 1],
                                                       in1=gd[0:r, i % 2, c], op0=ALU.mult, op1=ALU.mult)
                    ins.then_inc(mix_done, 1)

                def queries_lo(i):
                    dve.wait_ge(qhi_done, i + 2)
                    query_lo(dve, i, 1, own[0])
                    query_lo(dve, i, 1, own[1]).then_inc(qlo1_done, 1)

                def keys_lo(p):
                    dve.wait_ge(khi_done, p + 2)
                    key_lo(dve, p, 0)
                    key_lo(dve, p, 1).then_inc(klo_done, 1)

                query_hi(dve, 0, 1, own[0])
                query_hi(dve, 0, 1, own[1]).then_inc(qhi_done, 1)
                key_hi(dve, 0, 1).then_inc(khi_done, 1)
                dve.memset(eps[:], EPS)
                queries_lo(0)
                keys_lo(0)
                dve.wait_ge(band_in, 16 * (1 + H))
                dve.tensor_scalar(dw[:], dw[:], 1.0 - LAM_INIT, None, ALU.mult).then_inc(dw_scaled, 1)
                dve.wait_ge(bandhi_done, 2)
                dve.tensor_tensor(bl[:].rearrange("p h x -> p (h x)"), pT[:, 0:2 * H, :].rearrange("p j x -> p (j x)"),
                                  bh[:].rearrange("p h x -> p (h x)").bitcast(F32), ALU.subtract)\
                   .then_inc(bandlo_done, 1)
                for u in range(NU + 1):
                    if u >= 1:
                        combine(u - 1)
                    if u < NU:
                        maxima(u)
                    if u < NU and units[u][1] == 2 and units[u][0] + 1 < TILES:
                        queries_lo(units[u][0] + 1)
                    if u < NU and units[u][1] == 3 and units[u][0] % 2 == 0 and units[u][0] + 2 <= TILES - 1:
                        keys_lo(units[u][0] // 2 + 1)
                    if u >= 2 and units[u - 2][1] == 3:
                        norm(units[u - 2][0])
                        if units[u - 2][0] == TILES - 2:
                            dve.wait_ge(mix_done, TILES - 1)
                            linked(dve.memset(ob[0:S0, :], 0.0))
                            dve.tensor_copy(ob[S0:S0 + NS, :], od_s[:]).then_inc(tail_ready, 1)
                norm(TILES - 1)
        wo_raw = [a[:].rearrange("p h t -> p (h t)")[:, k * D:(k + 1) * D] for a in (qT, kT) for k in range(KT // 2)]
        wo_in = sem("wo_in")
        sp_ = sb(ctx, "state_p", [P, 2, DV])
        ss_ = sb(ctx, "state_s", [P, NB, 2, DV])
        with ExitStack() as st:
            NL = LV + 1
            vg = sb(st, "vg", [P, 2, W])
            gg = sb(st, "gg", [P, 2, W])
            gw = sb(st, "gw", [P, DV])
            mask = sb(st, "mask", [P, P])
            mask8 = sb(st, "mask8", [LASTW, LASTW])
            colm = sb(st, "colm", [P, NB + 1, LASTW])
            rowm = sb(st, "rowm", [LASTW, NB + 1])
            dd = sb(st, "dd", [P, 2, NL, 2, 2, P])
            ff = sb(st, "ff", [P, 3, NL, 2, 2, P])
            ebl = sb(st, "ebl", [P, 3, 2, NB + 1])
            at = sb(st, "at", [P, 2, 2, 2, P])
            kd = sb(st, "kd", [P, 2, P])
            kd8 = sb(st, "kd8", [LASTW, NB + 1, 2 * P])
            q8 = sb(st, "q8", [P, 2, 2, NB + 1, LASTW])
            og = sb(st, "og", [P, W])
            squares_g = sb(st, "squares_g", [P, W])
            eps_g = sb(st, "eps_g", [P, 1])
            mixg = sb(st, "mix_g", [P, W])
            r4g = sb(st, "r4g", [P, 3, 4])
            pA = ps(st, "pA", [P, 4, 512])
            qz = sb(st, "qz", [P, 3, 2, 2, P])
            pOg = ps(st, "pOg", [P, 512])
            pK = ps(st, "pK", [P, 512])
            pdS = ps(st, "pdS", [P, 512])
            pM = ps(st, "pM", [P, 512])
            state_banks = [pdS[:, :], pA[:, 0, :], pA[:, 1, :]]
            state_bank = lambda c: state_banks[c % 3]
            g_in = sem("g_in")
            vg_in = [sem(f"vg_in{n}") for n in range(2)]
            dzero = sem("dzero")
            dd_clear = sem("dd_clear")
            dexp_in = sem("dexp_in")
            dexp = sem("dexp")
            fdone = sem("fdone")
            adone = sem("adone")
            amask = sem("amask")
            diag_done = sem("diag_done")
            ogd = sem("ogd")
            ogc = sem("ogc")
            kdt = sem("kdt")
            kdo = sem("kdo")
            kd8d = sem("kd8d")
            q8d = sem("q8d")
            dsd = sem("dsd")
            sdn = sem("state_done")
            ggd = sem("ggd")
            grr = sem("grr")
            mgd = sem("mgd")
            mgt = sem("mgt")
            mgo = sem("mgo")
            g_out = sem("g_out")
            pch3 = sem("pchain_g")
            dch3 = sem("dchain_g")
            ach3 = sem("achain_g")
            def level_groups(i):
                return [[LV - 1, LV - 2], list(range(LV - 2))] if i < TILES - 1 else [[LV - 1]]

            def groups_done(i, g):
                return 2 * i + g + 1

            block = st.enter_context(nc.Block())

            @block.sync
            def _(sp):
                sp.dma_start(gw[:], gla_norm_w.to_broadcast([P, DV])).then_inc(g_in, 16)
                sp.dma_start(mask[:], c_mask).then_inc(g_in, 16)
                sp.dma_start(mask8[:], c_mask8).then_inc(g_in, 16)
                sp.dma_start(colm[:], c_colm).then_inc(g_in, 16)
                sp.dma_start(rowm[:], c_rowm).then_inc(g_in, 16)
                for m in range(2):
                    sp.dma_start(ss_[:, :, m, :], state_gla[0].rearrange("b (m r) d e -> m (r d) b e", m=2)[m])\
                      .then_inc(g_in, 16)
                for i in range(TILES):
                    r = rows_of(i)
                    if i == 2:
                        for k in range(KT):
                            sp.dma_start(wo_raw[k], w_out[0, k * P:(k + 1) * P, :]).then_inc(wo_in, 16)
                    if i >= 2:
                        sp.wait_ge(mgd, i - 1)
                        sp.wait_ge(dsd, i - 1)
                        sp.wait_ge(ogd, i - 1)
                    sp.dma_start(vg[0:r, i % 2, :], val_g[i, 0:r, :]).then_inc(vg_in[i % 2], 16)
                    sp.dma_start(gg[0:r, i % 2, :], gate_g[i, 0:r, :]).then_inc(vg_in[i % 2], 16)
                sp.wait_ge(sdn, TILES + NB)
                for m in range(2):
                    sp.dma_start(s_sample[0].rearrange("b (m r) d e -> m (r d) b e", m=2)[m], ss_[:, :, m, :])\
                      .then_inc(g_out, 16)
                    sp.dma_start(s_prompt[0, 0].rearrange("(m r) d e -> m (r d) e", m=2)[m], sp_[:, m, :])\
                      .then_inc(g_out, 16)
                sp.wait_ge(wo_in, 16 * KT)

            @block.tensor
            def _(pe):
                def products(i):
                    r = rows_of(i)
                    pe.wait_ge(fdone, i + 1)
                    for g, group in enumerate(level_groups(i)):
                        if i >= 1:
                            pe.wait_ge(amask, groups_done(i - 1, g))
                        for n in group:
                            s1, t0 = (HALVES[0], HALVES[0]) if n == 0 else (r, 0)
                            for h in range(H):
                                half = slice(DK * (h % 2), DK * (h % 2) + DK)
                                c0 = (n % 2) * 256 + (h // 2) * P
                                ins = pe.matmul(pA[0:s1, 2 * (n // 2) + h % 2, c0 + t0:c0 + r],
                                                ff[half, i % 3, n, 1, h // 2, 0:s1],
                                                ff[half, i % 3, n, 0, h // 2, t0:r], start=True, stop=True)
                        ins.then_inc(adone, 1)
                    if i >= 1:
                        pe.wait_ge(kdo, i)
                    for m in range(2):
                        ins = pe.transpose(pK[0:r, m * P:(m + 1) * P], ff[:, i % 3, LV, 1, m, 0:r], ident[:])
                    ins.then_inc(kdt, 1)

                def output(i):
                    r = rows_of(i)
                    pe.wait_ge(amask, groups_done(i, len(level_groups(i)) - 1))
                    pe.wait_ge(vg_in[i % 2], 32 * (i // 2 + 1))
                    if i >= 1:
                        pe.wait_ge(sdn, i)
                        pe.wait_ge(ogc, i)
                    if i == TILES - 1:
                        pe.wait_ge(q8d, 1)
                    for h in range(H):
                        to = pOg[0:r, h * DV:(h + 1) * DV]
                        ins = pe.matmul(to, at[0:r, i % 2, h % 2, h // 2, 0:r], vg[0:r, i % 2, h * DV:(h + 1) * DV],
                                        start=True, stop=(i == 0))
                        if 0 < i < TILES - 1:
                            ins = pe.matmul(to, qz[:, i % 3, h % 2, h // 2, :], sp_[:, h // 2, :],
                                            start=False, stop=True)
                        if i == TILES - 1:
                            for c in range(NB + 1):
                                of = sp_[:, h // 2, :] if c == 0 else ss_[:, c - 1, h // 2, :]
                                ins = pe.matmul(to, q8[:, h % 2, h // 2, c, :], of, start=False, stop=(c == NB))
                    ins.then_inc(ogd, 1)

                def state(i):
                    r = rows_of(i)
                    pe.wait_ge(kdo, i + 1)
                    if i >= 1:
                        pe.wait_ge(sdn, i)
                    for c in range(1 if i < TILES - 1 else NB + 1):
                        if i == TILES - 1:
                            if c == 0:
                                pe.wait_ge(kd8d, 1)
                            if c >= len(state_banks):
                                pe.wait_ge(sdn, i + c - len(state_banks) + 1)
                        for m in range(2):
                            k = kd[:, m, :] if i < TILES - 1 else kd8[:, c, m * P:(m + 1) * P]
                            ins = pe.matmul(state_bank(c)[:, m * 256:(m + 1) * 256], k,
                                            vg[0:r, i % 2, m * 256:(m + 1) * 256],
                                            start=True, stop=True)
                        ins.then_inc(dsd, 1)

                def turn_mix(i):
                    r = rows_of(i)
                    pe.wait_ge(mgd, i + 1)
                    if i >= 1:
                        pe.wait_ge(mgo, i)
                    for k in range(H):
                        ins = pe.transpose(pM[:, k * P:k * P + r], mixg[0:r, k * P:(k + 1) * P], ident[0:r, 0:r])
                    ins.then_inc(mgt, 1)

                pe.wait_ge(g_in, 16 * 7)
                pe.wait_ge(dzero, 1)
                products(0)
                for i in range(TILES):
                    if i + 1 < TILES:
                        products(i + 1)
                    output(i)
                    state(i)
                    if i >= 1:
                        turn_mix(i - 1)
                turn_mix(TILES - 1)

            @block.scalar
            def _(act):
                link = [0]

                def linked(ins):
                    link[0] += 1
                    ins.then_inc(ach3, 1)
                    act.wait_ge(ach3, link[0])

                def decays(i):
                    r = rows_of(i)
                    act.wait_ge(dexp_in, i + 1)
                    if i >= 3:
                        act.wait_ge(sdn, i - 2)
                    n0 = 0 if i < TILES - 1 else LV - 1
                    for n in range(n0, NL):
                        act.activation(ff[:, i % 3, n, :, :, 0:r], dd[:, i % 2, n, :, :, 0:r], ACT.Exp)
                    if i < TILES - 1:
                        act.activation(ebl[:, i % 3, :, 0:1], bT[:, :, P * i + P - 1:P * i + P], ACT.Exp)\
                           .then_inc(dexp, 1)
                    else:
                        act.activation(ebl[:, i % 3, :, 0:1], bT[:, :, P * i + TAIL - 1:P * i + TAIL], ACT.Exp)
                        act.activation(ebl[:, i % 3, :, 1:NB + 1],
                                       bT[:, :, P * i + S0:P * i + S0 + NS].rearrange("p m (b t) -> p m b t", t=TS)
                                       [:, :, :, TS - 1], ACT.Exp).then_inc(dexp, 1)

                def turned_k(i):
                    r = rows_of(i)
                    act.wait_ge(kdt, i + 1)
                    if i >= 1:
                        act.wait_ge(dsd, i)
                    act.activation(kd[0:r, :, :], pK[0:r, 0:2 * P].rearrange("p (m d) -> p m d", m=2), ACT.Copy)\
                       .then_inc(kdo, 1)

                def out(i):
                    r = rows_of(i)
                    act.wait_ge(ogd, i + 1)
                    if i >= 1:
                        act.wait_ge(mgd, i)
                    act.activation(og[0:r, :], pOg[0:r, :], ACT.Copy).then_inc(ogc, 1)
                    act.wait_ge(ogc, i + 1)
                    for h in range(H):
                        c = slice(h * DV, (h + 1) * DV)
                        ins = act.activation(squares_g[0:r, c], og[0:r, c], ACT.Square, accum_out=r4g[0:r, 0, h:h + 1])
                    linked(ins)
                    linked(act.activation(r4g[0:r, 1, :], r4g[0:r, 0, :], ACT.Ln, scale=1.0 / DV, bias=eps_g[0:r, :]))
                    act.activation(r4g[0:r, 2, :], r4g[0:r, 1, :], ACT.Exp, scale=-0.5).then_inc(grr, 1)

                def mixed(i):
                    r = rows_of(i)
                    act.wait_ge(mgt, i + 1)
                    act.activation(mixT[:, H:2 * H, P * i:P * i + r],
                                   pM[:, :].rearrange("p (k t) -> p k t", k=H)[:, :, 0:r], ACT.Copy)\
                       .then_inc(mgo, 1)

                decays(0)
                act.wait_ge(dzero, 1)
                decays(1)
                turned_k(0)
                for i in range(TILES):
                    if i + 2 < TILES:
                        decays(i + 2)
                    out(i)
                    if i + 1 < TILES:
                        turned_k(i + 1)
                    if i >= 1:
                        mixed(i - 1)
                mixed(TILES - 1)

            def exponents(eng, linked, i):
                r = rows_of(i)
                b = bT[:, :, P * i:P * i + r]
                if i >= 2:
                    eng.wait_ge(dexp, i - 1)
                if i < TILES - 1:
                    v = lambda a: a.rearrange("p m (n x) -> p m n x", x=DIAG)
                    ref = v(b)[:, :, :, DIAG // 2 - 1:DIAG // 2].to_broadcast([P, 2, P // DIAG, DIAG])
                    eng.tensor_tensor(v(dd[:, i % 2, LV - 1, 0]), v(b), ref, ALU.subtract)
                    linked(eng.tensor_tensor(v(dd[:, i % 2, LV - 1, 1]), ref, v(b), ALU.subtract))
                    last = b[:, :, P - 1:P].to_broadcast([P, 2, P])
                    eng.tensor_tensor(dd[:, i % 2, LV, 1], last, b, ALU.subtract)
                    if i == 0:
                        eng.wait_ge(dd_clear, 1)
                    for n, half in enumerate(HALVES):
                        v = lambda a: a.rearrange("p m (n two x) -> p m n two x", two=2, x=half)
                        nb = P // (2 * half)
                        to_q, to_k, bb = v(dd[:, i % 2, n, 0]), v(dd[:, i % 2, n, 1]), v(b)
                        if nb == 1:
                            for m in range(2):
                                ref = b[:, m, half - 1:half].to_broadcast([P, half])
                                eng.tensor_tensor(dd[:, i % 2, n, 0, m, half:P], b[:, m, half:P], ref, ALU.subtract)
                                eng.tensor_tensor(dd[:, i % 2, n, 1, m, 0:half], ref, b[:, m, 0:half], ALU.subtract)
                            continue
                        ref = bb[:, :, :, 0, half - 1:half].to_broadcast([P, 2, nb, half])
                        eng.tensor_tensor(to_q[:, :, :, 1, :], bb[:, :, :, 1, :], ref, ALU.subtract)
                        eng.tensor_tensor(to_k[:, :, :, 0, :], ref, bb[:, :, :, 0, :], ALU.subtract)
                else:
                    t, s = slice(0, TAIL), slice(S0, S0 + NS)
                    linked(eng.memset(dd[:, i % 2, LV - 1:NL, :, :, 0:r], 0.0))
                    ref = b[:, :, TAIL // 2 - 1:TAIL // 2].to_broadcast([P, 2, TAIL])
                    eng.tensor_tensor(dd[:, i % 2, LV - 1, 0, :, t], b[:, :, t], ref, ALU.subtract)
                    eng.tensor_tensor(dd[:, i % 2, LV - 1, 1, :, t], ref, b[:, :, t], ALU.subtract)
                    eng.tensor_copy(dd[:, i % 2, LV - 1, 0, :, s], b[:, :, s])
                    linked(eng.tensor_scalar(dd[:, i % 2, LV - 1, 1, :, s], b[:, :, s], -1.0, None, ALU.mult))
                    eng.tensor_tensor(dd[:, i % 2, LV, 1, :, t], b[:, :, TAIL - 1:TAIL].to_broadcast([P, 2, TAIL]),
                                      b[:, :, t], ALU.subtract)
                    v = lambda a: a.rearrange("p m (b t) -> p m b t", t=TS)
                    eng.tensor_tensor(v(dd[:, i % 2, LV, 1, :, s]), v(b[:, :, s])[:, :, :, TS - 1:TS]
                                      .to_broadcast([P, 2, NB, TS]), v(b[:, :, s]), ALU.subtract)
                eng.tensor_copy(dd[:, i % 2, LV, 0, :, 0:r], b)
                eng.tensor_scalar(dd[:, i % 2, LV - 1, :, :, 0:r], dd[:, i % 2, LV - 1, :, :, 0:r], 80.0, None, ALU.min)\
                   .then_inc(dexp_in, 1)

            @block.gpsimd
            def _(pool):
                link = [0]

                def linked(ins):
                    link[0] += 1
                    ins.then_inc(pch3, 1)
                    pool.wait_ge(pch3, link[0])

                def gate(i):
                    r = rows_of(i)
                    pool.wait_ge(vg_in[i % 2], 32 * (i // 2 + 1))
                    g = gg[0:r, i % 2, :].rearrange("p (h d) -> p h d", h=H)
                    pool.tensor_tensor(g, g, gw[0:r, :].unsqueeze(1).to_broadcast([r, H, DV]), ALU.mult)\
                        .then_inc(ggd, 1)

                for slot in range(2):
                    pool.memset(dd[:, slot, 0:LV - 1], 0.0).then_inc(dd_clear, 1)
                pool.wait_ge(dd_clear, 2)
                pool.wait_ge(dexp_in, 1)
                exponents(pool, linked, 1)
                pool.wait_ge(g_in, 16 * 7)
                for i in range(TILES):
                    if i + 2 < TILES:
                        exponents(pool, linked, i + 2)
                    gate(i)

            @block.vector
            def _(dve):
                def factors(i):
                    r = rows_of(i)
                    dve.wait_ge(dexp, i + 1)
                    n0 = 0 if i < TILES - 1 else LV - 1
                    t = slice(P * i, P * i + r)
                    for hh in range(2):
                        half = slice(DK * hh, DK * hh + DK)
                        dve.tensor_tensor(qz[half, i % 3, hh, :, 0:r], ff[half, i % 3, LV, 0, :, 0:r], gqT[half, :, t],
                                          ALU.mult)
                    to = ff[:, i % 3, n0:LV, 0, :, 0:r]
                    dve.tensor_tensor(to, to, gqT[:, :, t].unsqueeze(1).to_broadcast([P, LV - n0, 2, r]), ALU.mult)
                    to = ff[:, i % 3, n0:NL, 1, :, 0:r]
                    dve.tensor_tensor(to, to, gkT[:, :, t].unsqueeze(1).to_broadcast([P, NL - n0, 2, r]), ALU.mult)\
                       .then_inc(fdone, 1)
                    if i == TILES - 1:
                        dve.wait_ge(fdone, i + 1)
                        for hh in range(2):
                            for m in range(2):
                                ins = dve.tensor_tensor(q8[:, hh, m], qz[:, i % 3, hh, m, 0:r].unsqueeze(1)
                                                        .to_broadcast([P, NB + 1, r]), colm[:], ALU.mult)
                        ins.then_inc(q8d, 1)

                def masks(i):
                    r = rows_of(i)
                    if i >= 2:
                        dve.wait_ge(ogd, i - 1)

                    def sums(n, s, t):
                        return pA[s, 2 * (n // 2):2 * (n // 2) + 2, (n % 2) * 256:(n % 2) * 256 + 256]\
                            .rearrange("p a (m t) -> p a m t", m=2)[:, :, :, t]

                    for g, group in enumerate(level_groups(i)):
                        dve.wait_ge(adone, groups_done(i, g))
                        for n in group:
                            if n == LV - 1:
                                mk = (mask if r == P else mask8)[:, :].unsqueeze(1).unsqueeze(1)\
                                    .to_broadcast([r, 2, 2, r])
                                every = slice(0, r)
                                ins = dve.tensor_tensor(at[0:r, i % 2, :, :, 0:r], sums(n, every, every), mk, ALU.mult)
                                if i < TILES - 1:
                                    ins.then_inc(diag_done, 1)
                                    dve.wait_ge(diag_done, i + 1)
                                continue
                            half = HALVES[n]
                            for s0 in range(0, P, 2 * half):
                                s, t = slice(s0, s0 + half), slice(s0 + half, s0 + 2 * half)
                                ins = dve.tensor_copy(at[s, i % 2, :, :, t], sums(n, s, t))
                        ins.then_inc(amask, 1)

                def state(i):
                    r = rows_of(i)
                    if i == TILES - 1:
                        dve.wait_ge(kdo, i + 1)
                        dve.tensor_tensor(kd8[:], kd[0:r].rearrange("p m d -> p (m d)").unsqueeze(1)
                                          .to_broadcast([r, NB + 1, 2 * P]),
                                          rowm[:].unsqueeze(2).to_broadcast([r, NB + 1, 2 * P]), ALU.mult)\
                           .then_inc(kd8d, 1)
                        dve.wait_ge(ogd, i + 1)
                    for c in range(1 if i < TILES - 1 else NB + 1):
                        dve.wait_ge(dsd, i + c + 1)
                        if c == 0 and i >= 1:
                            dve.wait_ge(ogd, i + 1)
                        for m in range(2):
                            for hh in range(2):
                                half = slice(DK * hh, DK * hh + DK)
                                ds = state_bank(c)[half, m * 256 + hh * P:m * 256 + hh * P + P]
                                to = sp_[half, m, :] if c == 0 else ss_[half, c - 1, m, :]
                                if i == 0:
                                    ins = dve.tensor_copy(to, ds)
                                else:
                                    ins = dve.scalar_tensor_tensor(out=to, in0=to,
                                                                   scalar=ebl[half, i % 3, m, c:c + 1],
                                                                   in1=ds, op0=ALU.mult, op1=ALU.add)
                        ins.then_inc(sdn, 1)

                def norm(i):
                    r = rows_of(i)
                    dve.wait_ge(ggd, i + 1)
                    dve.wait_ge(grr, i + 1)
                    if i >= 1:
                        dve.wait_ge(mgt, i)
                    for h in range(H):
                        c = slice(h * DV, (h + 1) * DV)
                        ins = dve.scalar_tensor_tensor(out=mixg[0:r, c], in0=og[0:r, c], scalar=r4g[0:r, 2, h:h + 1],
                                                       in1=gg[0:r, i % 2, c], op0=ALU.mult, op1=ALU.mult)
                    ins.then_inc(mgd, 1)

                link = [0]

                def linked(ins):
                    link[0] += 1
                    ins.then_inc(dch3, 1)
                    dve.wait_ge(dch3, link[0])

                exponents(dve, linked, 0)
                dve.memset(eps_g[:], EPS)
                dve.memset(qz[:], 0.0).then_inc(dzero, 1)
                dve.wait_ge(dzero, 1)
                dve.wait_ge(g_in, 16 * 7)
                factors(0)
                factors(1)
                for i in range(TILES):
                    masks(i)
                    if i >= 1:
                        state(i - 1)
                        norm(i - 1)
                    if i + 2 < TILES:
                        factors(i + 2)
                state(TILES - 1)
                norm(TILES - 1)

        with ExitStack() as st:
            woh = sb(st, "woh", [P, KT, D], F32R)
            wol = sb(st, "wol", [P, KT, D], F32R)
            mh = sb(st, "mh", [P, 2, KT, P], F32R)
            ml = sb(st, "ml", [P, 2, KT, P], F32R)
            xr = sb(st, "xr", [P, 2, D])
            pY = [ps(st, f"pY{n}", [P, 512]) for n in range(4)]
            xr_in = [sem(f"xr_in{n}") for n in range(2)]
            woh_d = sem("woh_d")
            wol_d = sem("wol_d")
            mh_d = sem("mh_d")
            ml_d = sem("ml_d")
            y_done = sem("y_done")
            y_sum = sem("y_sum")
            y_out = [sem(f"y_out{n}") for n in range(2)]

            def parts(i):
                if i == 0:
                    return [(NMETA, P, x_prompt[0, 0:P - NMETA, :], y_prompt[0, 0:P - NMETA, :])]
                if i < TILES - 1:
                    rows = slice(P * i - NMETA, P * (i + 1) - NMETA)
                    return [(0, P, x_prompt[0, rows, :], y_prompt[0, rows, :])]
                return [(0, TAIL, x_prompt[0, SEQ - TAIL:SEQ, :], y_prompt[0, SEQ - TAIL:SEQ, :]),
                        (S0, S0 + NS, x_sample.rearrange("b t d -> (b t) d"),
                         y_sample.rearrange("b t d -> (b t) d"))]

            def moved(i):
                return 16 * sum(len(parts(j)) for j in range(i % 2, i + 1, 2))

            block = st.enter_context(nc.Block())
            xz = sem("xr_zero")

            @block.sync
            def _(sp):
                sp.wait_ge(xz, 1)
                for i in range(TILES + 1):
                    if i < TILES:
                        if i >= 2:
                            sp.wait_ge(y_out[i % 2], moved(i - 2))
                        if i == TILES - 1:
                            sp.wait_ge(xz, 2)
                        for a, b, x, _ in parts(i):
                            sp.dma_start(xr[a:b, i % 2, :], x).then_inc(xr_in[i % 2], 16)
                    if i >= 1:
                        sp.wait_ge(y_sum, 2 * i)
                        for a, b, _, y in parts(i - 1):
                            sp.dma_start(y, xr[a:b, (i - 1) % 2, :]).then_inc(y_out[(i - 1) % 2], 16)
                sp.wait_ge(y_out[0], moved(TILES - 1))
                sp.wait_ge(y_out[1], moved(TILES - 2))
                sp.wait_ge(g_out, 64)

            @block.scalar
            def _(act):
                def mix_hi(i):
                    r = rows_of(i)
                    if i >= 2:
                        act.wait_ge(y_done, 2 * (i - 1))
                    act.activation(mh[:, i % 2, :, 0:r], mixT[:, :, P * i:P * i + r], ACT.Copy).then_inc(mh_d, 1)

                mix_hi(0)
                for k in range(KT):
                    act.activation(woh[:, k, :], wo_raw[k], ACT.Copy).then_inc(woh_d, 1)
                for i in range(1, TILES):
                    mix_hi(i)

            @block.vector
            def _(dve):
                def mix_lo(i):
                    r = rows_of(i)
                    dve.wait_ge(mh_d, i + 1)
                    dve.tensor_tensor(ml[:, i % 2, :, 0:r], mixT[:, :, P * i:P * i + r],
                                      mh[:, i % 2, :, 0:r].bitcast(F32), ALU.subtract).then_inc(ml_d, 1)

                def add(i):
                    r = rows_of(i)
                    for n in range(2):
                        dve.wait_ge(y_done, 2 * i + n + 1)
                        dve.wait_ge(xr_in[i % 2], moved(i))
                        x = xr[0:r, i % 2, n * 512:(n + 1) * 512]
                        dve.tensor_tensor(x, x, pY[2 * (i % 2) + n][0:r, :], ALU.add).then_inc(y_sum, 1)

                dve.memset(xr[0:S0, 0, :], 0.0).then_inc(xz, 1)
                mix_lo(0)
                for k in range(KT):
                    dve.wait_ge(woh_d, k + 1)
                    dve.tensor_tensor(wol[:, k, :], wo_raw[k], woh[:, k, :].bitcast(F32), ALU.subtract)\
                       .then_inc(wol_d, 1)
                for i in range(TILES):
                    if i + 1 < TILES:
                        mix_lo(i + 1)
                    add(i)
                    if i == TILES - 3:
                        dve.wait_ge(y_out[0], moved(TILES - 3))
                        dve.memset(xr[0:S0, 0, :], 0.0).then_inc(xz, 1)

            @block.tensor
            def _(pe):
                for i in range(TILES):
                    r = rows_of(i)
                    pe.wait_ge(mh_d, i + 1)
                    pe.wait_ge(ml_d, i + 1)
                    for n in range(2):
                        if i >= 2:
                            pe.wait_ge(y_sum, 2 * (i - 2) + n + 1)
                        for k in range(KT):
                            if i == 0 and n == 0:
                                pe.wait_ge(woh_d, k + 1)
                                pe.wait_ge(wol_d, k + 1)
                            for x, (a, b) in enumerate(((mh, woh), (ml, woh), (mh, wol))):
                                ins = pe.matmul(pY[2 * (i % 2) + n][0:r, :], a[:, i % 2, k, 0:r],
                                                b[:, k, n * 512:(n + 1) * 512], start=(k == 0 and x == 0),
                                                stop=(k == KT - 1 and x == 2))
                        ins.then_inc(y_done, 1)


def shape_constants():
    import numpy as np
    f = np.float32
    c = {"c_ident": np.eye(P, dtype=f)}
    a = np.arange(P)
    c["c_cum"] = ((a[:, None] <= a[None, :]) / 16.0).astype(f)
    a8 = np.arange(LASTW)
    chunk = np.where(a8 < TAIL, 0, np.where(a8 < S0, 100 + a8, 1 + (a8 - S0) // TS))
    same = (chunk[:, None] == chunk[None, :]) & (a8[:, None] <= a8[None, :])
    c["c_cum8"] = (same / 16.0).astype(f)
    s, t = a[:, None], a[None, :]
    c["c_mask"] = ((s // DIAG == t // DIAG) & (s <= t)).astype(f)
    c["c_mask8"] = same.astype(f)
    n = np.arange(0, PAST + TS)
    nf = np.maximum(n, 1).astype(f)
    large = 16 + (np.log(nf / f(16)) / f(math.log(128 / 16)) * f(16)).astype(np.int32)
    bucket = np.where(n < 16, n, np.minimum(large, 31))

    def hot(n):
        o = np.zeros((32, n.size), f)
        ok = n.ravel() >= 0
        o[bucket[np.maximum(n.ravel(), 0)], np.arange(n.size)] = 1
        o[31, :] -= 1
        o[:, ~ok] = 0
        return o
    d = 255 - np.arange(384)
    c["c_oh"] = hot(d)
    c["c_negp"] = np.broadcast_to(np.where(d < 0, NEG, 0).astype(f), (H, 384)).copy()
    q = np.arange(TS)
    c["c_hotp"] = hot(PAST + q[:, None] - (PAST - PAGE + np.arange(PAGE))[None, :]).reshape(32, TS * PAGE)
    j = np.arange(NS)
    dn = np.stack([np.where((j // TS == b), q[:, None] - (j % TS)[None, :], -1) for b in range(NB)], 1)
    c["c_hotn"] = hot(dn).reshape(32, TS, NB * NS)
    row = np.arange(32)
    neg = np.where(dn < 0, NEG, 0).astype(f)
    c["c_negn"] = neg[row % TS].reshape(32, NB * NS)
    c["c_rowq"] = np.broadcast_to((row[None, :] % TS == q[:, None]).astype(f), (32, TS, 32)).copy()
    pr = np.arange(P) % 32
    sel = np.zeros((P, NB, H, NS), f)
    for b in range(NB):
        for h in range(H):
            sel[:, b, h, :] = (pr[:, None] // 8 == h) & (b * TS + pr[:, None] % TS == np.arange(NS)[None, :])
    c["c_selT"] = sel
    c["c_m01"] = np.stack([(row // 4 % 2 == 0), (row // 4 % 2 == 1)], 1).astype(f)
    own = (chunk[None, :] == np.arange(NB + 1)[:, None]).astype(f)
    c["c_colm"] = np.broadcast_to(own, (P, NB + 1, LASTW)).copy()
    c["c_rowm"] = own.T.copy()
    return c


_INS = ["x_prompt", "x_sample", "cache_k", "cache_v", "state_gla", "page_table", "meta_tokens", "rel_bias",
        "norm_w", "w_in", "q_norm_w", "k_norm_w", "lam_q", "lam_k", "diff_norm_w", "gla_wa2", "gla_ba",
        "gla_norm_w", "w_out"]
_CONSTS = ["c_ident", "c_cum", "c_cum8", "c_mask", "c_mask8", "c_oh", "c_hotp", "c_hotn", "c_negn", "c_negp",
           "c_rowq", "c_selT", "c_colm", "c_rowm", "c_m01"]
_OUTS = [(1, SEQ, D), (NB, TS, D), (1, 1, L, H, 2 * DK), (1, 1, L, H, DV), (1, 1, H, DK, DV),
         (1, NB, TS, H, 2 * DK), (1, NB, TS, H, DV), (1, NB, H, DK, DV)]


def kernel(**inputs):
    import numpy as np
    import concourse.bacc as bacc
    from concourse.bass_utils import run_bass_kernel_spmd

    nc = bacc.Bacc("TRN2", target_bir_lowering=False, num_devices=1)
    consts = shape_constants()
    arrays, args = {}, []
    for name in _INS + _CONSTS:
        a = np.ascontiguousarray(inputs[name] if name in inputs else consts[name])
        arrays[f"in_{name}"] = a
        args.append(nc.dram_tensor(f"in_{name}", a.shape, mybir.dt.from_np(a.dtype), kind="ExternalInput").ap())
    for n, shape in enumerate(_OUTS):
        args.append(nc.dram_tensor(f"out_{n}", shape, F32, kind="ExternalOutput").ap())
    hymba_kernel(nc, *args)
    r = run_bass_kernel_spmd(nc, [arrays], core_ids=[0])
    return tuple(r.results[0][f"out_{n}"] for n in range(len(_OUTS)))
```
